# Optimizing a Trainium2 kernel written in Bass

```python
import math
import jax, jax.numpy as jnp
from jax import lax
import numpy as np

D_MODEL = 2048
BATCH = 1
SEQ = 512
DEPTH = 1

GRID_W = 64
CTX_LEN = 256

D_FOURIER = D_MODEL // 4
N_FOURIER_GROUPS = 4
FOURIER_GROUP = D_FOURIER // N_FOURIER_GROUPS
D_CONV = D_MODEL // 4
CONV_WIDTH = 31
CONV_PAD = CONV_WIDTH // 2
N_ATT_HEADS = 8
ATT_QK_DIM = 64
ATT_V_DIM = 2 * ATT_QK_DIM
D_ATT = N_ATT_HEADS * ATT_V_DIM
D_MIX = D_FOURIER + D_CONV + D_ATT
QK_COLS = N_ATT_HEADS * 2 * ATT_QK_DIM
ATT_SCALE = 1.0 / math.sqrt(ATT_QK_DIM)
Q_BLOCK = 128
ROPE_BASE = 10000.0
ROPE_PAIRS_PER_AXIS = ATT_QK_DIM // 4

OFF_CONV = D_FOURIER
OFF_Q = OFF_CONV + 2 * D_CONV
OFF_K = OFF_Q + QK_COLS
OFF_V = OFF_K + QK_COLS
D_IN_PROJ = OFF_V + D_ATT

N_GROUPS = 4
EXPERTS_PER_GROUP = 8
N_EXPERTS = N_GROUPS * EXPERTS_PER_GROUP
TOP_K = 2
D_EXPERT = D_MODEL // 4
MOE_BLOCK = 128

N_MOD = 6
LN_EPS = 1e-6
ALPHA = (2.0 * DEPTH) ** 0.25
BETA = (8.0 * DEPTH) ** -0.25

kernel_name = "hybrid_fourier_conv_diffattn_hmoe_dit"

def _layernorm(x):
    xf = x.astype(jnp.float32)
    mu = xf.mean(-1, keepdims=True)
    var = jnp.square(xf - mu).mean(-1, keepdims=True)
    return ((xf - mu) * lax.rsqrt(var + LN_EPS)).astype(x.dtype)

def _ln_affine(x, g, b):
    return _layernorm(x) * g + b

def _modulate(h, shift, scale):
    return h * (1.0 + scale[:, None, :]) + shift[:, None, :]

def _axial_rope_tables(n_tokens, dtype):
    rows = n_tokens // GRID_W
    row = jnp.repeat(jnp.arange(rows), GRID_W).astype(jnp.float32)
    col = jnp.tile(jnp.arange(GRID_W), rows).astype(jnp.float32)
    inv = 1.0 / (ROPE_BASE ** (jnp.arange(ROPE_PAIRS_PER_AXIS, dtype=jnp.float32) / ROPE_PAIRS_PER_AXIS))
    ang = jnp.concatenate([row[:, None] * inv, col[:, None] * inv], -1)
    return jnp.cos(ang).astype(dtype), jnp.sin(ang).astype(dtype)

def _apply_rope(x, cos, sin):
    x1, x2 = jnp.split(x, 2, axis=-1)
    return jnp.concatenate([x1 * cos - x2 * sin, x1 * sin + x2 * cos], -1)

def _qk_heads(p):
    B, L, _ = p.shape
    return p.reshape(B, L, N_ATT_HEADS, 2, ATT_QK_DIM).transpose(0, 2, 3, 1, 4)

def _v_heads(p):
    B, L, _ = p.shape
    return p.reshape(B, L, N_ATT_HEADS, ATT_V_DIM).transpose(0, 2, 1, 3)

def _diff_attend(q, k, v, lam):
    s = jnp.einsum('bhmqd,bhmkd->bhmqk', q, k).astype(jnp.float32) * ATT_SCALE
    p = jax.nn.softmax(s, axis=-1)
    a = p[:, :, 0] - lam * p[:, :, 1]
    return jnp.einsum('bhqk,bhkd->bhqd', a.astype(v.dtype), v)

def _diff_attention_blocks(q, k, v, lam):
    B, H, M, S, d = q.shape
    nb = S // Q_BLOCK
    qb = q.reshape(B, H, M, nb, Q_BLOCK, d).transpose(3, 0, 1, 2, 4, 5)
    ob = lax.map(lambda qi: _diff_attend(qi, k, v, lam), qb)
    return ob.transpose(1, 2, 0, 3, 4).reshape(B, H, S, ATT_V_DIM)

def _diff_head_out(o, g, lam_init):
    B, H, L, Dv = o.shape
    of = o.astype(jnp.float32)
    of = of * lax.rsqrt(jnp.mean(of * of, -1, keepdims=True) + LN_EPS) * g * (1.0 - lam_init)
    return of.astype(o.dtype).transpose(0, 2, 1, 3).reshape(B, L, H * Dv)

def _fourier_mix(u, w):
    B, L, _ = u.shape
    ug = u.astype(jnp.float32).reshape(B, L, N_FOURIER_GROUPS, FOURIER_GROUP)
    y = jnp.fft.fft2(ug, axes=(1, 3), norm='ortho').real
    return y.astype(u.dtype).reshape(B, L, D_FOURIER) @ w

def _conformer_conv(a, gt, conv_w, conv_b, ln_g, ln_b, w_pw):
    u = a * jax.nn.sigmoid(gt)
    y = lax.conv_general_dilated(u, conv_w[:, None, :], window_strides=(1,),
                                 padding=((CONV_PAD, CONV_PAD),),
                                 dimension_numbers=('NWC', 'WIO', 'NWC'),
                                 feature_group_count=D_CONV) + conv_b
    y = _ln_affine(y, ln_g, ln_b)
    return jax.nn.silu(y) @ w_pw

def _split_groups(pr):
    return (pr[..., :OFF_CONV], pr[..., OFF_CONV:OFF_CONV + D_CONV], pr[..., OFF_CONV + D_CONV:OFF_Q],
            pr[..., OFF_Q:OFF_K], pr[..., OFF_K:OFF_V], pr[..., OFF_V:])

def _grouped_experts(h, expert, weight, w_gate, w_up, w_down):
    N, D = h.shape
    K = expert.shape[1]
    A = N * K
    n_blocks = -(-A // MOE_BLOCK) + N_EXPERTS
    cap = n_blocks * MOE_BLOCK
    flat_e = expert.reshape(A)
    order = jnp.argsort(flat_e)
    e_sorted = flat_e[order]
    tok_sorted = (order // K).astype(jnp.int32)
    w_sorted = weight.reshape(A)[order]
    counts = jnp.bincount(flat_e, length=N_EXPERTS)
    padded = (counts + MOE_BLOCK - 1) // MOE_BLOCK * MOE_BLOCK
    pad_end = jnp.cumsum(padded)
    pad_start = pad_end - padded
    start = jnp.cumsum(counts) - counts
    dest = pad_start[e_sorted] + jnp.arange(A) - start[e_sorted]
    row_tok = jnp.full((cap,), N, jnp.int32).at[dest].set(tok_sorted)
    block_e = jnp.minimum(jnp.searchsorted(pad_end, jnp.arange(n_blocks) * MOE_BLOCK, side='right'),
                          N_EXPERTS - 1)
    h_pad = jnp.concatenate([h, jnp.zeros((1, D), h.dtype)], 0)
    xb = h_pad[row_tok].reshape(n_blocks, MOE_BLOCK, D)

    def expert_block(args):
        xblk, e = args
        return (jax.nn.silu(xblk @ w_gate[e]) * (xblk @ w_up[e])) @ w_down[e]

    yb = lax.map(expert_block, (xb, block_e)).reshape(cap, D)
    return jnp.zeros((N, D), h.dtype).at[tok_sorted].add(yb[dest] * w_sorted[:, None])

def _hier_moe(h, w_rg, b_rg, w_re, b_re, w_gate, w_up, w_down):
    N = h.shape[0]
    p_g = jax.nn.softmax((h @ w_rg).astype(jnp.float32) + b_rg, axis=-1)
    wg, gidx = lax.top_k(p_g, 1)
    logit_e = ((h @ w_re).astype(jnp.float32) + b_re).reshape(N, N_GROUPS, EXPERTS_PER_GROUP)
    logit_in = logit_e[jnp.arange(N), gidx[:, 0]]
    we, eidx = lax.top_k(jax.nn.softmax(logit_in, axis=-1), TOP_K)
    we = we / we.sum(-1, keepdims=True)
    weights = (wg * we).astype(h.dtype)
    expert = gidx * EXPERTS_PER_GROUP + eidx
    return _grouped_experts(h, expert, weights, w_gate, w_up, w_down)

def setup_inputs(seed: int = 0) -> dict:
    key = jax.random.key(seed)
    ks = iter(jax.random.split(key, 40))

    def nrm(shape, scale):
        return jax.random.normal(next(ks), shape, jnp.float32) * scale

    L = DEPTH
    w_in = nrm((L, D_MODEL, D_IN_PROJ), D_MODEL ** -0.5)
    w_in = w_in.at[:, :, OFF_V:].multiply(BETA)
    return {
        "x": nrm((BATCH, SEQ, D_MODEL), 1.0),
        "c": nrm((BATCH, D_MODEL), 1.0),
        "ctx": nrm((BATCH, CTX_LEN, D_MODEL), 1.0),
        "c_ctx": nrm((D_MODEL,), 1.0),
        "w_mod": nrm((L, D_MODEL, N_MOD * D_MODEL), 0.5 * D_MODEL ** -0.5),
        "b_mod": nrm((L, N_MOD * D_MODEL), 0.01),
        "w_in": w_in,
        "b_in": nrm((L, D_IN_PROJ), 0.01),
        "w_fourier": nrm((L, D_FOURIER, D_FOURIER), BETA * D_FOURIER ** -0.5),
        "conv_w": nrm((L, CONV_WIDTH, D_CONV), CONV_WIDTH ** -0.5),
        "conv_b": nrm((L, D_CONV), 0.01),
        "conv_ln_g": 1.0 + nrm((L, D_CONV), 0.01),
        "conv_ln_b": nrm((L, D_CONV), 0.01),
        "w_pw": nrm((L, D_CONV, D_CONV), BETA * D_CONV ** -0.5),
        "lam_q1": nrm((L, ATT_QK_DIM), 0.1),
        "lam_k1": nrm((L, ATT_QK_DIM), 0.1),
        "lam_q2": nrm((L, ATT_QK_DIM), 0.1),
        "lam_k2": nrm((L, ATT_QK_DIM), 0.1),
        "subln_g": 1.0 + nrm((L, ATT_V_DIM), 0.01),
        "w_out": nrm((L, D_MIX, D_MODEL), BETA * D_MIX ** -0.5),
        "ln_a_g": 1.0 + nrm((L, D_MODEL), 0.01),
        "ln_a_b": nrm((L, D_MODEL), 0.01),
        "w_rg": nrm((L, D_MODEL, N_GROUPS), D_MODEL ** -0.5),
        "b_rg": nrm((L, N_GROUPS), 0.01),
        "w_re": nrm((L, D_MODEL, N_EXPERTS), D_MODEL ** -0.5),
        "b_re": nrm((L, N_EXPERTS), 0.01),
        "w_gate": nrm((L, N_EXPERTS, D_MODEL, D_EXPERT), D_MODEL ** -0.5),
        "w_up": nrm((L, N_EXPERTS, D_MODEL, D_EXPERT), D_MODEL ** -0.5),
        "w_down": nrm((L, N_EXPERTS, D_EXPERT, D_MODEL), BETA * D_EXPERT ** -0.5),
        "ln_f_g": 1.0 + nrm((L, D_MODEL), 0.01),
        "ln_f_b": nrm((L, D_MODEL), 0.01),
    }

def reference(x, c, ctx, c_ctx, w_mod, b_mod, w_in, b_in, w_fourier, conv_w, conv_b, conv_ln_g, conv_ln_b,
              w_pw, lam_q1, lam_k1, lam_q2, lam_k2, subln_g, w_out, ln_a_g, ln_a_b, w_rg, b_rg, w_re, b_re,
              w_gate, w_up, w_down, ln_f_g, ln_f_b):
    B, S, D = x.shape
    cos, sin = _axial_rope_tables(S, x.dtype)
    sc_l = jax.nn.silu(c)
    sc_c = jax.nn.silu(c_ctx)[None, :]
    xl, xc = x, ctx
    for i in range(DEPTH):
        last = i == DEPTH - 1
        mod_l = jnp.split(sc_l @ w_mod[i] + b_mod[i], N_MOD, axis=-1)
        mod_c = jnp.split(sc_c @ w_mod[i] + b_mod[i], N_MOD, axis=-1)
        lam_init = 0.8 - 0.6 * math.exp(-0.3 * i)
        lam = (jnp.exp(jnp.sum(lam_q1[i].astype(jnp.float32) * lam_k1[i].astype(jnp.float32)))
               - jnp.exp(jnp.sum(lam_q2[i].astype(jnp.float32) * lam_k2[i].astype(jnp.float32)))
               + lam_init)

        hl = _modulate(_layernorm(xl), mod_l[0], mod_l[1])
        hc = _modulate(_layernorm(xc), mod_c[0], mod_c[1])
        fl, al, gl, ql, kl, vl = _split_groups(hl @ w_in[i] + b_in[i])
        if last:
            pkv = hc @ w_in[i][:, OFF_K:] + b_in[i][OFF_K:]
            kc, vc = pkv[..., :OFF_V - OFF_K], pkv[..., OFF_V - OFF_K:]
        else:
            fc, ac, gc, qc, kc, vc = _split_groups(hc @ w_in[i] + b_in[i])
        Kc, Vc = _qk_heads(kc), _v_heads(vc)
        Ql = _apply_rope(_qk_heads(ql), cos, sin)
        Kl = _apply_rope(_qk_heads(kl), cos, sin)
        K_all = jnp.concatenate([Kc, Kl], axis=3)
        V_all = jnp.concatenate([Vc, _v_heads(vl)], axis=2)
        att_l = _diff_head_out(_diff_attention_blocks(Ql, K_all, V_all, lam), subln_g[i], lam_init)
        mix_l = jnp.concatenate([
            _fourier_mix(fl, w_fourier[i]),
            _conformer_conv(al, gl, conv_w[i], conv_b[i], conv_ln_g[i], conv_ln_b[i], w_pw[i]),
            att_l], axis=-1) @ w_out[i]
        if not last:
            att_c = _diff_head_out(_diff_attend(_qk_heads(qc), Kc, Vc, lam), subln_g[i], lam_init)
            mix_c = jnp.concatenate([
                _fourier_mix(fc, w_fourier[i]),
                _conformer_conv(ac, gc, conv_w[i], conv_b[i], conv_ln_g[i], conv_ln_b[i], w_pw[i]),
                att_c], axis=-1) @ w_out[i]
            xc = _ln_affine(ALPHA * xc + mod_c[2][:, None, :] * mix_c, ln_a_g[i], ln_a_b[i])
        xl = _ln_affine(ALPHA * xl + mod_l[2][:, None, :] * mix_l, ln_a_g[i], ln_a_b[i])

        hl = _modulate(_layernorm(xl), mod_l[3], mod_l[4])
        moe = functools_partial_moe = (w_rg[i], b_rg[i], w_re[i], b_re[i], w_gate[i], w_up[i], w_down[i])
        if last:
            y_l = _hier_moe(hl.reshape(-1, D), *moe).reshape(hl.shape)
        else:
            hc = _modulate(_layernorm(xc), mod_c[3], mod_c[4])
            n_c = hc.shape[0] * hc.shape[1]
            y = _hier_moe(jnp.concatenate([hc.reshape(-1, D), hl.reshape(-1, D)], 0), *moe)
            y_c = y[:n_c].reshape(hc.shape)
            y_l = y[n_c:].reshape(hl.shape)
            xc = _ln_affine(ALPHA * xc + mod_c[5][:, None, :] * y_c, ln_f_g[i], ln_f_b[i])
        xl = _ln_affine(ALPHA * xl + mod_l[5][:, None, :] * y_l, ln_f_g[i], ln_f_b[i])
    return xl


_drawn_inputs = setup_inputs


def setup_inputs(seed=0):
    import zlib

    import numpy as np

    out = dict(_drawn_inputs(seed))
    spreads = {}
    factors = {'ctx': 2.732,
     'b_mod': 7.408,
     'b_in': 7.644,
     'conv_b': 8.0,
     'conv_ln_g': 64.0,
     'conv_ln_b': 64.0,
     'lam_q1': 64.0,
     'lam_k1': 8.0,
     'lam_q2': 7.793,
     'lam_k2': 4.596,
     'subln_g': 64.0,
     'ln_a_g': 30.042,
     'ln_a_b': 29.213,
     'b_rg': 64.0,
     'b_re': 64.0,
     'ln_f_g': 32.284,
     'ln_f_b': 31.545,
     'w_rg': 8.0,
     'w_re': 8.0,
     'w_gate': 7.486,
     'w_up': 6.897,
     'w_down': 6.945}
    for name, (base, spread) in spreads.items():
        noise = np.random.default_rng([zlib.crc32(name.encode()), seed]).standard_normal(out[name].shape)
        drawn = base * np.exp(spread * noise) if base else spread * noise
        out[name] = __import__('jax').numpy.asarray(drawn.astype(out[name].dtype))
    for name, factor in factors.items():
        out[name] = (out[name] * factor).astype(out[name].dtype)
    return out
```

```python
import math
from contextlib import ExitStack

import concourse.bass as bass
from concourse import mybir

F32, I32 = mybir.dt.float32, mybir.dt.int32
ALU = mybir.AluOpType
ACT = mybir.ActivationFunctionType
AX = mybir.AxisListType

P = 128
D = 2048
KD = D // P
S = 512
C = 256
TS, TC = S // P, C // P
NT = S + C
HEADS, DQ = 8, 64
NF, NCV = 4, 4
CW = 31
PAD = CW // 2
UW = S + 2 * PAD
N_IN = 36
N_MODT = 96
N_MOD01 = 2 * KD
NE, NG, EG = 32, 4, 8
DE = 512
KE = DE // P
B = 64
NB = 48
EPS = 1e-6
ALPHA = 2.0 ** 0.25
LAM_INIT = 0.8 - 0.6 * math.exp(0.0)
ATT_SCALE = 1.0 / math.sqrt(DQ)
EMPTY = 8192

CONST = {}
_at = 0
for _n, _w in (("ident", P), ("ones", P), ("upper", P), ("cos", S), ("sin", S), ("dftc", 2 * P),
               ("iota", NB), ("first", EG), ("val", 2 * TS)):
    CONST[_n] = (_at, _at + _w)
    _at += _w
N_CONST = _at
PARAM = {}
_at = 0
for _n, _w in (("c", 2 * KD), ("b_in", 28), ("b_mod", N_MODT), ("conv_w", NCV * CW), ("conv_b", NCV),
               ("cln_g", NCV), ("cln_b", NCV), ("subln", 1), ("lam", 4), ("b_r", NG + NE)):
    PARAM[_n] = (_at, _at + _w)
    _at += _w
N_PARAM = _at


def build(nc, consts, dfts, params, x, ctx_in, w_mod, w_in, b_v, w_fourier, w_pw, w_out, ln_a, ln_f,
          w_r, w_gate, w_up, w_down, out):
    stack = ExitStack()
    with stack:
        arena = stack.enter_context(nc.sbuf_tensor("arena", [P, 207 * 256], F32))

        def at(kb, *shape):
            lo = int(kb * 256)
            n = math.prod(shape)
            v = arena[:, lo:lo + n]
            if len(shape) == 2:
                v = v.rearrange("p (a b) -> p a b", b=shape[1])
            if len(shape) == 3:
                v = v.rearrange("p (a b c) -> p a b c", b=shape[1], c=shape[2])
            return v

        sem = lambda name: stack.enter_context(nc.semaphore(name))
        bank = [stack.enter_context(nc.psum_tensor(f"bank{i}", [P, 512], F32)) for i in range(8)]
        row_dram = nc.dram_tensor("normed_rows", (S, D), F32, kind="Internal").ap()
        slot_dram = nc.dram_tensor("slot_table", (B * NB, 1), I32, kind="Internal").ap()
        y_dram = nc.dram_tensor("expert_rows", (2 * S, D), F32, kind="Internal").ap()

        K_ = at(193, N_CONST)
        cst = lambda n: K_[:, CONST[n][0]:CONST[n][1]]
        P_ = at(193 + N_CONST / 256, N_PARAM)
        par = lambda n: P_[:, PARAM[n][0]:PARAM[n][1]]
        base = 193 + (N_CONST + N_PARAM) / 256
        mods = at(base, N_MODT, 2)
        base += N_MODT * 2 / 256
        wr = at(base, KD, NG + NE)
        base += KD * (NG + NE) / 256
        silu_c = at(base, KD, 2)
        base += KD * 2 / 256
        stats = at(base, 6, 4, 6)
        base += 144 / 256
        mv = at(base, 6, 2)
        rstd = at(base + 12 / 256, 6, 1)
        half = at(base + 18 / 256, 8)
        qb8 = at(base + 26 / 256, 8)
        lamt = at(base + 34 / 256, 8)
        g08 = at(base + 42 / 256, 1)
        nmax = at(base + 43 / 256, 64, 1)
        zsum = at(base + 107 / 256, 64, 1)
        rz = at(base + 171 / 256, 64, 1)
        wtok = at(base + 235 / 256, TS, 2)
        assert base + 243 / 256 <= 207
        ident, ones, upper = cst("ident"), cst("ones"), cst("upper")

        fill_i = at(144, NB).bitcast(I32)
        hT = at(0, KD, NT)
        ring = at(48, 6, KD, P)
        xn = at(96, 6, D)
        uT = at(96, NF, S)
        ab = at(104, TS, NF, 2 * P)
        dft_s = at(120, TS, 2, S)
        yT = at(136, NF, S)
        wf = at(144, NF, S)
        wpw = at(104, NCV, S)
        cmean, crstd = at(96, S), at(98, TS)
        rope_raw, rope_swap = at(112, 2, S), at(116, 2, S)
        V = at(96, TS + TC, HEADS * P)
        KT = at(120, HEADS, NT)
        QT = at(144, HEADS, S)
        mixT = at(160, KD, S)
        sig = at(168, NCV, S)
        glu = at(176, NCV, UW)
        conv = at(176 + NCV * UW / 256, NCV, S)
        bv_b = at(176, HEADS * P)
        AT = at(0, 2, 6, S)
        E = at(24, 2, 2, NT)
        o_sq, o_var = at(36, S), at(38, TS)
        zpart = at(40, 128, 1)
        Z = at(0, TS, D)
        lna_b = at(32, 2, D)
        zT = at(96, 2, S)
        XH = at(100, TS, D)
        h2 = at(132, 2, S)
        rt = 136
        lg = at(rt, TS, NG + NE)
        gl = at(rt + 1, TS, NG)
        gs = at(rt + 1.25, TS, NG)
        r1 = at(rt + 1.5, TS, 1)
        r2 = at(rt + 1.75, TS, 1)
        r3 = at(rt + 2, TS, 1)
        le = at(rt + 2.25, TS, EG)
        t8 = at(rt + 2.5, TS, EG)
        oh = at(rt + 3, 2, TS, EG)
        O = at(rt + 4, 2, TS, NE)
        Osum = at(rt + 5, TS, NE)
        cnt = at(rt + 6, NE)
        nblk = at(rt + 6.25, NE)
        cum = at(rt + 6.5, NE)
        act_e = at(rt + 6.75, NE)
        ordn = at(rt + 7, NE)
        pst = at(rt + 7.25, NE)
        prk = at(rt + 7.5, TS, NE)
        t32 = at(rt + 8, TS, NE)
        slot = at(rt + 8.5, 2, TS)
        addr = at(rt + 8.75, 2, TS)
        vali = at(rt + 9, 2 * TS).bitcast(I32)
        addri = at(rt + 9.25, 2 * TS).bitcast(I32)
        sloti = at(rt + 9.5, 2 * TS).bitcast(I32)
        colf = at(rt + 9.75, 2 * TS)
        big = at(rt + 10, NB, NE)
        bigb = at(rt + 20, NE, NE)[0:1]
        elist = at(rt + 16, NE)
        clist = at(rt + 16.25, NE)
        jlist = at(rt + 16.5, NB)
        tab = at(rt + 17, 2 + 2 * NE + NB).bitcast(I32)
        slots_i = at(rt + 18, NB).bitcast(I32)
        gidx_i = at(rt + 18.5, NB).bitcast(I32)
        cnti = at(rt + 19.5, NE).bitcast(I32)
        OFF_E, OFF_C, OFF_J = 2, 2 + NE, 2 + 2 * NE
        X1 = at(160, TS, D)
        W = at(0, 12, 4 * DE)
        xg = at(96, D)
        xgT = at(104, KD, B)
        sil = at(108, KE, B)
        actT = at(109, KE, B)
        yeT = at(110, KD, B)
        ye = at(114, D)
        igat = at(122, 1).bitcast(I32)
        isca = at(122.25, 1).bitcast(I32)
        Y = at(0, TS, 2 * D)
        lnf_b = at(64, 2, D)
        g5 = at(80, D)

        consts_in = sem("consts_in")
        params_in = sem("params_in")
        x_in = [sem(f"x_in{t}") for t in range(6)]
        wr_in = sem("wr_in")
        ring_full = [sem(f"ring_full{s}") for s in range(6)]
        ring_used = [sem(f"ring_used{s}") for s in range(6)]
        mod_bank_free = sem("mod_bank_free")
        tile_bank_free = sem("tile_bank_free")
        silu_ready = sem("silu_ready")
        xn_ready = sem("xn_ready")
        mod1_ready = sem("mod1_ready")
        xt_out = sem("xt_out")
        xt_evac = sem("xt_evac")
        dft_in = sem("dft_in")
        wf_in = sem("wf_in")
        wpw_in = sem("wpw_in")
        bv_in = sem("bv_in")
        f_out = sem("f_out")
        f_evac = sem("f_evac")
        glu_zero = sem("glu_zero")
        a_ready = sem("a_ready")
        sig_ready = sem("sig_ready")
        u_ready = sem("u_ready")
        conv_done = sem("conv_done")
        cstat_out = sem("cstat_out")
        cmean_done = sem("cmean_done")
        csq_ready = sem("csq_ready")
        cvar_done = sem("cvar_done")
        crstd_ready = sem("crstd_ready")
        cnorm_done = sem("cnorm_done")
        csilu_done = sem("csilu_done")
        pw_out = sem("pw_out")
        pw_evac = sem("pw_evac")
        raw_ready = sem("raw_ready")
        raw_free = sem("raw_free")
        act_chain = sem("act_chain")
        dve_chain = sem("dve_chain")
        pool_chain = sem("pool_chain")
        rope_raw_done = sem("rope_raw_done")
        ctx_keys_done = sem("ctx_keys_done")
        rot = sem("rot")
        conv_step = sem("conv_step")
        dve_max = sem("dve_max")
        yeb_half = sem("yeb_half")
        ye_free = sem("ye_free")
        pe_step = sem("pe_step")
        pool_step = sem("pool_step")
        v_tile_out = sem("v_tile_out")
        lam_out = sem("lam_out")
        lam_exp = sem("lam_exp")
        lam_prod = sem("lam_prod")
        sc_out = sem("sc_out")
        mx_done = sem("mx_done")
        e_done = sem("e_done")
        comb_done = sem("comb_done")
        at_out = sem("at_out")
        at_evac = sem("at_evac")
        pv_out = sem("pv_out")
        o_copied = sem("o_copied")
        o_squared = sem("o_squared")
        oss_out = sem("oss_out")
        ovar_done = sem("ovar_done")
        orow_out = sem("orow_out")
        orstd_ready = sem("orstd_ready")
        att_done = sem("att_done")
        wo_out = sem("wo_out")
        zt_ready = sem("zt_ready")
        zt_out = sem("zt_out")
        z_added = sem("z_added")
        xres_in = sem("xres_in")
        lna_in = sem("lna_in")
        z_rstd_need = sem("z_rstd_need")
        z_rstd_ready = sem("z_rstd_ready")
        xh_ready = sem("xh_ready")
        rows_out = sem("rows_out")
        h_out = sem("h_out")
        h_evac = sem("h_evac")
        logits_out = sem("logits_out")
        gexp_need = sem("gexp_need")
        gexp_done = sem("gexp_done")
        o_ready = sem("o_ready")
        rank_out = sem("rank_out")
        fill_ready = sem("fill_ready")
        fill_done = sem("fill_done")
        addr_ready = sem("addr_ready")
        slots_scattered = sem("slots_scattered")
        slots_in = sem("slots_in")
        table_ready = sem("table_ready")
        gidx_ready = sem("gidx_ready")
        w_full = [sem(f"w_full{c}") for c in range(12)]
        w_used = [sem(f"w_used{c}") for c in range(12)]
        idx_ready = sem("idx_ready")
        gathered = sem("gathered")
        xg_turned = sem("xg_turned")
        xg_scaled = sem("xg_scaled")
        xgT_ready = sem("xgT_ready")
        gate_out = sem("gate_out")
        up_out = sem("up_out")
        silu_done = sem("silu_done")
        act_ready = sem("act_ready")
        down_out = sem("down_out")
        yeT_a = sem("yeT_a")
        yeT_b = sem("yeT_b")
        ye_out = sem("ye_out")
        ye_a = sem("ye_a")
        ye_b = sem("ye_b")
        isca_ready = sem("isca_ready")
        scattered = sem("scattered")
        y_in = [sem(f"y_in{t}") for t in range(TS)]
        lnf_in = sem("lnf_in")
        g5_out = sem("g5_out")
        g5_ready = sem("g5_ready")
        w0_done = sem("w0_done")
        fin_need = sem("fin_need")
        fin_rstd = sem("fin_rstd")
        fin_ready = sem("fin_ready")
        out_done = sem("out_done")

        FAG_IT, QK_IT = 6, 4
        MOD_IT = FAG_IT + 2 * QK_IT
        S1_IT, S1_TAIL = N_MOD01 // 6, N_MOD01 % 6
        filled = lambda s: S1_IT + (s < S1_TAIL)
        ATT_STEPS = 32
        head_at = lambda s, lag: (s - lag) // 4 if s >= lag and (s - lag) % 4 == 3 and (s - lag) // 4 < HEADS else None

        block = stack.enter_context(nc.Block())

        @block.sync
        def _(sp):
            sp.dma_start(P_, params).then_inc(params_in, 16)
            sp.dma_start(K_, consts).then_inc(consts_in, 16)
            for t in range(TS):
                sp.dma_start(xn[:, t, :], x[t * P:(t + 1) * P, :]).then_inc(x_in[t], 16)
            for t in range(TC):
                sp.dma_start(xn[:, TS + t, :], ctx_in[t * P:(t + 1) * P, :]).then_inc(x_in[TS + t], 16)

            for s in range(6):
                sp.sem_inc(ring_used[s], 1)
            for c in range(12):
                sp.sem_inc(w_used[c], 1)

            def load(s, src, n):
                sp.wait_ge(ring_used[s], n)
                sp.dma_start(ring[:, s, :, :], src).then_inc(ring_full[s], 16)

            with sp.Fori(0, S1_IT) as i:
                for s in range(6):
                    load(s, w_mod[bass.ds(i * 6 + s, 1), :, :].rearrange("o p n -> p (o n)"), i + 1)
            for s in range(S1_TAIL):
                load(s, w_mod[S1_IT * 6 + s], filled(s))
            with sp.Fori(0, MOD_IT) as j:
                for s in range(6):
                    if s % 3 == 0:
                        src = w_in[bass.ds(j * 2 + s // 3, 1), :, :]
                    else:
                        src = w_mod[bass.ds(j * 4 + (N_MOD01 + s - 1 - s // 3), 1), :, :]
                    load(s, src.rearrange("o p n -> p (o n)"), j + (filled(s) + 1))
            for g in range(2):
                for s in range(4):
                    load(s, w_in[28 + 4 * g + s], filled(s) + MOD_IT + g + 1)
                for q in range(4):
                    s = 4 + q % 2
                    load(s, w_mod[N_MOD01 + 4 * MOD_IT + 4 * g + q], filled(s) + MOD_IT + 2 * g + q // 2 + 1)
            sp.dma_start(wr.rearrange("p k n -> p (k n)"), w_r).then_inc(wr_in, 16)
            wo_base = [filled(s) + MOD_IT + (2 if s < 4 else 4) for s in range(6)]
            for m in range(6):
                load(m, w_out[m], wo_base[m] + 1)
            sp.wait_ge(att_done, HEADS)
            sp.dma_start(Z, x.rearrange("(t p) d -> p t d", p=P)).then_inc(xres_in, 16)
            for n in range(2):
                sp.dma_start(lna_b[:, n, :], ln_a[n:n + 1, :].to_broadcast([P, D])).then_inc(lna_in, 16)
            for m in range(6, KD):
                load(m % 6, w_out[m], wo_base[m % 6] + m // 6 + 1)
            for t in range(TS):
                sp.wait_ge(xh_ready, t + 1)
                sp.dma_start(row_dram[t * P:(t + 1) * P, :], XH[:, t, :]).then_inc(rows_out, 16)
            sp.wait_ge(slots_scattered, 16 * 2 * TS)
            sp.dma_start(slots_i[0:B, :], slot_dram.rearrange("(p n) o -> p (n o)", n=NB)).then_inc(slots_in, 16)
            sp.wait_ge(table_ready, 1)
            n_exp = sp.value_load(tab[0:1, 0:1], min_val=1, max_val=NE)
            with sp.Fori(0, n_exp) as j:
                e = sp.value_load(tab[0:1, bass.ds(j + OFF_E, 1)], min_val=0, max_val=NE - 1)
                before = sp.value_load(tab[0:1, bass.ds(j + OFF_C, 1)], min_val=0, max_val=NB)
                for c in range(12):
                    sp.wait_ge(w_used[c], before + 1)
                    if c < 8:
                        w = w_gate if c < 4 else w_up
                        src = w[bass.ds(e, 1), (c % 4) * 4 * P:(c % 4 + 1) * 4 * P, :].rearrange("o (k p) n -> p (o k) n", p=P)
                        dst = W[:, c, :].rearrange("p (k n) -> p k n", k=4)
                    else:
                        src = w_down[bass.ds(e, 1), (c - 8) * P:(c - 7) * P, :].rearrange("o p n -> p (o n)")
                        dst = W[:, c, :]
                    sp.dma_start(dst, src).then_inc(w_full[c], 16)
            n_blk = sp.value_load(tab[0:1, 1:2], min_val=1, max_val=NB - 1)
            sp.wait_ge(scattered, n_blk * 16)
            yv = y_dram.rearrange("(t p k) d -> t p (k d)", p=P, k=2)
            for t in range(TS):
                sp.dma_start(Y[:, t, :], yv[t]).then_inc(y_in[t], 16)
            for n in range(2):
                sp.dma_start(lnf_b[:, n, :], ln_f[n:n + 1, :].to_broadcast([P, D])).then_inc(lnf_in, 16)
            for t in range(TS):
                sp.wait_ge(fin_ready, t + 1)
                sp.dma_start(out[t * P:(t + 1) * P, :], X1[:, t, :]).then_inc(out_done, 16)
            sp.wait_ge(out_done, 16 * TS)

        @block.tensor
        def _(pe):
            def mod_tile(s, n, b, free):
                pe.wait_ge(ring_full[s], n * 16)
                pe.wait_ge(mod_bank_free, free)
                for k in range(KD):
                    mm = nc.tensor.matmul(bank[4 + b][:, 0:2], ring[:, s, k, :], silu_c[:, k, :],
                                          start=(k == 0), stop=(k == KD - 1))
                mm.then_inc(ring_used[s], 1)

            pe.wait_ge(consts_in, 16)
            pe.wait_ge(silu_ready, 1)
            with pe.Fori(0, S1_IT) as i:
                for s in range(6):
                    mod_tile(s, i + 1, s % 2, i * 6 + s + 1)
            for s in range(S1_TAIL):
                mod_tile(s, filled(s), s % 2, S1_IT * 6 + s + 1)

            pe.wait_ge(lam_prod, 1)
            nc.tensor.matmul(bank[7][:, 0:2], ones[0:DQ, :], lamt[0:DQ, 0:2], start=True, stop=True).then_inc(lam_out, 1)

            for k in range(KD):
                for part, tiles in enumerate((range(TS), range(TS, TS + TC))):
                    n = 2 * k + part
                    if n >= 4:
                        pe.wait_ge(xt_evac, n - 3)
                    for i, t in enumerate(tiles):
                        if k == 0:
                            pe.wait_ge(xn_ready, t + 1)
                        mm = nc.tensor.transpose(bank[n % 4][:, i * P:(i + 1) * P], xn[:, t, k * P:(k + 1) * P], ident)
                    mm.then_inc(xt_out, 1)
            pe.wait_ge(xt_evac, 2 * KD)

            def in_tile(s, n, b, free, with_ctx):
                pe.wait_ge(ring_full[s], n * 16)
                pe.wait_ge(tile_bank_free, free)
                for k in range(KD):
                    mm = nc.tensor.matmul(bank[b][:, :], ring[:, s, k, :], hT[:, k, 0:S], start=(k == 0), stop=(k == KD - 1))
                    if with_ctx:
                        mm = nc.tensor.matmul(bank[2 + b][:, 0:C], ring[:, s, k, :], hT[:, k, S:NT],
                                              start=(k == 0), stop=(k == KD - 1))
                mm.then_inc(ring_used[s], 1)

            def project(j0, count, with_ctx):
                with pe.Fori(j0, j0 + count) as j:
                    for u in range(2):
                        in_tile(3 * u, j + (filled(3 * u) + 1), u, j * 2 + u + 1, with_ctx)
                        for q in range(2):
                            s = 3 * u + 1 + q
                            mod_tile(s, j + (filled(s) + 1), q, j * 4 + (N_MOD01 + 2 * u + q + 1))

            def spread(b, col, done):
                for t in range(TS):
                    mm = nc.tensor.matmul(bank[b][:, t * P:(t + 1) * P], col[:, t:t + 1].to_broadcast([P, P]), ident,
                                          start=True, stop=True)
                mm.then_inc(done, 1)

            project(0, FAG_IT, False)

            pe.wait_ge(f_evac, NF)
            pe.wait_ge(lam_exp, 1)
            nf = 0
            for t in range(TS):
                for h in range(2):
                    if nf >= 2:
                        pe.wait_ge(f_evac, NF + nf - 1)
                    for g in range(2):
                        mm = nc.tensor.matmul(bank[6 + nf % 2][:, g * 2 * P:(g + 1) * 2 * P],
                                              uT[:, 2 * h + g, t * P:(t + 1) * P], cst("dftc"), start=True, stop=True)
                    mm.then_inc(f_out, 1)
                    nf += 1
            pe.wait_ge(dft_in, 16)
            pe.wait_ge(f_evac, NF + nf)
            for g in range(NF):
                if g >= 2:
                    pe.wait_ge(f_evac, NF + nf - 1)
                for t in range(TS):
                    for r in range(2):
                        mm = nc.tensor.matmul(bank[6 + nf % 2][:, :], ab[:, t, g, r * P:(r + 1) * P], dft_s[:, t, r, :],
                                              start=(t == 0 and r == 0), stop=(t == TS - 1 and r == 1))
                mm.then_inc(f_out, 1)
                nf += 1
            pe.wait_ge(wf_in, 16)
            pe.wait_ge(f_evac, NF + nf)
            for m in range(NF):
                if m >= 2:
                    pe.wait_ge(f_evac, NF + nf - 1)
                for k in range(NF):
                    mm = nc.tensor.matmul(bank[6 + nf % 2][:, :], wf[:, k, m * P:(m + 1) * P], yT[:, k, :],
                                          start=(k == 0), stop=(k == NF - 1))
                mm.then_inc(f_out, 1)
                nf += 1

            project(FAG_IT, QK_IT, False)

            pe.wait_ge(conv_done, NCV)
            pe.wait_ge(f_evac, NF + nf)
            for k in range(NCV):
                mm = nc.tensor.matmul(bank[6][:, :], ones, conv[:, k, :], start=(k == 0), stop=(k == NCV - 1))
            mm.then_inc(cstat_out, 1)
            pe.wait_ge(csq_ready, NCV)
            for t in range(TS):
                for k in range(NCV):
                    mm = nc.tensor.matmul(bank[7][:, t:t + 1], sig[:, k, t * P:(t + 1) * P], ones[:, 0:1], start=(k == 0), stop=(k == NCV - 1))
            mm.then_inc(cstat_out, 1)
            pe.wait_ge(crstd_ready, 1)
            spread(7, crstd, cstat_out)
            pe.wait_ge(wpw_in, 16)
            pe.wait_ge(csilu_done, NCV)
            for m in range(NCV):
                if m >= 2:
                    pe.wait_ge(pw_evac, m - 1)
                for k in range(NCV):
                    mm = nc.tensor.matmul(bank[6 + m % 2][:, :], wpw[:, k, m * P:(m + 1) * P], conv[:, k, :],
                                          start=(k == 0), stop=(k == NCV - 1))
                mm.then_inc(pw_out, 1)

            project(FAG_IT + QK_IT, QK_IT, True)

            for g in range(2):
                n_in = 28 + 6 * g
                for s in range(4):
                    pe.wait_ge(ring_full[s], 16 * (filled(s) + MOD_IT + g + 1))
                for t in range(TS + TC):
                    pe.wait_ge(tile_bank_free, n_in + t + 1)
                    for k in range(KD):
                        mm = nc.tensor.matmul(bank[t % 2][:, :].rearrange("p (s n) -> p s n", n=P), hT[:, k, t * P:(t + 1) * P],
                                              ring[:, 0:4, k, :], start=(k == 0), stop=(k == KD - 1))
                    mm.then_inc(v_tile_out, 1)
                for s in range(4):
                    if s == 0:
                        pe.wait_ge(v_tile_out, 6 * (g + 1))
                    pe.sem_inc(ring_used[s], 1)
                for q in range(4):
                    s = 4 + q % 2
                    mod_tile(s, filled(s) + MOD_IT + 2 * g + q // 2 + 1, q % 2, N_MOD01 + 4 * MOD_IT + 4 * g + q + 1)
            pe.wait_ge(mod_bank_free, N_MODT + 2)
            pe.wait_ge(raw_free, 2 * HEADS + 2)
            pe.wait_ge(tile_bank_free, 28 + 12 + 2)

            for s in range(ATT_STEPS + 6):
                if s < ATT_STEPS:
                    h, qb = divmod(s, TS)
                    for m in range(2):
                        if s >= 1:
                            pe.wait_ge(e_done, 2 * (s - 1) + m + 1)
                        rows = slice(m * DQ, (m + 1) * DQ)
                        q = QT[rows, h, qb * P:(qb + 1) * P]
                        nc.tensor.matmul(bank[2 * m][:, :], q, KT[rows, h, 0:S], start=True, stop=True)
                        nc.tensor.matmul(bank[2 * m + 1][:, 0:C], q, KT[rows, h, S:NT], start=True, stop=True)\
                            .then_inc(sc_out, 1)
                if 1 <= s <= ATT_STEPS:
                    u = s - 1
                    pe.wait_ge(comb_done, u + 1)
                    if u >= 1:
                        pe.wait_ge(at_evac, 2 * u)
                    for kt in range(TS + TC):
                        mm = nc.tensor.transpose(bank[4 + kt // 4][:, (kt % 4) * P:(kt % 4 + 1) * P],
                                                 E[:, u % 2, 0, kt * P:(kt + 1) * P], ident)
                        if kt in (3, 5):
                            mm.then_inc(at_out, 1)
                h = head_at(s, 2)
                if h is not None:
                    pe.wait_ge(at_evac, 8 * (h + 1))
                    if h >= 1:
                        pe.wait_ge(o_copied, h)
                    for kt in range(TS + TC):
                        mm = nc.tensor.matmul(bank[6][:, :], V[:, kt, h * P:(h + 1) * P], AT[:, h % 2, kt, :],
                                              start=(kt == 0), stop=(kt == TS + TC - 1))
                    mm.then_inc(pv_out, 1)
                h = head_at(s, 4)
                if h is not None:
                    pe.wait_ge(o_squared, h + 1)
                    if h >= 1:
                        pe.wait_ge(att_done, h)
                    for qb in range(TS):
                        mm = nc.tensor.matmul(bank[7][:, qb:qb + 1], o_sq[:, qb * P:(qb + 1) * P], ones[:, 0:1], start=True, stop=True)
                    mm.then_inc(oss_out, 1)
                h = head_at(s, 5)
                if h is not None:
                    pe.wait_ge(orstd_ready, h + 1)
                    spread(7, o_var, orow_out)
            pe.wait_ge(att_done, HEADS)

            wo_base = [filled(s) + MOD_IT + (2 if s < 4 else 4) for s in range(6)]

            def turn(m):
                pe.wait_ge(zt_ready, m + 1)
                if m >= 2:
                    pe.wait_ge(z_added, m - 1)
                for t in range(TS):
                    mm = nc.tensor.transpose(bank[4 + m % 2][:, t * P:(t + 1) * P], zT[:, m % 2, t * P:(t + 1) * P], ident)
                mm.then_inc(zt_out, 1)

            for m in range(KD):
                s = m % 6
                pe.wait_ge(ring_full[s], 16 * (wo_base[s] + m // 6 + 1))
                if m >= 2:
                    pe.wait_ge(zt_ready, m - 1)
                for k in range(KD):
                    mm = nc.tensor.matmul(bank[m % 2][:, :], ring[:, s, k, :], mixT[:, k, :], start=(k == 0), stop=(k == KD - 1))
                mm.then_inc(ring_used[s], 1)
                if m >= 1:
                    turn(m - 1)
            turn(KD - 1)
            def logits(k):
                pe.wait_ge(h_evac, k + 1)
                for t in range(TS):
                    mm = nc.tensor.matmul(bank[2][:, t * (NG + NE):(t + 1) * (NG + NE)], h2[:, k % 2, t * P:(t + 1) * P],
                                          wr[:, k, :], start=(k == 0 and t == 0), stop=(k == KD - 1), skip_group_check=True)
                return mm

            pe.wait_ge(wr_in, 16)
            for k in range(KD):
                if k >= 2:
                    pe.wait_ge(h_evac, k - 1)
                for t in range(TS):
                    if k == 0:
                        pe.wait_ge(xh_ready, t + 1)
                    mm = nc.tensor.transpose(bank[k % 2][:, t * P:(t + 1) * P], XH[:, t, k * P:(k + 1) * P], ident)
                mm.then_inc(h_out, 1)
                if k >= 1:
                    logits(k - 1)
            logits(KD - 1).then_inc(logits_out, 1)
            pe.wait_ge(o_ready, 1)
            for t in range(TS):
                for tt in range(t + 1):
                    nc.tensor.matmul(bank[3][:, t * NE:(t + 1) * NE], upper if tt == t else ones, Osum[:, tt, :],
                                     start=(tt == 0), stop=(tt == t))
            for t in range(TS):
                mm = nc.tensor.matmul(bank[3][:, TS * NE:(TS + 1) * NE], ones, Osum[:, t, :], start=(t == 0), stop=(t == TS - 1))
            mm.then_inc(rank_out, 1)

            pe.wait_ge(table_ready, 1)
            n_blk = pe.value_load(tab[0:1, 1:2], min_val=1, max_val=NB - 1)
            with pe.Fori(0, n_blk) as g:
                j = pe.value_load(tab[0:1, bass.ds(g + OFF_J, 1)], min_val=0, max_val=NE - 1)
                pe.wait_ge(gathered, g * 16 + 16)
                pe.wait_ge(ye_b, g + 1)
                pe.sem_inc(pe_step, 1)
                for k in range(KD):
                    mm = nc.tensor.transpose(bank[k // 8][:, (k % 8) * B:(k % 8 + 1) * B], xg[0:B, k * P:(k + 1) * P], ident[0:B, 0:B])
                mm.then_inc(xg_turned, 1)
                pe.wait_ge(xgT_ready, g + 1)
                for half_, bk, done in ((0, 2, gate_out), (1, 3, up_out)):
                    for c in range(4):
                        pe.wait_ge(w_full[4 * half_ + c], j * 16 + 16)
                        w = W[:, 4 * half_ + c, :].rearrange("p (k n) -> p k n", k=4)
                        for kk in range(4):
                            k = 4 * c + kk
                            for m in range(KE):
                                mm = nc.tensor.matmul(bank[bk][:, m * B:(m + 1) * B], w[:, kk, m * P:(m + 1) * P], xgT[:, k, :],
                                                      start=(k == 0 and m == 0), stop=(k == KD - 1), skip_group_check=True)
                        if c < 3:
                            mm.then_inc(w_used[4 * half_ + c], 1)
                    mm.then_inc(done, 1)
                    pe.wait_ge(done, g + 1)
                    pe.sem_inc(w_used[4 * half_ + 3], 1)
                pe.wait_ge(act_ready, g + 2)
                for c in range(4):
                    pe.wait_ge(w_full[8 + c], j * 16 + 16)
                    for m in range(KD):
                        mm = nc.tensor.matmul(bank[4 + m // 8][:, (m % 8) * B:(m % 8 + 1) * B], W[:, 8 + c, m * P:(m + 1) * P],
                                              actT[:, c, :], start=(c == 0 and m % 8 == 0), stop=(c == KE - 1), skip_group_check=True)
                    if c < 3:
                        mm.then_inc(w_used[8 + c], 1)
                mm.then_inc(down_out, 1)
                pe.wait_ge(down_out, g + 1)
                pe.sem_inc(w_used[11], 1)
                pe.wait_ge(yeT_a, g + 1)
                pe.wait_ge(yeT_b, g + 1)
                pe.sem_inc(pe_step, 1)
                for k in range(KD):
                    bk = (6, 7, 0, 1)[k // 4]
                    mm = nc.tensor.transpose(bank[bk][0:B, (k % 4) * P:(k % 4 + 1) * P], yeT[:, k, :], ident)
                    if k % 8 == 7:
                        mm.then_inc(ye_out, 1)
            pe.wait_ge(ye_a, n_blk)
            pe.wait_ge(ye_b, n_blk + 1)
            for k in range(KD):
                mm = nc.tensor.matmul(bank[k // 4][:, (k % 4) * P:(k % 4 + 1) * P], mods[:, 5 * KD + k, 0:1].to_broadcast([P, P]),
                                      ident, start=True, stop=True)
            mm.then_inc(g5_out, 1)

        @block.scalar
        def _(act):
            n_chain = [0]

            def after(ins):
                n_chain[0] += 1
                ins.then_inc(act_chain, 1)
                act.wait_ge(act_chain, n_chain[0])

            act.sem_inc(mod_bank_free, 2)
            act.sem_inc(tile_bank_free, 2)
            act.wait_ge(params_in, 16)
            nc.scalar.activation(silu_c, par("c").rearrange("p (k n) -> p k n", n=2), ACT.Silu).then_inc(silu_ready, 1)

            def mod_evac(s, n, b, t):
                act.wait_ge(ring_used[s], n + 1)
                bias = par("b_mod")[:, t:t + 1] if isinstance(t, int) else par("b_mod")[:, bass.ds(t, 1)]
                dst = mods[:, t, :] if isinstance(t, int) else mods[:, bass.ds(t, 1), :].rearrange("p o n -> p (o n)")
                return nc.scalar.activation(dst, bank[4 + b][:, 0:2], ACT.Identity, bias=bias).then_inc(mod_bank_free, 1)

            with act.Fori(0, S1_IT) as i:
                for s in range(6):
                    mod_evac(s, i + 1, s % 2, i * 6 + s)
            for s in range(S1_TAIL):
                mod_evac(s, filled(s), s % 2, S1_IT * 6 + s)
            act.wait_ge(mod_bank_free, N_MOD01 + 2)
            act.wait_ge(lam_out, 1)
            nc.scalar.activation(lamt[:, 2:4], bank[7][:, 0:2], ACT.Exp).then_inc(lam_exp, 1)
            nc.scalar.activation(mods[:, KD:2 * KD, :], mods[:, KD:2 * KD, :], ACT.Copy, bias=1.0).then_inc(mod1_ready, 1)
            act.wait_ge(mod1_ready, 1)
            for k in range(KD):
                for part in range(2):
                    n = 2 * k + part
                    act.wait_ge(xt_out, n + 1)
                    w = C if part else S
                    nc.scalar.activation(hT[:, k, part * S:part * S + w], bank[n % 4][:, 0:w], ACT.Identity,
                                         bias=mods[:, k, part:part + 1], scale=mods[:, KD + k, part:part + 1]).then_inc(xt_evac, 1)
            act.wait_ge(xt_evac, 2 * KD)
            nc.scalar.mul(qb8, par("b_in")[:, 12:20], ATT_SCALE).then_inc(silu_ready, 1)
            act.wait_ge(silu_ready, 2)

            def mod_pair(j, u):
                for q in range(2):
                    s = 3 * u + 1 + q
                    mod_evac(s, j + (filled(s) + 1), q, j * 4 + (N_MOD01 + 2 * u + q))

            def done_tile(j, u):
                act.wait_ge(ring_used[3 * u], j + (filled(3 * u) + 2))

            b_in = par("b_in")
            for j0, kind in ((0, "f"), (2, "a"), (4, "g")):
                with act.Fori(j0, j0 + 2) as j:
                    for u in range(2):
                        done_tile(j, u)
                        bias = b_in[:, bass.ds(j * 2 + u, 1)]
                        i = (j - j0) * 2 + u
                        if kind == "f":
                            o = nc.scalar.activation(uT[:, bass.ds(i, 1), :].rearrange("p o n -> p (o n)"), bank[u][:, :], ACT.Identity, bias=bias)
                        elif kind == "a":
                            if u == 0:
                                act.wait_ge(glu_zero, 1)
                            o = nc.scalar.activation(glu[:, bass.ds(i, 1), PAD:PAD + S].rearrange("p o n -> p (o n)"), bank[u][:, :], ACT.Identity, bias=bias)
                        else:
                            o = nc.scalar.activation(sig[:, bass.ds(i, 1), :].rearrange("p o n -> p (o n)"), bank[u][:, :], ACT.Sigmoid, bias=bias)
                        o.then_inc(tile_bank_free, 1)
                        mod_pair(j, u)
                act.wait_ge(tile_bank_free, 2 + 2 * (j0 + 2))
                {"f": lambda: act.sem_inc(f_evac, NF), "a": lambda: act.sem_inc(a_ready, 1), "g": lambda: act.sem_inc(sig_ready, 1)}[kind]()

            nf = 0
            for t in range(TS):
                for h in range(2):
                    act.wait_ge(f_out, nf + 1)
                    nc.scalar.copy(ab[:, t, 2 * h:2 * h + 2, :], bank[6 + nf % 2][:, :].rearrange("p (g n) -> p g n", g=2)).then_inc(f_evac, 1)
                    nf += 1
            for g in range(NF):
                act.wait_ge(f_out, nf + 1)
                nc.scalar.copy(yT[:, g, :], bank[6 + nf % 2][:, :]).then_inc(f_evac, 1)
                nf += 1
            for m in range(NF):
                act.wait_ge(f_out, nf + 1)
                nc.scalar.copy(mixT[:, m, :], bank[6 + nf % 2][:, :]).then_inc(f_evac, 1)
                nf += 1

            def rope_source(j0, count, scale, bias_all, bias_at, ctx_too):
                with act.Fori(j0, j0 + count) as j:
                    for u in range(2):
                        done_tile(j, u)
                        i = (j - j0) * 2 + u
                        bias = bias_all[:, bass.ds(i + bias_at, 1)]
                        act.wait_ge(raw_free, j * 2 + (u + 1 - 2 * FAG_IT))
                        main = nc.scalar.activation(rope_raw[:, u, :], bank[u][:, :], ACT.Identity, bias=bias, scale=scale)
                        main.then_inc(rope_raw_done, 1)
                        if ctx_too:
                            nc.scalar.activation(KT[:, bass.ds(i, 1), S:NT].rearrange("p o n -> p (o n)"), bank[2 + u][:, 0:C],
                                                 ACT.Identity, bias=bias).then_inc(ctx_keys_done, 1)
                            act.wait_ge(ctx_keys_done, i + 1)
                        act.wait_ge(rope_raw_done, j * 2 + (u + 1 - 2 * FAG_IT))
                        act.sem_inc(tile_bank_free, 1)
                        for q in range(4):
                            o = nc.scalar.copy(rope_swap[32 * q:32 * q + 32, u, :], rope_raw[32 * (q ^ 1):32 * (q ^ 1) + 32, u, :])
                        o.then_inc(raw_ready, 1)
                        mod_pair(j, u)

            act.sem_inc(raw_free, 2)
            rope_source(FAG_IT, QK_IT, ATT_SCALE, qb8, 0, False)

            for k in range(NCV):
                act.wait_ge(cmean_done, k + 1)
                nc.scalar.activation(sig[:, k, :], conv[:, k, :], ACT.Square).then_inc(csq_ready, 1)
            for k in range(NCV):
                act.wait_ge(cnorm_done, k + 1)
                nc.scalar.activation(conv[:, k, :], conv[:, k, :], ACT.Silu, bias=par("cln_b")[:, k:k + 1],
                                     scale=par("cln_g")[:, k:k + 1]).then_inc(csilu_done, 1)
            for m in range(NCV):
                act.wait_ge(pw_out, m + 1)
                nc.scalar.copy(mixT[:, NCV + m, :], bank[6 + m % 2][:, :]).then_inc(pw_evac, 1)

            rope_source(FAG_IT + QK_IT, QK_IT, 1.0, b_in, 20, True)

            for g in range(2):
                for q in range(4):
                    s = 4 + q % 2
                    mod_evac(s, filled(s) + MOD_IT + 2 * g + q // 2 + 1, q % 2, N_MOD01 + 4 * MOD_IT + 4 * g + q)
            act.wait_ge(mod_bank_free, N_MODT + 2)
            nc.scalar.activation(mods[:, 4 * KD:5 * KD, :], mods[:, 4 * KD:5 * KD, :], ACT.Copy, bias=1.0).then_inc(mod1_ready, 1)

            for s in range(ATT_STEPS + 6):
                if s < ATT_STEPS:
                    for m in range(2):
                        n = 2 * s + m
                        act.wait_ge(mx_done, n + 1)
                        if s >= 2:
                            act.wait_ge(at_out, 2 * (s - 1))
                        for i, (lo, w) in enumerate(((0, S), (S, C))):
                            e = nc.scalar.activation(E[:, s % 2, m, lo:lo + w], bank[2 * m + i][:, 0:w], ACT.Exp, bias=nmax[:, n, :],
                                                     accum_out=zpart[:, 2 * n + i, :])
                        e.then_inc(e_done, 1)
                if 1 <= s <= ATT_STEPS:
                    u = s - 1
                    h, qb = divmod(u, TS)
                    if h >= 2:
                        act.wait_ge(pv_out, h - 1)
                    act.wait_ge(at_out, 2 * u + 1)
                    nc.scalar.copy(AT[:, h % 2, 0:4, qb * P:(qb + 1) * P], bank[4][:, :].rearrange("p (k n) -> p k n", n=P)).then_inc(at_evac, 1)
                    act.wait_ge(at_out, 2 * u + 2)
                    nc.scalar.copy(AT[:, h % 2, 4:6, qb * P:(qb + 1) * P], bank[5][:, 0:C].rearrange("p (k n) -> p k n", n=P)).then_inc(at_evac, 1)
                h = head_at(s, 3)
                if h is not None:
                    act.wait_ge(o_copied, h + 1)
                    if h >= 1:
                        act.wait_ge(oss_out, h)
                    nc.scalar.activation(o_sq, mixT[:, 8 + h, :], ACT.Square).then_inc(o_squared, 1)
            for m in range(KD):
                act.wait_ge(ring_used[m % 6], filled(m % 6) + MOD_IT + (2 if m % 6 < 4 else 4) + m // 6 + 2)
                if m >= 2:
                    act.wait_ge(zt_out, m - 1)
                nc.scalar.activation(zT[:, m % 2, :], bank[m % 2][:, :], ACT.Copy, scale=mods[:, 2 * KD + m, 0:1]).then_inc(zt_ready, 1)
            act.wait_ge(mod1_ready, 2)
            for k in range(KD):
                act.wait_ge(h_out, k + 1)
                nc.scalar.activation(h2[:, k % 2, :], bank[k % 2][:, :], ACT.Identity, bias=mods[:, 3 * KD + k, 0:1],
                                     scale=mods[:, 4 * KD + k, 0:1]).then_inc(h_evac, 1)
            for n in range(2):
                act.wait_ge(gexp_need, n + 1)
                v = (gl, le)[n]
                nc.scalar.activation(v, v, ACT.Exp).then_inc(gexp_done, 1)

            act.wait_ge(table_ready, 1)
            n_blk = act.value_load(tab[0:1, 1:2], min_val=1, max_val=NB - 1)
            with act.Fori(0, n_blk) as g:
                act.wait_ge(gate_out, g + 1)
                act.wait_ge(act_ready, g + 1)
                nc.scalar.activation(sil, bank[2][:, 0:KE * B].rearrange("p (k n) -> p k n", n=B), ACT.Silu).then_inc(silu_done, 1)
                act.wait_ge(down_out, g + 1)
                act.wait_ge(ye_b, g + 1)
                nc.scalar.copy(yeT[:, 0:8, :], bank[4][:, :].rearrange("p (k n) -> p k n", n=B)).then_inc(yeT_a, 1)
                act.wait_ge(ye_out, g * 2 + 1)
                act.wait_ge(ye_free, g + 1)
                nc.scalar.copy(ye[0:B, 0:S], bank[6][0:B, :]).then_inc(act_chain, 1)
                nc.scalar.copy(ye[0:B, S:2 * S], bank[7][0:B, :]).then_inc(ye_a, 1)
            for t in range(TS):
                act.wait_ge(y_in[t], 16)
                nc.scalar.activation(Y[:, t, 0:D], Y[:, t, 0:D], ACT.Copy, scale=wtok[:, t, 0:1]).then_inc(w0_done, 1)

        @block.vector
        def _(dve):
            v = nc.vector
            n_chain = [0]

            def after(ins):
                n_chain[0] += 1
                ins.then_inc(dve_chain, 1)
                dve.wait_ge(dve_chain, n_chain[0])

            after(v.memset(half, -0.5))
            for t in range(TS + TC):
                dve.wait_ge(x_in[t], 16)
                for q in range(4):
                    o = v.bn_stats(stats[:, t, q, :], xn[:, t, q * S:(q + 1) * S])
                after(o)
                after(v.bn_aggr(mv[:, t, :], stats[:, t, :, :].rearrange("p q n -> p (q n)")))
                v.tensor_scalar_add(rstd[:, t, :], mv[:, t, 1:2], EPS).then_inc(z_rstd_need, 1)
                dve.wait_ge(z_rstd_ready, t + 1)
                v.tensor_scalar(xn[:, t, :], xn[:, t, :], mv[:, t, 0:1], rstd[:, t, :], ALU.subtract, ALU.mult).then_inc(xn_ready, 1)
            dve.wait_ge(params_in, 16)
            v.tensor_tensor(lamt[0:DQ, 0:2], par("lam")[0:DQ, 0:2], par("lam")[0:DQ, 2:4], ALU.mult).then_inc(lam_prod, 1)
            v.tensor_scalar_mul(g08, par("subln"), 1.0 - LAM_INIT).then_inc(lam_prod, 1)

            dve.wait_ge(a_ready, 1)
            dve.wait_ge(sig_ready, 1)
            for k in range(NCV):
                after(v.tensor_tensor(glu[:, k, PAD:PAD + S], glu[:, k, PAD:PAD + S], sig[:, k, :], ALU.mult))
            cw = par("conv_w").rearrange("p (k t) -> p k t", t=CW)
            for tap in range(CW):
                for k in range(NCV):
                    if tap == 0:
                        o = v.tensor_scalar(conv[:, k, :], glu[:, k, 0:S], cw[:, k, 0:1], par("conv_b")[:, k:k + 1], ALU.mult, ALU.add)
                    else:
                        dve.wait_ge(conv_step, (tap - 1) * NCV + k + 1)
                        o = v.scalar_tensor_tensor(conv[:, k, :], glu[:, k, tap:tap + S], cw[:, k, tap:tap + 1], conv[:, k, :],
                                                   ALU.mult, ALU.add)
                    o.then_inc(conv_done if tap == CW - 1 else conv_step, 1)
            dve.wait_ge(cstat_out, 1)
            after(v.tensor_scalar_mul(cmean, bank[6][:, :], 1.0 / (NCV * P)))
            for k in range(NCV):
                v.tensor_tensor(conv[:, k, :], conv[:, k, :], cmean, ALU.subtract).then_inc(cmean_done, 1)
            dve.wait_ge(cstat_out, 2)
            v.tensor_scalar(crstd, bank[7][:, 0:TS], 1.0 / (NCV * P), EPS, ALU.mult, ALU.add).then_inc(cvar_done, 1)
            dve.wait_ge(cstat_out, 3)
            for k in range(NCV):
                v.tensor_tensor(conv[:, k, :], conv[:, k, :], bank[7][:, :], ALU.mult).then_inc(cnorm_done, 1)

            dve.wait_ge(bv_in, 16)
            dve.wait_ge(raw_free, 2 * HEADS + 2)
            for g in range(2):
                for t in range(TS + TC):
                    dve.wait_ge(v_tile_out, 6 * g + t + 1)
                    v.tensor_tensor(V[:, t, g * S:(g + 1) * S], bank[t % 2][:, :], bv_b[:, g * S:(g + 1) * S], ALU.add)\
                        .then_inc(tile_bank_free, 1)
            dve.wait_ge(lam_exp, 1)
            after(v.tensor_tensor(lamt[:, 4:5], lamt[:, 3:4], lamt[:, 2:3], ALU.subtract))
            after(v.tensor_scalar_add(lamt[:, 5:6], lamt[:, 4:5], -LAM_INIT))

            def head_copy(h):
                dve.wait_ge(pv_out, h + 1)
                v.tensor_copy(mixT[:, 8 + h, :], bank[6][:, :]).then_inc(o_copied, 1)

            for s in range(ATT_STEPS + 6):
                if s < ATT_STEPS:
                    for m in range(2):
                        n = 2 * s + m
                        dve.wait_ge(sc_out, n + 1)
                        v.reduce_max(zpart[:, 2 * n, :], bank[2 * m][:, :], axis=AX.X).then_inc(dve_max, 1)
                        v.reduce_max(zpart[:, 2 * n + 1, :], bank[2 * m + 1][:, 0:C], axis=AX.X).then_inc(dve_max, 1)
                        dve.wait_ge(dve_max, 2 * n + 2)
                        v.tensor_scalar(nmax[:, n, :], zpart[:, 2 * n, :], zpart[:, 2 * n + 1, :], -1.0, ALU.max, ALU.mult).then_inc(mx_done, 1)
                    dve.wait_ge(e_done, 2 * s + 2)
                    after(v.tensor_tensor(zsum[:, 2 * s:2 * s + 2, :], zpart[:, 4 * s:4 * s + 4:2, :], zpart[:, 4 * s + 1:4 * s + 4:2, :], ALU.add))
                    after(v.reciprocal(rz[:, 2 * s:2 * s + 2, :], zsum[:, 2 * s:2 * s + 2, :]))
                    after(v.tensor_scalar(E[:, s % 2, 1, :], E[:, s % 2, 1, :], rz[:, 2 * s + 1, :], lamt[:, 5:6], ALU.mult, ALU.mult))
                    v.scalar_tensor_tensor(E[:, s % 2, 0, :], E[:, s % 2, 0, :], rz[:, 2 * s, :], E[:, s % 2, 1, :],
                                           ALU.mult, ALU.add).then_inc(comb_done, 1)
                h = head_at(s, 2)
                if h is not None:
                    head_copy(h)
                h = head_at(s, 4)
                if h is not None:
                    dve.wait_ge(oss_out, h + 1)
                    if h >= 1:
                        dve.wait_ge(dve_chain, n_chain[0])
                    v.tensor_scalar(o_var, bank[7][:, 0:TS], 1.0 / P, EPS, ALU.mult, ALU.add).then_inc(ovar_done, 1)
                h = head_at(s, 5)
                if h is not None:
                    dve.wait_ge(orow_out, h + 1)
                    v.scalar_tensor_tensor(mixT[:, 8 + h, :], mixT[:, 8 + h, :], g08, bank[7][:, :], ALU.mult, ALU.mult).then_inc(att_done, 1)

            dve.wait_ge(xres_in, 16)
            for m in range(KD):
                dve.wait_ge(zt_out, m + 1)
                zz = Z[:, :, m * P:(m + 1) * P]
                v.scalar_tensor_tensor(zz, zz, ALPHA, bank[4 + m % 2][:, :].rearrange("p (t n) -> p t n", n=P), ALU.mult, ALU.add)\
                    .then_inc(z_added, 1)
                if m % 4 == 3:
                    dve.wait_ge(z_added, m + 1)
                    q = m // 4
                    for t in range(TS):
                        o = v.bn_stats(stats[:, t, q, :], Z[:, t, q * S:(q + 1) * S])
            after(o)
            dve.wait_ge(lna_in, 32)

            def norm(t, src, dst, n_root, need, ready):
                after(v.bn_aggr(mv[:, t, :], stats[:, t, :, :].rearrange("p q n -> p (q n)")))
                v.tensor_scalar_add(rstd[:, t, :], mv[:, t, 1:2], EPS).then_inc(need, 1)
                dve.wait_ge(ready, n_root)
                return v.tensor_scalar(dst, src, mv[:, t, 0:1], rstd[:, t, :], ALU.subtract, ALU.mult)

            def full_stats(t, src):
                for q in range(4):
                    o = v.bn_stats(stats[:, t, q, :], src[:, q * S:(q + 1) * S])
                after(o)

            for t in range(TS):
                after(norm(t, Z[:, t, :], Z[:, t, :], 6 + 2 * t + 1, z_rstd_need, z_rstd_ready))
                after(v.tensor_tensor(Z[:, t, :], Z[:, t, :], lna_b[:, 0, :], ALU.mult))
                after(v.tensor_tensor(X1[:, t, :], Z[:, t, :], lna_b[:, 1, :], ALU.add))
                full_stats(t, X1[:, t, :])
                norm(t, X1[:, t, :], XH[:, t, :], 6 + 2 * t + 2, z_rstd_need, z_rstd_ready).then_inc(xh_ready, 1)

            bc = lambda ap, *shape: ap.to_broadcast(list(shape))
            after(v.tensor_copy(vali, cst("val")))
            dve.wait_ge(logits_out, 1)
            br = par("b_r").rearrange("p (o n) -> p o n", o=1)
            after(v.tensor_tensor(lg, bank[2][:, 0:TS * (NG + NE)].rearrange("p (t n) -> p t n", t=TS), bc(br, P, TS, NG + NE), ALU.add))
            after(v.tensor_reduce(r1, lg[:, :, 0:NG], axis=AX.X, op=ALU.max))
            v.tensor_tensor(gl, lg[:, :, 0:NG], bc(r1, P, TS, NG), ALU.subtract).then_inc(gexp_need, 1)
            dve.wait_ge(gexp_done, 1)
            after(v.tensor_reduce(r2, gl, axis=AX.X, op=ALU.add))
            after(v.reciprocal(r3, r2))

            def first_max(dst, src, mx, n, tmp):
                first = cst("first")[:, EG - n:EG].rearrange("p (o n) -> p o n", o=1)
                after(v.tensor_tensor(tmp, src, bc(mx, P, TS, n), ALU.is_equal))
                after(v.tensor_tensor(tmp, tmp, bc(first, P, TS, n), ALU.mult))
                after(v.tensor_reduce(r2, tmp, axis=AX.X, op=ALU.max))
                after(v.tensor_tensor(dst, tmp, bc(r2, P, TS, n), ALU.is_equal))

            after(v.tensor_reduce(r1, gl, axis=AX.X, op=ALU.max))
            first_max(gs, gl, r1, NG, t8[:, :, 0:NG])
            after(v.tensor_tensor(le, lg[:, :, NG:NG + EG], bc(gs[:, :, 0:1], P, TS, EG), ALU.mult))
            for g in range(1, NG):
                after(v.tensor_tensor(t8, lg[:, :, NG + g * EG:NG + (g + 1) * EG], bc(gs[:, :, g:g + 1], P, TS, EG), ALU.mult))
                after(v.tensor_tensor(le, le, t8, ALU.add))
            after(v.tensor_reduce(r1, le, axis=AX.X, op=ALU.max))
            v.tensor_tensor(le, le, bc(r1, P, TS, EG), ALU.subtract).then_inc(gexp_need, 1)
            dve.wait_ge(gexp_done, 2)
            after(v.tensor_reduce(r1, le, axis=AX.X, op=ALU.max))
            first_max(oh[:, 0], le, r1, EG, t8)
            after(v.scalar_tensor_tensor(le, oh[:, 0], -2.0, le, ALU.mult, ALU.add))
            after(v.tensor_reduce(r1, le, axis=AX.X, op=ALU.max))
            first_max(oh[:, 1], le, r1, EG, t8)
            after(v.tensor_scalar_add(r2, r1, 1.0))
            after(v.reciprocal(r2, r2))
            after(v.tensor_tensor(wtok[:, :, 0:1], r2, r3, ALU.mult))
            after(v.tensor_tensor(wtok[:, :, 1:2], wtok[:, :, 0:1], r1, ALU.mult))
            for k in range(2):
                for g in range(NG):
                    o = v.tensor_tensor(O[:, k, :, g * EG:(g + 1) * EG], oh[:, k], bc(gs[:, :, g:g + 1], P, TS, EG), ALU.mult)
            after(o)
            v.tensor_tensor(Osum, O[:, 0], O[:, 1], ALU.add).then_inc(o_ready, 1)
            dve.wait_ge(rank_out, 1)
            after(v.tensor_copy(cnti, bank[3][:, TS * NE:(TS + 1) * NE]))
            after(v.tensor_single_scalar(cnti, cnti, B - 1, ALU.add))
            after(v.tensor_single_scalar(cnti, cnti, 6, ALU.logical_shift_right))
            after(v.tensor_copy(nblk, cnti))
            after(v.tensor_tensor_scan(cum, bc(ones[:, 0:1], P, NE), nblk, 0.0, ALU.mult, ALU.add))
            after(v.tensor_single_scalar(act_e, nblk, 0.0, ALU.is_gt))
            after(v.tensor_tensor_scan(ordn, bc(ones[:, 0:1], P, NE), act_e, 0.0, ALU.mult, ALU.add))
            after(v.tensor_tensor(cnt, cum, nblk, ALU.subtract))
            after(v.tensor_scalar_mul(pst, cnt, float(B)))
            after(v.tensor_tensor(prk, bank[3][:, 0:TS * NE].rearrange("p (t n) -> p t n", t=TS),
                                  bc(pst.rearrange("p (o n) -> p o n", o=1), P, TS, NE), ALU.add))
            for k in range(2):
                after(v.tensor_tensor(t32, O[:, k], prk, ALU.mult))
                after(v.tensor_reduce(slot[:, k, :], t32, axis=AX.X, op=ALU.add))
            after(v.tensor_copy(sloti, slot.rearrange("p k t -> p (k t)")))
            after(v.tensor_single_scalar(addri, sloti, 6, ALU.logical_shift_right))
            after(v.tensor_copy(colf, addri))
            after(v.tensor_single_scalar(sloti, sloti, B - 1, ALU.bitwise_and))
            after(v.tensor_copy(addr.rearrange("p k t -> p (k t)"), sloti))
            after(v.scalar_tensor_tensor(addr.rearrange("p k t -> p (k t)"), addr.rearrange("p k t -> p (k t)"), float(NB), colf, ALU.mult, ALU.add))
            v.tensor_copy(addri, addr.rearrange("p k t -> p (k t)")).then_inc(addr_ready, 1)
            after(v.tensor_scalar_add(ordn, ordn, -1.0))
            row = lambda ap: ap[0:1].rearrange("p (o n) -> p o n", o=1)
            col = lambda ap, n: ap[0:1].rearrange("p (n o) -> p n o", o=1)[:, 0:n, :]
            io = cst("iota")
            eq = big[0:1, 0:NE, :]
            after(v.tensor_tensor(eq, row(ordn).to_broadcast([1, NE, NE]), col(io, NE).to_broadcast([1, NE, NE]), ALU.is_equal))
            after(v.tensor_tensor(eq, eq, row(act_e).to_broadcast([1, NE, NE]), ALU.mult))
            after(v.tensor_tensor(bigb, eq, row(io[:, 0:NE]).to_broadcast([1, NE, NE]), ALU.mult))
            after(v.tensor_reduce(elist[0:1], bigb, axis=AX.X, op=ALU.add))
            after(v.tensor_tensor(bigb, eq, row(cnt).to_broadcast([1, NE, NE]), ALU.mult))
            after(v.tensor_reduce(clist[0:1], bigb, axis=AX.X, op=ALU.add))
            after(v.tensor_tensor(big[0:1], row(cum).to_broadcast([1, NB, NE]), col(io, NB).to_broadcast([1, NB, NE]), ALU.is_le))
            after(v.tensor_tensor(big[0:1], big[0:1], row(act_e).to_broadcast([1, NB, NE]), ALU.mult))
            after(v.tensor_reduce(jlist[0:1], big[0:1], axis=AX.X, op=ALU.add))
            v.tensor_scalar_add(tab[0:1, 0:1], ordn[0:1, NE - 1:NE], 1.0)
            v.tensor_copy(tab[0:1, 1:2], cum[0:1, NE - 1:NE])
            v.tensor_copy(tab[0:1, OFF_E:OFF_E + NE], elist[0:1])
            v.tensor_copy(tab[0:1, OFF_C:OFF_C + NE], clist[0:1])
            after(v.tensor_copy(tab[0:1, OFF_J:OFF_J + NB], jlist[0:1]))
            dve.sem_inc(table_ready, 1)
            dve.wait_ge(slots_in, 16)
            v.tensor_single_scalar(gidx_i[0:B], slots_i[0:B], 1, ALU.logical_shift_right).then_inc(gidx_ready, 1)

            dve.sem_inc(ye_b, 1)
            dve.sem_inc(act_ready, 1)
            n_blk = dve.value_load(tab[0:1, 1:2], min_val=1, max_val=NB - 1)
            sc4 = mods[:, 4 * KD:5 * KD, 0:1]
            sh3 = mods[:, 3 * KD:4 * KD, 0:1]
            with dve.Fori(0, n_blk) as g:
                dve.wait_ge(xg_turned, g + 1)
                for hf in range(2):
                    o = v.tensor_tensor(xgT[:, 8 * hf:8 * hf + 8, :], bank[hf][:, :].rearrange("p (k n) -> p k n", n=B),
                                        bc(sc4[:, 8 * hf:8 * hf + 8, :], P, 8, B), ALU.mult)
                    o.then_inc(xg_scaled, 1)
                dve.wait_ge(xg_scaled, g * 2 + 2)
                v.tensor_tensor(xgT, xgT, bc(sh3, P, KD, B), ALU.add).then_inc(xgT_ready, 1)
                dve.wait_ge(up_out, g + 1)
                dve.wait_ge(silu_done, g + 1)
                v.tensor_tensor(actT, bank[3][:, 0:KE * B].rearrange("p (k n) -> p k n", n=B), sil, ALU.mult).then_inc(act_ready, 1)
                dve.wait_ge(down_out, g + 1)
                v.tensor_copy(yeT[:, 8:16, :], bank[5][:, :].rearrange("p (k n) -> p k n", n=B)).then_inc(yeT_b, 1)
                dve.wait_ge(ye_out, g * 2 + 2)
                dve.wait_ge(ye_free, g + 1)
                v.tensor_copy(ye[0:B, 2 * S:3 * S], bank[0][0:B, :]).then_inc(yeb_half, 1)
                v.tensor_copy(ye[0:B, 3 * S:4 * S], bank[1][0:B, :]).then_inc(ye_b, 1)

            dve.wait_ge(g5_out, 1)
            for q in range(4):
                o = v.tensor_copy(g5[:, q * S:(q + 1) * S], bank[q][:, :])
            after(o)
            for t in range(TS):
                y0, y1 = Y[:, t, 0:D], Y[:, t, D:2 * D]
                dve.wait_ge(w0_done, t + 1)
                after(v.scalar_tensor_tensor(y0, y1, wtok[:, t, 1:2], y0, ALU.mult, ALU.add))
                after(v.tensor_tensor(y0, y0, g5, ALU.mult))
                after(v.scalar_tensor_tensor(y0, X1[:, t, :], ALPHA, y0, ALU.mult, ALU.add))
                full_stats(t, y0)
                after(norm(t, y0, y0, t + 1, fin_need, fin_rstd))
                if t == 0:
                    dve.wait_ge(lnf_in, 32)
                after(v.tensor_tensor(y0, y0, lnf_b[:, 0, :], ALU.mult))
                v.tensor_tensor(X1[:, t, :], y0, lnf_b[:, 1, :], ALU.add).then_inc(fin_ready, 1)

        @block.gpsimd
        def _(pool):
            gp = nc.gpsimd
            gp.memset(fill_i[0:B, :], EMPTY).then_inc(fill_ready, 1)
            pool.wait_ge(fill_ready, 1)
            pool.dma_start(slot_dram.rearrange("(p n) o -> p (n o)", n=NB), fill_i[0:B, :]).then_inc(fill_done, 16)
            gp.memset(glu, 0.0).then_inc(glu_zero, 1)

            def root(ap, need, n, ready):
                pool.wait_ge(need, n)
                gp.tensor_tensor(ap, ap, half[:, 0:1].to_broadcast([P, ap.shape[1]]), ALU.pow).then_inc(ready, 1)

            for t in range(TS + TC):
                root(rstd[:, t, :], z_rstd_need, t + 1, z_rstd_ready)
            pool.wait_ge(xt_out, 2 * KD)
            pool.wait_ge(fill_done, 16)
            pool.dma_start(dft_s.rearrange("p t r n -> p (t r n)"), dfts).then_inc(dft_in, 16)
            pool.dma_start(wf, w_fourier.rearrange("(k p) n -> p k n", p=P)).then_inc(wf_in, 16)
            pool.wait_ge(f_out, 8 + NF)
            pool.dma_start(wpw, w_pw.rearrange("(k p) n -> p k n", p=P)).then_inc(wpw_in, 16)

            def rotate(i0, dst, width_at):
                with pool.Fori(0, QK_IT) as i:
                    for u in range(2):
                        pool.wait_ge(raw_ready, i * 2 + (i0 + u + 1))
                        o = dst[:, bass.ds(i * 2 + u, 1), 0:S].rearrange("p o n -> p (o n)")
                        gp.tensor_tensor(rope_raw[:, u, :], rope_raw[:, u, :], cst("cos"), ALU.mult).then_inc(rot, 1)
                        gp.tensor_tensor(rope_swap[:, u, :], rope_swap[:, u, :], cst("sin"), ALU.mult).then_inc(rot, 1)
                        pool.wait_ge(rot, i * 4 + (2 * i0 + 2 * u + 2))
                        gp.tensor_tensor(o, rope_raw[:, u, :], rope_swap[:, u, :], ALU.add).then_inc(raw_free, 1)

            rotate(0, QT, 0)
            root(crstd, cvar_done, 1, crstd_ready)
            pool.wait_ge(pw_out, NCV)
            pool.dma_start(bv_b, b_v.to_broadcast([P, HEADS * P])).then_inc(bv_in, 16)
            rotate(HEADS, KT, 0)
            for h in range(HEADS):
                root(o_var, ovar_done, h + 1, orstd_ready)
            for n in range(2 * TS):
                root(rstd[:, n // 2, :], z_rstd_need, 6 + n + 1, z_rstd_ready)

            pool.wait_ge(addr_ready, 1)
            for k in range(2):
                for t in range(TS):
                    c = k * TS + t
                    pool.indirect_dma_start(slot_dram, bass.IndirectOffsetOnAxis(ap=addri[:, c:c + 1], axis=0),
                                            vali[:, c:c + 1], None).then_inc(slots_scattered, 16)
            pool.wait_ge(gidx_ready, 1)
            pool.wait_ge(rows_out, 16 * TS)
            gp.memset(xg, 0.0).then_inc(idx_ready, 1)
            gp.tensor_copy(igat[0:B], gidx_i[0:B, 0:1]).then_inc(idx_ready, 1)
            pool.wait_ge(idx_ready, 2)

            def gather():
                pool.indirect_dma_start(xg[0:B, :], None, row_dram, bass.IndirectOffsetOnAxis(ap=igat[0:B], axis=0),
                                        bounds_check=S - 1, oob_is_err=False).then_inc(gathered, 16)

            gather()
            pool.sem_inc(ye_free, 1)
            n_blk = pool.value_load(tab[0:1, 1:2], min_val=1, max_val=NB - 1)
            with pool.Fori(0, n_blk) as g:
                pool.wait_ge(xg_turned, g + 1)
                pool.wait_ge(gathered, g * 16 + 16)
                gp.tensor_copy(igat[0:B], gidx_i[0:B, bass.ds(g + 1, 1)]).then_inc(idx_ready, 1)
                pool.wait_ge(idx_ready, g + 3)
                pool.sem_inc(pool_step, 1)
                gather()
                gp.tensor_copy(isca[0:B], slots_i[0:B, bass.ds(g, 1)]).then_inc(isca_ready, 1)
                pool.wait_ge(isca_ready, g + 1)
                pool.wait_ge(ye_a, g + 1)
                pool.wait_ge(ye_b, g + 2)
                pool.sem_inc(pool_step, 1)
                pool.indirect_dma_start(y_dram, bass.IndirectOffsetOnAxis(ap=isca[0:B], axis=0), ye[0:B, :], None,
                                        bounds_check=2 * S - 1, oob_is_err=False).then_inc(scattered, 16)
                pool.wait_ge(scattered, g * 16 + 16)
                pool.sem_inc(ye_free, 1)
            pool.wait_ge(gathered, n_blk * 16 + 16)
            pool.wait_ge(scattered, n_blk * 16)
            for t in range(TS):
                root(rstd[:, t, :], fin_need, t + 1, fin_rstd)


def kernel(**inputs):
    import numpy as np
    import concourse.bacc as bacc
    from concourse.bass_utils import run_bass_kernel_spmd

    f = {k: np.asarray(v) for k, v in inputs.items()}
    consts = np.zeros((P, N_CONST), np.float32)

    def put(name, v):
        lo, hi = CONST[name]
        consts[:, lo:hi] = v

    put("ident", np.eye(P))
    put("ones", 1.0)
    put("upper", np.triu(np.ones((P, P)), 1))
    t = np.arange(S)
    inv = (1.0 / (10000.0 ** (np.arange(16, dtype=np.float32) / np.float32(16)))).astype(np.float32)
    ang = np.concatenate([(t // 64).astype(np.float32)[:, None] * inv, (t % 64).astype(np.float32)[:, None] * inv], -1)
    cos, sin = np.cos(ang).T, np.sin(ang).T
    put("cos", np.concatenate([cos] * 4, 0))
    put("sin", np.concatenate([-sin, sin] * 2, 0))
    th = 2 * np.pi * (np.outer(np.arange(P), np.arange(P)) % P) / P
    put("dftc", np.concatenate([np.cos(th), np.sin(th)], 1) / np.sqrt(P))
    put("iota", np.arange(NB))
    put("first", np.arange(EG, 0, -1))
    put("val", 2 * (np.arange(TS)[None, None, :] * P + np.arange(P)[:, None, None]).repeat(2, 1).reshape(P, 2 * TS)
        + np.repeat(np.arange(2), TS)[None, :])
    ph = 2 * np.pi * (np.outer(t, t) % S) / S
    dfts = (np.stack([np.cos(ph), -np.sin(ph)], 1) / np.sqrt(S)).reshape(TS, P, 2, S).transpose(1, 0, 2, 3)
    dfts = np.ascontiguousarray(dfts.reshape(P, -1), dtype=np.float32)

    params = np.zeros((P, N_PARAM), np.float32)

    def lay(name, v):
        lo, hi = PARAM[name]
        params[:v.shape[0], lo:hi] = v

    cols = lambda v: v.reshape(-1, P).T
    lay("c", np.stack([f["c"][0].reshape(KD, P).T, f["c_ctx"].reshape(KD, P).T], 2).reshape(P, 2 * KD))
    lay("b_in", cols(f["b_in"][0, :28 * P]))
    lay("b_mod", cols(f["b_mod"][0]))
    lay("conv_w", f["conv_w"][0].reshape(CW, NCV, P).transpose(2, 1, 0).reshape(P, NCV * CW))
    lay("conv_b", cols(f["conv_b"][0]))
    lay("cln_g", cols(f["conv_ln_g"][0]))
    lay("cln_b", cols(f["conv_ln_b"][0]))
    lay("subln", cols(f["subln_g"][0]))
    lay("lam", np.stack([f["lam_q1"][0], f["lam_q2"][0], f["lam_k1"][0], f["lam_k2"][0]], 1))
    lay("b_r", np.broadcast_to(np.concatenate([f["b_rg"][0], f["b_re"][0]])[None, :], (P, NG + NE)))
    tiled = lambda w: np.ascontiguousarray(w.reshape(KD, P, -1, P).transpose(2, 1, 0, 3).reshape(-1, P, KD * P))
    arrays = {
        "consts": consts, "dfts": dfts, "params": params, "x": f["x"][0], "ctx_in": f["ctx"][0],
        "w_mod": tiled(f["w_mod"][0]), "w_in": tiled(f["w_in"][0]), "b_v": f["b_in"][:, 28 * P:],
        "w_fourier": f["w_fourier"][0], "w_pw": f["w_pw"][0], "w_out": tiled(f["w_out"][0]),
        "ln_a": np.concatenate([f["ln_a_g"], f["ln_a_b"]], 0), "ln_f": np.concatenate([f["ln_f_g"], f["ln_f_b"]], 0),
        "w_r": np.concatenate([f["w_rg"][0], f["w_re"][0]], 1).reshape(KD, P, NG + NE).transpose(1, 0, 2).reshape(P, -1),
        "w_gate": f["w_gate"][0], "w_up": f["w_up"][0], "w_down": f["w_down"][0],
    }
    arrays = {k: np.ascontiguousarray(v) for k, v in arrays.items()}
    nc = bacc.Bacc("TRN2", target_bir_lowering=False, num_devices=1)
    args = {k: nc.dram_tensor(f"in_{k}", v.shape, mybir.dt.from_np(v.dtype), kind="ExternalInput").ap() for k, v in arrays.items()}
    res = nc.dram_tensor("out_rows", (S, D), F32, kind="ExternalOutput").ap()
    build(nc, out=res, **args)
    r = run_bass_kernel_spmd(nc, [{f"in_{k}": v for k, v in arrays.items()}], core_ids=[0])
    return r.results[0]["out_rows"].reshape(1, S, D)
```

```python
import math
from contextlib import ExitStack

import concourse.bass as bass
from concourse import mybir

F32, I32 = mybir.dt.float32, mybir.dt.int32
ALU = mybir.AluOpType
ACT = mybir.ActivationFunctionType
AX = mybir.AxisListType

P = 128
D = 2048
KD = D // P
S = 512
C = 256
TS, TC = S // P, C // P
NT = S + C
HEADS, DQ = 8, 64
NF, NCV = 4, 4
CW = 31
PAD = CW // 2
UW = S + 2 * PAD
N_IN = 36
N_MODT = 96
N_MOD01 = 2 * KD
NE, NG, EG = 32, 4, 8
DE = 512
KE = DE // P
B = 64
NB = 48
EPS = 1e-6
ALPHA = 2.0 ** 0.25
LAM_INIT = 0.8 - 0.6 * math.exp(0.0)
ATT_SCALE = 1.0 / math.sqrt(DQ)
EMPTY = 8192
CB = 32

CONST = {}
_at = 0
for _n, _w in (("ident", P), ("ones", P), ("upper", P), ("cos", S), ("sin", S), ("dftc", 2 * P),
               ("iota", NB), ("first", EG), ("val", 2 * TS)):
    CONST[_n] = (_at, _at + _w)
    _at += _w
N_CONST = _at
PARAM = {}
_at = 0
for _n, _w in (("c", KD * CB), ("b_in", 28), ("b_mod", N_MODT), ("conv_w", NCV * CW), ("conv_b", NCV),
               ("cln_g", NCV), ("cln_b", NCV), ("subln", 1), ("lam", 4), ("b_r", NG + NE)):
    PARAM[_n] = (_at, _at + _w)
    _at += _w
N_PARAM = _at


def build(nc, consts, dfts, params, x, ctx_in, w_mod, w_in, b_v, w_fourier, w_pw, w_out, ln_a, ln_f,
          w_r, w_gate, w_up, w_down, out):
    stack = ExitStack()
    with stack:
        arena = stack.enter_context(nc.sbuf_tensor("arena", [P, 207 * 256], F32))

        def at(kb, *shape):
            lo = int(kb * 256)
            n = math.prod(shape)
            v = arena[:, lo:lo + n]
            if len(shape) == 2:
                v = v.rearrange("p (a b) -> p a b", b=shape[1])
            if len(shape) == 3:
                v = v.rearrange("p (a b c) -> p a b c", b=shape[1], c=shape[2])
            return v

        sem = lambda name: stack.enter_context(nc.semaphore(name))
        bank = [stack.enter_context(nc.psum_tensor(f"bank{i}", [P, 512], F32)) for i in range(8)]
        row_dram = nc.dram_tensor("normed_rows", (2 * S, D // 2), F32, kind="Internal").ap()
        slot_dram = nc.dram_tensor("slot_table", (B * NB, 1), I32, kind="Internal").ap()
        y_dram = nc.dram_tensor("expert_rows", (4 * S, D // 2), F32, kind="Internal").ap()

        K_ = at(193, N_CONST)
        cst = lambda n: K_[:, CONST[n][0]:CONST[n][1]]
        P_ = at(193 + N_CONST / 256, N_PARAM)
        par = lambda n: P_[:, PARAM[n][0]:PARAM[n][1]]
        base = 193 + (N_CONST + N_PARAM) / 256
        mods = at(base, N_MODT, 2)
        base += N_MODT * 2 / 256
        wr = at(base, KD, NG + NE)
        base += KD * (NG + NE) / 256
        cond = par("c").rearrange("p (k n) -> p k n", n=CB)
        stats = at(base, 6, 4, 6)
        base += 144 / 256
        mv = at(base, 6, 2)
        rstd = at(base + 12 / 256, 6, 1)
        half = at(base + 18 / 256, 8)
        qb8 = at(base + 26 / 256, 8)
        lamt = at(base + 34 / 256, 8)
        g08 = at(base + 42 / 256, 1)
        wtok = at(base + 43 / 256, TS, 2)
        assert base + 51 / 256 <= 207
        ident, ones, upper = cst("ident"), cst("ones"), cst("upper")

        fill_i = at(144, NB).bitcast(I32)
        hT = at(0, KD, NT)
        ring = at(48, 6, KD, P)
        ring_row = at(48, 6, D)
        xn = at(96, 6, D)
        uT = at(96, NF, S)
        ab = at(104, TS, NF, 2 * P)
        dft_s = at(120, TS, 2, S)
        yT = at(136, NF, S)
        wf = at(144, NF, S)
        wpw = at(104, NCV, S)
        cmean, crstd = at(96, S), at(98, TS)
        rope_raw, rope_swap = at(112, 2, S), at(116, 2, S)
        V = at(96, TS + TC, HEADS * P)
        KT = at(120, HEADS, NT)
        QT = at(144, HEADS, S)
        mixT = at(160, KD, S)
        sig = at(168, NCV, S)
        glu = at(176, NCV, UW)
        conv = at(176 + NCV * UW / 256, NCV, S)
        bv_b = at(176, HEADS * P)
        mod_row = [at(kb, S) for kb in (158, 156, 158, 102, 182, 184)]
        AT = at(0, 2, 6, S)
        E = at(24, 2, 2, NT)
        o_sq, o_var = at(36, S), at(38, TS)
        nmax, zsum, rz = at(41, 64, 1), at(41.25, 64, 1), at(41.5, 64, 1)
        zpart = at(40, 128, 1)
        Z = at(0, TS, D)
        lna_b = at(32, 2, D)
        zT = at(96, 2, S)
        XH = at(100, TS, D)
        h2 = at(132, 2, S)
        rt = 136
        lg = at(rt, TS, NG + NE)
        gl = at(rt + 1, TS, NG)
        gs = at(rt + 1.25, TS, NG)
        r1 = at(rt + 1.5, TS, 1)
        r2 = at(rt + 1.75, TS, 1)
        r3 = at(rt + 2, TS, 1)
        le = at(rt + 2.25, TS, EG)
        t8 = at(rt + 2.5, TS, EG)
        oh = at(rt + 3, 2, TS, EG)
        O = at(rt + 4, 2, TS, NE)
        Osum = at(rt + 5, TS, NE)
        cnt = at(rt + 6, NE)
        nblk = at(rt + 6.25, NE)
        cum = at(rt + 6.5, NE)
        act_e = at(rt + 6.75, NE)
        ordn = at(rt + 7, NE)
        pst = at(rt + 7.25, NE)
        prk = at(rt + 7.5, TS, NE)
        t32 = at(rt + 8, TS, NE)
        slot = at(rt + 8.5, 2, TS)
        addr = at(rt + 8.75, 2, TS)
        vali = at(rt + 9, 2 * TS).bitcast(I32)
        addri = at(rt + 9.25, 2 * TS).bitcast(I32)
        sloti = at(rt + 9.5, 2 * TS).bitcast(I32)
        colf = at(rt + 9.75, 2 * TS)
        big = at(rt + 10, NB, NE)
        bigb = at(rt + 20, NE, NE)[0:1]
        elist = at(rt + 16, NE)
        clist = at(rt + 16.25, NE)
        jlist = at(rt + 16.5, NB)
        tab = at(rt + 17, 2 + 2 * NE + NB).bitcast(I32)
        slots_i = at(rt + 18, NB).bitcast(I32)
        gidx_i = at(rt + 18.5, NB).bitcast(I32)
        cnti = at(rt + 19.5, NE).bitcast(I32)
        OFF_E, OFF_C, OFF_J = 2, 2 + NE, 2 + 2 * NE
        X1 = at(160, TS, D)
        H2 = D // 2
        WGU = at(0, 4, 2, 4 * DE)
        WD = at(64, KE, D)
        xg = at(96, H2)
        xgT = at(100, KD, B)
        gu = at(104, DE)
        sil = at(106, KE, B)
        actT = at(107, KE, B)
        ye = at(108, H2)
        igat = at(112, 1).bitcast(I32)
        isca = at(112.25, 1).bitcast(I32)
        Y = at(0, TS, 2, D)
        lnf_b = at(64, 2, D)
        g5 = at(80, D)

        consts_in = sem("consts_in")
        params_in = sem("params_in")
        x_in = [sem(f"x_in{t}") for t in range(6)]
        wr_in = sem("wr_in")
        ring_full = [sem(f"ring_full{s}") for s in range(6)]
        ring_used = [sem(f"ring_used{s}") for s in range(6)]
        mod_row_ready = sem("mod_row_ready")
        mod_turned = sem("mod_turned")
        mod_col_ready = sem("mod_col_ready")
        mod_biased = sem("mod_biased")
        tile_bank_free = sem("tile_bank_free")
        silu_ready = sem("silu_ready")
        xn_ready = sem("xn_ready")
        xt_out = sem("xt_out")
        xt_evac = sem("xt_evac")
        dft_in = sem("dft_in")
        wf_in = sem("wf_in")
        wpw_in = sem("wpw_in")
        bv_in = sem("bv_in")
        f_out = sem("f_out")
        f_evac = sem("f_evac")
        glu_zero = sem("glu_zero")
        a_ready = sem("a_ready")
        sig_ready = sem("sig_ready")
        conv_done = sem("conv_done")
        cstat_out = sem("cstat_out")
        cmean_done = sem("cmean_done")
        csq_ready = sem("csq_ready")
        cvar_done = sem("cvar_done")
        crstd_ready = sem("crstd_ready")
        cnorm_done = sem("cnorm_done")
        csilu_done = sem("csilu_done")
        pw_out = sem("pw_out")
        pw_evac = sem("pw_evac")
        raw_ready = sem("raw_ready")
        raw_free = sem("raw_free")
        dve_chain = sem("dve_chain")
        rope_raw_done = sem("rope_raw_done")
        ctx_keys_done = sem("ctx_keys_done")
        rot = sem("rot")
        mod_one = sem("mod_one")
        conv_step = sem("conv_step")
        dve_max = sem("dve_max")
        ye_free = sem("ye_free")
        pool_step = sem("pool_step")
        v_tile_out = sem("v_tile_out")
        lam_out = sem("lam_out")
        lam_exp = sem("lam_exp")
        lam_prod = sem("lam_prod")
        sc_out = sem("sc_out")
        mx_done = sem("mx_done")
        e_done = sem("e_done")
        comb_done = sem("comb_done")
        at_out = sem("at_out")
        at_evac = sem("at_evac")
        pv_out = sem("pv_out")
        o_copied = sem("o_copied")
        o_squared = sem("o_squared")
        oss_out = sem("oss_out")
        ovar_done = sem("ovar_done")
        orow_out = sem("orow_out")
        orstd_ready = sem("orstd_ready")
        att_done = sem("att_done")
        zt_ready = sem("zt_ready")
        zt_out = sem("zt_out")
        z_added = sem("z_added")
        xres_in = sem("xres_in")
        lna_in = sem("lna_in")
        z_rstd_need = sem("z_rstd_need")
        z_rstd_ready = sem("z_rstd_ready")
        xh_ready = sem("xh_ready")
        rows_out = sem("rows_out")
        h_out = sem("h_out")
        h_evac = sem("h_evac")
        logits_out = sem("logits_out")
        gexp_need = sem("gexp_need")
        gexp_done = sem("gexp_done")
        o_ready = sem("o_ready")
        rank_out = sem("rank_out")
        fill_ready = sem("fill_ready")
        fill_done = sem("fill_done")
        addr_ready = sem("addr_ready")
        slots_scattered = sem("slots_scattered")
        slots_in = sem("slots_in")
        table_ready = sem("table_ready")
        gidx_ready = sem("gidx_ready")
        w_full = [sem(f"w_full{c}") for c in range(8)]
        w_used = [sem(f"w_used{c}") for c in range(8)]
        idx_ready = sem("idx_ready")
        gathered = sem("gathered")
        xg_turned = sem("xg_turned")
        xg_scaled = sem("xg_scaled")
        xgT_ready = sem("xgT_ready")
        gu_ready = sem("gu_ready")
        gu_turned = sem("gu_turned")
        silu_done = sem("silu_done")
        act_ready = sem("act_ready")
        ye_a = sem("ye_a")
        ye_b = sem("ye_b")
        isca_ready = sem("isca_ready")
        scattered = sem("scattered")
        y_in = [sem(f"y_in{t}") for t in range(TS)]
        lnf_in = sem("lnf_in")
        g5_out = sem("g5_out")
        w0_done = sem("w0_done")
        fin_need = sem("fin_need")
        fin_rstd = sem("fin_rstd")
        fin_ready = sem("fin_ready")
        out_done = sem("out_done")

        FAG_IT, QK_IT = 6, 4
        MOD_IT = FAG_IT + 2 * QK_IT
        filled = lambda s: (N_MOD01 - s + 5) // 6
        ATT_STEPS = 32
        head_at = lambda s, lag: (s - lag) // 4 if s >= lag and (s - lag) % 4 == 3 and (s - lag) // 4 < HEADS else None

        block = stack.enter_context(nc.Block())

        @block.sync
        def _(sp):
            sp.dma_start(P_, params).then_inc(params_in, 16)
            sp.dma_start(K_, consts).then_inc(consts_in, 16)
            for t in range(TS):
                sp.dma_start(xn[:, t, :], x[t * P:(t + 1) * P, :]).then_inc(x_in[t], 16)
            for t in range(TC):
                sp.dma_start(xn[:, TS + t, :], ctx_in[t * P:(t + 1) * P, :]).then_inc(x_in[TS + t], 16)

            for s in range(6):
                sp.sem_inc(ring_used[s], 1)
            for c in range(8):
                sp.sem_inc(w_used[c], 1)

            def load(s, src, n):
                sp.wait_ge(ring_used[s], n)
                sp.dma_start(ring[:, s, :, :], src).then_inc(ring_full[s], 16)

            for n in range(N_MOD01):
                load(n % 6, w_mod[n], n // 6 + 1)
            with sp.Fori(0, MOD_IT) as j:
                for s in range(6):
                    if s % 3 == 0:
                        src = w_in[bass.ds(j * 2 + s // 3, 1), :, :]
                    else:
                        src = w_mod[bass.ds(j * 4 + (N_MOD01 + s - 1 - s // 3), 1), :, :]
                    load(s, src.rearrange("o p n -> p (o n)"), j + (filled(s) + 1))
            for g in range(2):
                for s in range(4):
                    load(s, w_in[28 + 4 * g + s], filled(s) + MOD_IT + g + 1)
                for q in range(4):
                    s = 4 + q % 2
                    load(s, w_mod[N_MOD01 + 4 * MOD_IT + 4 * g + q], filled(s) + MOD_IT + 2 * g + q // 2 + 1)
            sp.dma_start(wr.rearrange("p k n -> p (k n)"), w_r).then_inc(wr_in, 16)
            wo_base = [filled(s) + MOD_IT + (2 if s < 4 else 4) for s in range(6)]
            for m in range(6):
                load(m, w_out[m], wo_base[m] + 1)
            sp.wait_ge(att_done, HEADS)
            sp.dma_start(Z, x.rearrange("(t p) d -> p t d", p=P)).then_inc(xres_in, 16)
            for n in range(2):
                sp.dma_start(lna_b[:, n, :], ln_a[n:n + 1, :].to_broadcast([P, D])).then_inc(lna_in, 16)
            for m in range(6, KD):
                load(m % 6, w_out[m], wo_base[m % 6] + m // 6 + 1)
            for t in range(TS):
                sp.wait_ge(xh_ready, t + 1)
                sp.dma_start(row_dram.rearrange("(t p h) d -> t p (h d)", t=TS, h=2)[t], XH[:, t, :]).then_inc(rows_out, 16)
            sp.wait_ge(slots_scattered, 16 * 2 * TS)
            for h in range(2):
                sp.dma_start(slots_i[h * B:(h + 1) * B, :], slot_dram.rearrange("(p n) o -> p (n o)", n=NB)).then_inc(slots_in, 16)
            sp.wait_ge(table_ready, 1)
            n_exp = sp.value_load(tab[0:1, 0:1], min_val=1, max_val=NE)
            with sp.Fori(0, n_exp) as j:
                e = sp.value_load(tab[0:1, bass.ds(j + OFF_E, 1)], min_val=0, max_val=NE - 1)
                before = sp.value_load(tab[0:1, bass.ds(j + OFF_C, 1)], min_val=0, max_val=NB)
                for c in range(8):
                    sp.wait_ge(w_used[c], before + 1)
                    if c < 4:
                        for n, w in enumerate((w_gate, w_up)):
                            src = w[bass.ds(e, 1), c * 4 * P:(c + 1) * 4 * P, :].rearrange("o (k p) n -> p (o k) n", p=P)
                            sp.dma_start(WGU[:, c, n, :].rearrange("p (k n) -> p k n", k=4), src).then_inc(w_full[c], 16)
                    else:
                        src = w_down[bass.ds(e, 1), (c - 4) * P:(c - 3) * P, :].rearrange("o p n -> p (o n)")
                        sp.dma_start(WD[:, c - 4, :], src).then_inc(w_full[c], 16)
            n_blk = sp.value_load(tab[0:1, 1:2], min_val=1, max_val=NB - 1)
            sp.wait_ge(scattered, n_blk * 16)
            yv = y_dram.rearrange("(h t p k) d -> t p h k d", h=2, p=P, k=2)
            for t in range(TS):
                for h in range(2):
                    sp.dma_start(Y[:, t, :, h * H2:(h + 1) * H2], yv[t, :, h]).then_inc(y_in[t], 16)
            for n in range(2):
                sp.dma_start(lnf_b[:, n, :], ln_f[n:n + 1, :].to_broadcast([P, D])).then_inc(lnf_in, 16)
            for t in range(TS):
                sp.wait_ge(fin_ready, t + 1)
                sp.dma_start(out[t * P:(t + 1) * P, :], X1[:, t, :]).then_inc(out_done, 16)
            sp.wait_ge(out_done, 16 * TS)

        @block.tensor
        def _(pe):
            taken = [0] * 6

            def take(s):
                taken[s] += 1
                pe.wait_ge(ring_full[s], 16 * taken[s])

            def mod_tile(s, n):
                i, k = divmod(n, KD)
                if k == 0 and i >= 2:
                    pe.wait_ge(mod_col_ready, i - 1)
                take(s)
                for q in range(4):
                    mm = nc.tensor.matmul(bank[4 + i % 2][32 * q:32 * q + 32, :], cond[:, k, :], ring_row[:, s, q * S:(q + 1) * S],
                                          start=(k == 0), stop=(k == KD - 1), tile_position=(0, 32 * q))
                mm.then_inc(ring_used[s], 1)

            def mod_turn(i):
                pe.wait_ge(mod_row_ready, i + 1)
                for q in range(4):
                    mm = nc.tensor.transpose(bank[4 + i % 2][:, q * P:(q + 1) * P], mod_row[i][:, q * P:(q + 1) * P], ident)
                mm.then_inc(mod_turned, 1)

            pe.wait_ge(consts_in, 16)
            pe.wait_ge(silu_ready, 1)
            for n in range(N_MOD01):
                mod_tile(n % 6, n)

            pe.wait_ge(lam_prod, 1)
            nc.tensor.matmul(bank[7][:, 0:2], ones[0:DQ, :], lamt[0:DQ, 0:2], start=True, stop=True).then_inc(lam_out, 1)

            mod_turn(0)
            mod_turn(1)
            for k in range(KD):
                for part, tiles in enumerate((range(TS), range(TS, TS + TC))):
                    n = 2 * k + part
                    if n >= 4:
                        pe.wait_ge(xt_evac, n - 3)
                    for i, t in enumerate(tiles):
                        if k == 0:
                            pe.wait_ge(xn_ready, t + 1)
                        mm = nc.tensor.transpose(bank[n % 4][:, i * P:(i + 1) * P], xn[:, t, k * P:(k + 1) * P], ident)
                    mm.then_inc(xt_out, 1)
            pe.wait_ge(xt_evac, 2 * KD)

            n_in = [0]

            def in_tile(s, b, with_ctx):
                take(s)
                n_in[0] += 1
                pe.wait_ge(tile_bank_free, n_in[0])
                for k in range(KD):
                    mm = nc.tensor.matmul(bank[b][:, :], ring[:, s, k, :], hT[:, k, 0:S], start=(k == 0), stop=(k == KD - 1))
                    if with_ctx:
                        mm = nc.tensor.matmul(bank[2 + b][:, 0:C], ring[:, s, k, :], hT[:, k, S:NT],
                                              start=(k == 0), stop=(k == KD - 1))
                mm.then_inc(ring_used[s], 1)

            def project(j0, count, with_ctx):
                for j in range(j0, j0 + count):
                    for u in range(2):
                        in_tile(3 * u, u, with_ctx)
                        for q in range(2):
                            mod_tile(3 * u + 1 + q, N_MOD01 + 4 * j + 2 * u + q)
                    if j == FAG_IT - 1:
                        mod_turn(2)

            def spread(b, col, done):
                for t in range(TS):
                    mm = nc.tensor.matmul(bank[b][:, t * P:(t + 1) * P], col[:, t:t + 1].to_broadcast([P, P]), ident,
                                          start=True, stop=True)
                mm.then_inc(done, 1)

            project(0, FAG_IT, False)

            pe.wait_ge(f_evac, NF)
            pe.wait_ge(lam_exp, 1)
            nf = 0
            for t in range(TS):
                for h in range(2):
                    if nf >= 2:
                        pe.wait_ge(f_evac, NF + nf - 1)
                    for g in range(2):
                        mm = nc.tensor.matmul(bank[6 + nf % 2][:, g * 2 * P:(g + 1) * 2 * P],
                                              uT[:, 2 * h + g, t * P:(t + 1) * P], cst("dftc"), start=True, stop=True)
                    mm.then_inc(f_out, 1)
                    nf += 1
            pe.wait_ge(dft_in, 16)
            pe.wait_ge(f_evac, NF + nf)
            for g in range(NF):
                if g >= 2:
                    pe.wait_ge(f_evac, NF + nf - 1)
                for t in range(TS):
                    for r in range(2):
                        mm = nc.tensor.matmul(bank[6 + nf % 2][:, :], ab[:, t, g, r * P:(r + 1) * P], dft_s[:, t, r, :],
                                              start=(t == 0 and r == 0), stop=(t == TS - 1 and r == 1))
                mm.then_inc(f_out, 1)
                nf += 1
            pe.wait_ge(wf_in, 16)
            pe.wait_ge(f_evac, NF + nf)
            for m in range(NF):
                if m >= 2:
                    pe.wait_ge(f_evac, NF + nf - 1)
                for k in range(NF):
                    mm = nc.tensor.matmul(bank[6 + nf % 2][:, :], wf[:, k, m * P:(m + 1) * P], yT[:, k, :],
                                          start=(k == 0), stop=(k == NF - 1))
                mm.then_inc(f_out, 1)
                nf += 1

            project(FAG_IT, QK_IT, False)

            pe.wait_ge(conv_done, NCV)
            pe.wait_ge(f_evac, NF + nf)
            for k in range(NCV):
                mm = nc.tensor.matmul(bank[6][:, :], ones, conv[:, k, :], start=(k == 0), stop=(k == NCV - 1))
            mm.then_inc(cstat_out, 1)
            pe.wait_ge(csq_ready, NCV)
            for t in range(TS):
                for k in range(NCV):
                    mm = nc.tensor.matmul(bank[7][:, t:t + 1], sig[:, k, t * P:(t + 1) * P], ones[:, 0:1], start=(k == 0), stop=(k == NCV - 1))
            mm.then_inc(cstat_out, 1)
            pe.wait_ge(crstd_ready, 1)
            spread(7, crstd, cstat_out)
            pe.wait_ge(wpw_in, 16)
            pe.wait_ge(csilu_done, NCV)
            for m in range(NCV):
                if m >= 2:
                    pe.wait_ge(pw_evac, m - 1)
                for k in range(NCV):
                    mm = nc.tensor.matmul(bank[6 + m % 2][:, :], wpw[:, k, m * P:(m + 1) * P], conv[:, k, :],
                                          start=(k == 0), stop=(k == NCV - 1))
                mm.then_inc(pw_out, 1)
            mod_turn(3)

            project(FAG_IT + QK_IT, QK_IT, True)

            for g in range(2):
                for s in range(4):
                    take(s)
                for t in range(TS + TC):
                    n_in[0] += 1
                    pe.wait_ge(tile_bank_free, n_in[0])
                    for k in range(KD):
                        mm = nc.tensor.matmul(bank[t % 2][:, :].rearrange("p (s n) -> p s n", n=P), hT[:, k, t * P:(t + 1) * P],
                                              ring[:, 0:4, k, :], start=(k == 0), stop=(k == KD - 1))
                    mm.then_inc(v_tile_out, 1)
                pe.wait_ge(v_tile_out, 6 * (g + 1))
                for s in range(4):
                    pe.sem_inc(ring_used[s], 1)
                for q in range(4):
                    mod_tile(4 + q % 2, N_MOD01 + 4 * MOD_IT + 4 * g + q)
            mod_turn(4)
            mod_turn(5)
            pe.wait_ge(raw_free, 2 * HEADS + 2)
            pe.wait_ge(tile_bank_free, 28 + 12 + 2)

            for s in range(ATT_STEPS + 6):
                if s < ATT_STEPS:
                    h, qb = divmod(s, TS)
                    for m in range(2):
                        if s >= 1:
                            pe.wait_ge(e_done, 2 * (s - 1) + m + 1)
                        rows = slice(m * DQ, (m + 1) * DQ)
                        q = QT[rows, h, qb * P:(qb + 1) * P]
                        nc.tensor.matmul(bank[2 * m][:, :], q, KT[rows, h, 0:S], start=True, stop=True)
                        nc.tensor.matmul(bank[2 * m + 1][:, 0:C], q, KT[rows, h, S:NT], start=True, stop=True)\
                            .then_inc(sc_out, 1)
                if 1 <= s <= ATT_STEPS:
                    u = s - 1
                    pe.wait_ge(comb_done, u + 1)
                    if u >= 1:
                        pe.wait_ge(at_evac, 2 * u)
                    for kt in range(TS + TC):
                        mm = nc.tensor.transpose(bank[4 + kt // 4][:, (kt % 4) * P:(kt % 4 + 1) * P],
                                                 E[:, u % 2, 0, kt * P:(kt + 1) * P], ident)
                        if kt in (3, 5):
                            mm.then_inc(at_out, 1)
                h = head_at(s, 2)
                if h is not None:
                    pe.wait_ge(at_evac, 8 * (h + 1))
                    if h >= 1:
                        pe.wait_ge(o_copied, h)
                    for kt in range(TS + TC):
                        mm = nc.tensor.matmul(bank[6][:, :], V[:, kt, h * P:(h + 1) * P], AT[:, h % 2, kt, :],
                                              start=(kt == 0), stop=(kt == TS + TC - 1))
                    mm.then_inc(pv_out, 1)
                h = head_at(s, 4)
                if h is not None:
                    pe.wait_ge(o_squared, h + 1)
                    if h >= 1:
                        pe.wait_ge(att_done, h)
                    for qb in range(TS):
                        mm = nc.tensor.matmul(bank[7][:, qb:qb + 1], o_sq[:, qb * P:(qb + 1) * P], ones[:, 0:1], start=True, stop=True)
                    mm.then_inc(oss_out, 1)
                h = head_at(s, 5)
                if h is not None:
                    pe.wait_ge(orstd_ready, h + 1)
                    spread(7, o_var, orow_out)
            pe.wait_ge(att_done, HEADS)

            wo_base = [filled(s) + MOD_IT + (2 if s < 4 else 4) for s in range(6)]

            def turn(m):
                pe.wait_ge(zt_ready, m + 1)
                if m >= 2:
                    pe.wait_ge(z_added, m - 1)
                for t in range(TS):
                    mm = nc.tensor.transpose(bank[4 + m % 2][:, t * P:(t + 1) * P], zT[:, m % 2, t * P:(t + 1) * P], ident)
                mm.then_inc(zt_out, 1)

            for m in range(KD):
                s = m % 6
                pe.wait_ge(ring_full[s], 16 * (wo_base[s] + m // 6 + 1))
                if m >= 2:
                    pe.wait_ge(zt_ready, m - 1)
                for k in range(KD):
                    mm = nc.tensor.matmul(bank[m % 2][:, :], ring[:, s, k, :], mixT[:, k, :], start=(k == 0), stop=(k == KD - 1))
                mm.then_inc(ring_used[s], 1)
                if m >= 1:
                    turn(m - 1)
            turn(KD - 1)
            def logits(k):
                pe.wait_ge(h_evac, k + 1)
                for t in range(TS):
                    mm = nc.tensor.matmul(bank[2][:, t * (NG + NE):(t + 1) * (NG + NE)], h2[:, k % 2, t * P:(t + 1) * P],
                                          wr[:, k, :], start=(k == 0 and t == 0), stop=(k == KD - 1), skip_group_check=True)
                return mm

            pe.wait_ge(wr_in, 16)
            for k in range(KD):
                if k >= 2:
                    pe.wait_ge(h_evac, k - 1)
                for t in range(TS):
                    if k == 0:
                        pe.wait_ge(xh_ready, t + 1)
                    mm = nc.tensor.transpose(bank[k % 2][:, t * P:(t + 1) * P], XH[:, t, k * P:(k + 1) * P], ident)
                mm.then_inc(h_out, 1)
                if k >= 1:
                    logits(k - 1)
            logits(KD - 1).then_inc(logits_out, 1)
            pe.wait_ge(o_ready, 1)
            for t in range(TS):
                for tt in range(t + 1):
                    nc.tensor.matmul(bank[3][:, t * NE:(t + 1) * NE], upper if tt == t else ones, Osum[:, tt, :],
                                     start=(tt == 0), stop=(tt == t))
            for t in range(TS):
                mm = nc.tensor.matmul(bank[3][:, TS * NE:(TS + 1) * NE], ones, Osum[:, t, :], start=(t == 0), stop=(t == TS - 1))
            mm.then_inc(rank_out, 1)

            pe.wait_ge(table_ready, 1)
            n_blk = pe.value_load(tab[0:1, 1:2], min_val=1, max_val=NB - 1)

            def turn_rows(n):
                pe.wait_ge(gathered, n * 16 + 16)
                for k in range(KD // 2):
                    mm = nc.tensor.transpose(bank[k // 4][:, (k % 4) * P:(k % 4 + 1) * P], xg[:, k * P:(k + 1) * P], ident)
                mm.then_inc(xg_turned, 1)

            turn_rows(0)
            with pe.Fori(0, n_blk) as g:
                j = pe.value_load(tab[0:1, bass.ds(g + OFF_J, 1)], min_val=0, max_val=NE - 1)
                pe.wait_ge(xgT_ready, g + 1)
                for c in range(4):
                    pe.wait_ge(w_full[c], j * 32 + 32)
                    for kk in range(4):
                        k = 4 * c + kk
                        for n in range(2):
                            mm = nc.tensor.matmul(bank[2][n * B:(n + 1) * B, :], xgT[:, k, :], WGU[:, c, n, kk * DE:(kk + 1) * DE],
                                                  start=(k == 0), stop=(k == KD - 1), tile_position=(0, n * B))
                    mm.then_inc(w_used[c], 1)
                turn_rows(g + 1)
                pe.wait_ge(gu_ready, g + 1)
                for m in range(KE):
                    mm = nc.tensor.transpose(bank[3][:, m * P:(m + 1) * P], gu[:, m * P:(m + 1) * P], ident)
                mm.then_inc(gu_turned, 1)
                pe.wait_ge(act_ready, g + 1)
                for c in range(KE):
                    pe.wait_ge(w_full[4 + c], j * 16 + 16)
                    for n in range(4):
                        h, b = n % 2, n // 2
                        mm = nc.tensor.matmul(bank[4 + b][h * B:(h + 1) * B, :], actT[:, c, :],
                                              WD[:, c, (2 * h + b) * S:(2 * h + b + 1) * S],
                                              start=(c == 0), stop=(c == KE - 1), tile_position=(0, h * B))
                    mm.then_inc(w_used[4 + c], 1)
            pe.wait_ge(ye_a, n_blk)
            pe.wait_ge(ye_b, n_blk)
            pe.wait_ge(xgT_ready, n_blk + 1)
            for k in range(KD):
                mm = nc.tensor.matmul(bank[k // 4][:, (k % 4) * P:(k % 4 + 1) * P], mods[:, 5 * KD + k, 0:1].to_broadcast([P, P]),
                                      ident, start=True, stop=True)
            mm.then_inc(g5_out, 1)

        @block.scalar
        def _(act):
            act.sem_inc(tile_bank_free, 2)
            act.wait_ge(params_in, 16)
            nc.scalar.activation(cond, cond, ACT.Silu).then_inc(silu_ready, 1)

            ring_need = lambda s, n: act.wait_ge(ring_used[s], n + 1)

            def mod_row_out(i, s, n):
                ring_need(s, n)
                nc.scalar.copy(mod_row[i], bank[4 + i % 2][:, :]).then_inc(mod_row_ready, 1)

            def mod_cols_out(i):
                act.wait_ge(mod_turned, i + 1)
                nc.scalar.copy(mods[:, i * KD:(i + 1) * KD, :].rearrange("p (q c) l -> p c q l", c=4),
                               bank[4 + i % 2][:, :].rearrange("p (c q r) -> p c q r", c=4, q=4)[:, :, :, 0:2]).then_inc(mod_col_ready, 1)

            mod_row_out(0, (KD - 1) % 6, (KD - 1) // 6 + 1)
            mod_row_out(1, (N_MOD01 - 1) % 6, (N_MOD01 - 1) // 6 + 1)
            mod_cols_out(0)
            mod_cols_out(1)
            act.wait_ge(lam_out, 1)
            nc.scalar.activation(lamt[:, 2:4], bank[7][:, 0:2], ACT.Exp).then_inc(lam_exp, 1)
            act.wait_ge(mod_biased, 2)
            for k in range(KD):
                for part in range(2):
                    n = 2 * k + part
                    act.wait_ge(xt_out, n + 1)
                    w = C if part else S
                    nc.scalar.activation(hT[:, k, part * S:part * S + w], bank[n % 4][:, 0:w], ACT.Identity,
                                         bias=mods[:, k, part:part + 1], scale=mods[:, KD + k, part:part + 1]).then_inc(xt_evac, 1)
            act.wait_ge(xt_evac, 2 * KD)
            nc.scalar.mul(qb8, par("b_in")[:, 12:20], ATT_SCALE).then_inc(silu_ready, 1)
            act.wait_ge(silu_ready, 2)

            def done_tile(j, u):
                act.wait_ge(ring_used[3 * u], j + (filled(3 * u) + 2))

            b_in = par("b_in")
            for j0, kind in ((0, "f"), (2, "a"), (4, "g")):
                with act.Fori(j0, j0 + 2) as j:
                    for u in range(2):
                        done_tile(j, u)
                        bias = b_in[:, bass.ds(j * 2 + u, 1)]
                        i = (j - j0) * 2 + u
                        if kind == "f":
                            o = nc.scalar.activation(uT[:, bass.ds(i, 1), :].rearrange("p o n -> p (o n)"), bank[u][:, :], ACT.Identity, bias=bias)
                        elif kind == "a":
                            if u == 0:
                                act.wait_ge(glu_zero, 1)
                            o = nc.scalar.activation(glu[:, bass.ds(i, 1), PAD:PAD + S].rearrange("p o n -> p (o n)"), bank[u][:, :], ACT.Identity, bias=bias)
                        else:
                            o = nc.scalar.activation(sig[:, bass.ds(i, 1), :].rearrange("p o n -> p (o n)"), bank[u][:, :], ACT.Sigmoid, bias=bias)
                        o.then_inc(tile_bank_free, 1)
                act.wait_ge(tile_bank_free, 2 + 2 * (j0 + 2))
                if kind == "a":
                    mod_row_out(2, 5, filled(5) + 4)
                {"f": lambda: act.sem_inc(f_evac, NF), "a": lambda: act.sem_inc(a_ready, 1), "g": lambda: act.sem_inc(sig_ready, 1)}[kind]()

            mod_cols_out(2)
            nf = 0
            for t in range(TS):
                for h in range(2):
                    act.wait_ge(f_out, nf + 1)
                    nc.scalar.copy(ab[:, t, 2 * h:2 * h + 2, :], bank[6 + nf % 2][:, :].rearrange("p (g n) -> p g n", g=2)).then_inc(f_evac, 1)
                    nf += 1
            for g in range(NF):
                act.wait_ge(f_out, nf + 1)
                nc.scalar.copy(yT[:, g, :], bank[6 + nf % 2][:, :]).then_inc(f_evac, 1)
                nf += 1
            for m in range(NF):
                act.wait_ge(f_out, nf + 1)
                nc.scalar.copy(mixT[:, m, :], bank[6 + nf % 2][:, :]).then_inc(f_evac, 1)
                nf += 1

            def rope_source(j0, count, scale, bias_all, bias_at, ctx_too):
                with act.Fori(j0, j0 + count) as j:
                    for u in range(2):
                        done_tile(j, u)
                        i = (j - j0) * 2 + u
                        bias = bias_all[:, bass.ds(i + bias_at, 1)]
                        act.wait_ge(raw_free, j * 2 + (u + 1 - 2 * FAG_IT))
                        main = nc.scalar.activation(rope_raw[:, u, :], bank[u][:, :], ACT.Identity, bias=bias, scale=scale)
                        main.then_inc(rope_raw_done, 1)
                        if ctx_too:
                            nc.scalar.activation(KT[:, bass.ds(i, 1), S:NT].rearrange("p o n -> p (o n)"), bank[2 + u][:, 0:C],
                                                 ACT.Identity, bias=bias).then_inc(ctx_keys_done, 1)
                            act.wait_ge(ctx_keys_done, i + 1)
                        act.wait_ge(rope_raw_done, j * 2 + (u + 1 - 2 * FAG_IT))
                        act.sem_inc(tile_bank_free, 1)
                        for q in range(4):
                            o = nc.scalar.copy(rope_swap[32 * q:32 * q + 32, u, :], rope_raw[32 * (q ^ 1):32 * (q ^ 1) + 32, u, :])
                        o.then_inc(raw_ready, 1)

            act.sem_inc(raw_free, 2)
            rope_source(FAG_IT, QK_IT, ATT_SCALE, qb8, 0, False)
            mod_row_out(3, 5, filled(5) + 8)

            for k in range(NCV):
                act.wait_ge(cmean_done, k + 1)
                nc.scalar.activation(sig[:, k, :], conv[:, k, :], ACT.Square).then_inc(csq_ready, 1)
            for k in range(NCV):
                act.wait_ge(cnorm_done, k + 1)
                nc.scalar.activation(conv[:, k, :], conv[:, k, :], ACT.Silu, bias=par("cln_b")[:, k:k + 1],
                                     scale=par("cln_g")[:, k:k + 1]).then_inc(csilu_done, 1)
            for m in range(NCV):
                act.wait_ge(pw_out, m + 1)
                nc.scalar.copy(mixT[:, NCV + m, :], bank[6 + m % 2][:, :]).then_inc(pw_evac, 1)
            mod_cols_out(3)

            rope_source(FAG_IT + QK_IT, QK_IT, 1.0, b_in, 20, True)

            mod_row_out(4, 5, filled(5) + 12)
            mod_row_out(5, 5, filled(5) + MOD_IT + 4)
            mod_cols_out(4)
            mod_cols_out(5)

            for s in range(ATT_STEPS + 6):
                if s < ATT_STEPS:
                    for m in range(2):
                        n = 2 * s + m
                        act.wait_ge(mx_done, n + 1)
                        if s >= 2:
                            act.wait_ge(at_out, 2 * (s - 1))
                        for i, (lo, w) in enumerate(((0, S), (S, C))):
                            e = nc.scalar.activation(E[:, s % 2, m, lo:lo + w], bank[2 * m + i][:, 0:w], ACT.Exp, bias=nmax[:, n, :],
                                                     accum_out=zpart[:, 2 * n + i, :])
                        e.then_inc(e_done, 1)
                if 1 <= s <= ATT_STEPS:
                    u = s - 1
                    h, qb = divmod(u, TS)
                    if h >= 2:
                        act.wait_ge(pv_out, h - 1)
                    act.wait_ge(at_out, 2 * u + 1)
                    nc.scalar.copy(AT[:, h % 2, 0:4, qb * P:(qb + 1) * P], bank[4][:, :].rearrange("p (k n) -> p k n", n=P)).then_inc(at_evac, 1)
                    act.wait_ge(at_out, 2 * u + 2)
                    nc.scalar.copy(AT[:, h % 2, 4:6, qb * P:(qb + 1) * P], bank[5][:, 0:C].rearrange("p (k n) -> p k n", n=P)).then_inc(at_evac, 1)
                h = head_at(s, 3)
                if h is not None:
                    act.wait_ge(o_copied, h + 1)
                    if h >= 1:
                        act.wait_ge(oss_out, h)
                    nc.scalar.activation(o_sq, mixT[:, 8 + h, :], ACT.Square).then_inc(o_squared, 1)
            act.wait_ge(mod_biased, 3)
            for m in range(KD):
                act.wait_ge(ring_used[m % 6], filled(m % 6) + MOD_IT + (2 if m % 6 < 4 else 4) + m // 6 + 2)
                if m >= 2:
                    act.wait_ge(zt_out, m - 1)
                nc.scalar.activation(zT[:, m % 2, :], bank[m % 2][:, :], ACT.Copy, scale=mods[:, 2 * KD + m, 0:1]).then_inc(zt_ready, 1)
            act.wait_ge(mod_biased, 6)
            for k in range(KD):
                act.wait_ge(h_out, k + 1)
                nc.scalar.activation(h2[:, k % 2, :], bank[k % 2][:, :], ACT.Identity, bias=mods[:, 3 * KD + k, 0:1],
                                     scale=mods[:, 4 * KD + k, 0:1]).then_inc(h_evac, 1)
            for n in range(2):
                act.wait_ge(gexp_need, n + 1)
                v = (gl, le)[n]
                nc.scalar.activation(v, v, ACT.Exp).then_inc(gexp_done, 1)

            act.wait_ge(table_ready, 1)
            n_blk = act.value_load(tab[0:1, 1:2], min_val=1, max_val=NB - 1)
            with act.Fori(0, n_blk) as g:
                act.wait_ge(w_used[3], g + 2)
                nc.scalar.copy(gu, bank[2][:, :]).then_inc(gu_ready, 1)
                act.wait_ge(gu_turned, g + 1)
                nc.scalar.activation(sil, bank[3][:, :].rearrange("p (k h n) -> p k h n", h=2, n=B)[:, :, 0, :], ACT.Silu).then_inc(silu_done, 1)
                act.wait_ge(w_used[7], g + 2)
                act.wait_ge(ye_free, g + 1)
                nc.scalar.copy(ye[:, 0:S], bank[4][:, :]).then_inc(ye_a, 1)
            for t in range(TS):
                act.wait_ge(y_in[t], 32)
                nc.scalar.activation(Y[:, t, 0, :], Y[:, t, 0, :], ACT.Copy, scale=wtok[:, t, 0:1]).then_inc(w0_done, 1)

        @block.vector
        def _(dve):
            v = nc.vector
            n_chain = [0]

            def after(ins):
                n_chain[0] += 1
                ins.then_inc(dve_chain, 1)
                dve.wait_ge(dve_chain, n_chain[0])

            after(v.memset(half, -0.5))
            for t in range(TS + TC):
                dve.wait_ge(x_in[t], 16)
                for q in range(4):
                    o = v.bn_stats(stats[:, t, q, :], xn[:, t, q * S:(q + 1) * S])
                after(o)
                after(v.bn_aggr(mv[:, t, :], stats[:, t, :, :].rearrange("p q n -> p (q n)")))
                v.tensor_scalar_add(rstd[:, t, :], mv[:, t, 1:2], EPS).then_inc(z_rstd_need, 1)
                dve.wait_ge(z_rstd_ready, t + 1)
                v.tensor_scalar(xn[:, t, :], xn[:, t, :], mv[:, t, 0:1], rstd[:, t, :], ALU.subtract, ALU.mult).then_inc(xn_ready, 1)
            dve.wait_ge(params_in, 16)
            v.tensor_tensor(lamt[0:DQ, 0:2], par("lam")[0:DQ, 0:2], par("lam")[0:DQ, 2:4], ALU.mult).then_inc(lam_prod, 1)
            v.tensor_scalar_mul(g08, par("subln"), 1.0 - LAM_INIT).then_inc(lam_prod, 1)

            dve.wait_ge(a_ready, 1)
            dve.wait_ge(sig_ready, 1)
            for k in range(NCV):
                after(v.tensor_tensor(glu[:, k, PAD:PAD + S], glu[:, k, PAD:PAD + S], sig[:, k, :], ALU.mult))
            cw = par("conv_w").rearrange("p (k t) -> p k t", t=CW)
            for tap in range(CW):
                for k in range(NCV):
                    if tap == 0:
                        o = v.tensor_scalar(conv[:, k, :], glu[:, k, 0:S], cw[:, k, 0:1], par("conv_b")[:, k:k + 1], ALU.mult, ALU.add)
                    else:
                        dve.wait_ge(conv_step, (tap - 1) * NCV + k + 1)
                        o = v.scalar_tensor_tensor(conv[:, k, :], glu[:, k, tap:tap + S], cw[:, k, tap:tap + 1], conv[:, k, :],
                                                   ALU.mult, ALU.add)
                    o.then_inc(conv_done if tap == CW - 1 else conv_step, 1)
            dve.wait_ge(cstat_out, 1)
            after(v.tensor_scalar_mul(cmean, bank[6][:, :], 1.0 / (NCV * P)))
            for k in range(NCV):
                v.tensor_tensor(conv[:, k, :], conv[:, k, :], cmean, ALU.subtract).then_inc(cmean_done, 1)
            dve.wait_ge(cstat_out, 2)
            v.tensor_scalar(crstd, bank[7][:, 0:TS], 1.0 / (NCV * P), EPS, ALU.mult, ALU.add).then_inc(cvar_done, 1)
            dve.wait_ge(cstat_out, 3)
            for k in range(NCV):
                v.tensor_tensor(conv[:, k, :], conv[:, k, :], bank[7][:, :], ALU.mult).then_inc(cnorm_done, 1)

            dve.wait_ge(bv_in, 16)
            dve.wait_ge(raw_free, 2 * HEADS + 2)
            for g in range(2):
                for t in range(TS + TC):
                    dve.wait_ge(v_tile_out, 6 * g + t + 1)
                    v.tensor_tensor(V[:, t, g * S:(g + 1) * S], bank[t % 2][:, :], bv_b[:, g * S:(g + 1) * S], ALU.add)\
                        .then_inc(tile_bank_free, 1)
            dve.wait_ge(lam_exp, 1)
            after(v.tensor_tensor(lamt[:, 4:5], lamt[:, 3:4], lamt[:, 2:3], ALU.subtract))
            after(v.tensor_scalar_add(lamt[:, 5:6], lamt[:, 4:5], -LAM_INIT))

            def head_copy(h):
                dve.wait_ge(pv_out, h + 1)
                v.tensor_copy(mixT[:, 8 + h, :], bank[6][:, :]).then_inc(o_copied, 1)

            for s in range(ATT_STEPS + 6):
                if s < ATT_STEPS:
                    for m in range(2):
                        n = 2 * s + m
                        dve.wait_ge(sc_out, n + 1)
                        v.reduce_max(zpart[:, 2 * n, :], bank[2 * m][:, :], axis=AX.X).then_inc(dve_max, 1)
                        v.reduce_max(zpart[:, 2 * n + 1, :], bank[2 * m + 1][:, 0:C], axis=AX.X).then_inc(dve_max, 1)
                        dve.wait_ge(dve_max, 2 * n + 2)
                        v.tensor_scalar(nmax[:, n, :], zpart[:, 2 * n, :], zpart[:, 2 * n + 1, :], -1.0, ALU.max, ALU.mult).then_inc(mx_done, 1)
                    dve.wait_ge(e_done, 2 * s + 2)
                    after(v.tensor_tensor(zsum[:, 2 * s:2 * s + 2, :], zpart[:, 4 * s:4 * s + 4:2, :], zpart[:, 4 * s + 1:4 * s + 4:2, :], ALU.add))
                    after(v.reciprocal(rz[:, 2 * s:2 * s + 2, :], zsum[:, 2 * s:2 * s + 2, :]))
                    after(v.tensor_scalar(E[:, s % 2, 1, :], E[:, s % 2, 1, :], rz[:, 2 * s + 1, :], lamt[:, 5:6], ALU.mult, ALU.mult))
                    v.scalar_tensor_tensor(E[:, s % 2, 0, :], E[:, s % 2, 0, :], rz[:, 2 * s, :], E[:, s % 2, 1, :],
                                           ALU.mult, ALU.add).then_inc(comb_done, 1)
                h = head_at(s, 2)
                if h is not None:
                    head_copy(h)
                h = head_at(s, 4)
                if h is not None:
                    dve.wait_ge(oss_out, h + 1)
                    if h >= 1:
                        dve.wait_ge(dve_chain, n_chain[0])
                    v.tensor_scalar(o_var, bank[7][:, 0:TS], 1.0 / P, EPS, ALU.mult, ALU.add).then_inc(ovar_done, 1)
                h = head_at(s, 5)
                if h is not None:
                    dve.wait_ge(orow_out, h + 1)
                    v.scalar_tensor_tensor(mixT[:, 8 + h, :], mixT[:, 8 + h, :], g08, bank[7][:, :], ALU.mult, ALU.mult).then_inc(att_done, 1)

            dve.wait_ge(xres_in, 16)
            for m in range(KD):
                dve.wait_ge(zt_out, m + 1)
                zz = Z[:, :, m * P:(m + 1) * P]
                v.scalar_tensor_tensor(zz, zz, ALPHA, bank[4 + m % 2][:, :].rearrange("p (t n) -> p t n", n=P), ALU.mult, ALU.add)\
                    .then_inc(z_added, 1)
                if m % 4 == 3:
                    dve.wait_ge(z_added, m + 1)
                    q = m // 4
                    for t in range(TS):
                        o = v.bn_stats(stats[:, t, q, :], Z[:, t, q * S:(q + 1) * S])
            after(o)
            dve.wait_ge(lna_in, 32)

            def norm(t, src, dst, n_root, need, ready):
                after(v.bn_aggr(mv[:, t, :], stats[:, t, :, :].rearrange("p q n -> p (q n)")))
                v.tensor_scalar_add(rstd[:, t, :], mv[:, t, 1:2], EPS).then_inc(need, 1)
                dve.wait_ge(ready, n_root)
                return v.tensor_scalar(dst, src, mv[:, t, 0:1], rstd[:, t, :], ALU.subtract, ALU.mult)

            def full_stats(t, src):
                for q in range(4):
                    o = v.bn_stats(stats[:, t, q, :], src[:, q * S:(q + 1) * S])
                after(o)

            for t in range(TS):
                after(norm(t, Z[:, t, :], Z[:, t, :], 6 + 2 * t + 1, z_rstd_need, z_rstd_ready))
                after(v.tensor_tensor(Z[:, t, :], Z[:, t, :], lna_b[:, 0, :], ALU.mult))
                after(v.tensor_tensor(X1[:, t, :], Z[:, t, :], lna_b[:, 1, :], ALU.add))
                full_stats(t, X1[:, t, :])
                norm(t, X1[:, t, :], XH[:, t, :], 6 + 2 * t + 2, z_rstd_need, z_rstd_ready).then_inc(xh_ready, 1)

            bc = lambda ap, *shape: ap.to_broadcast(list(shape))
            after(v.tensor_copy(vali, cst("val")))
            dve.wait_ge(logits_out, 1)
            br = par("b_r").rearrange("p (o n) -> p o n", o=1)
            after(v.tensor_tensor(lg, bank[2][:, 0:TS * (NG + NE)].rearrange("p (t n) -> p t n", t=TS), bc(br, P, TS, NG + NE), ALU.add))
            after(v.tensor_reduce(r1, lg[:, :, 0:NG], axis=AX.X, op=ALU.max))
            v.tensor_tensor(gl, lg[:, :, 0:NG], bc(r1, P, TS, NG), ALU.subtract).then_inc(gexp_need, 1)
            dve.wait_ge(gexp_done, 1)
            after(v.tensor_reduce(r2, gl, axis=AX.X, op=ALU.add))
            after(v.reciprocal(r3, r2))

            def first_max(dst, src, mx, n, tmp):
                first = cst("first")[:, EG - n:EG].rearrange("p (o n) -> p o n", o=1)
                after(v.tensor_tensor(tmp, src, bc(mx, P, TS, n), ALU.is_equal))
                after(v.tensor_tensor(tmp, tmp, bc(first, P, TS, n), ALU.mult))
                after(v.tensor_reduce(r2, tmp, axis=AX.X, op=ALU.max))
                after(v.tensor_tensor(dst, tmp, bc(r2, P, TS, n), ALU.is_equal))

            after(v.tensor_reduce(r1, gl, axis=AX.X, op=ALU.max))
            first_max(gs, gl, r1, NG, t8[:, :, 0:NG])
            after(v.tensor_tensor(le, lg[:, :, NG:NG + EG], bc(gs[:, :, 0:1], P, TS, EG), ALU.mult))
            for g in range(1, NG):
                after(v.tensor_tensor(t8, lg[:, :, NG + g * EG:NG + (g + 1) * EG], bc(gs[:, :, g:g + 1], P, TS, EG), ALU.mult))
                after(v.tensor_tensor(le, le, t8, ALU.add))
            after(v.tensor_reduce(r1, le, axis=AX.X, op=ALU.max))
            v.tensor_tensor(le, le, bc(r1, P, TS, EG), ALU.subtract).then_inc(gexp_need, 1)
            dve.wait_ge(gexp_done, 2)
            after(v.tensor_reduce(r1, le, axis=AX.X, op=ALU.max))
            first_max(oh[:, 0], le, r1, EG, t8)
            after(v.scalar_tensor_tensor(le, oh[:, 0], -2.0, le, ALU.mult, ALU.add))
            after(v.tensor_reduce(r1, le, axis=AX.X, op=ALU.max))
            first_max(oh[:, 1], le, r1, EG, t8)
            after(v.tensor_scalar_add(r2, r1, 1.0))
            after(v.reciprocal(r2, r2))
            after(v.tensor_tensor(wtok[:, :, 0:1], r2, r3, ALU.mult))
            after(v.tensor_tensor(wtok[:, :, 1:2], wtok[:, :, 0:1], r1, ALU.mult))
            for k in range(2):
                for g in range(NG):
                    o = v.tensor_tensor(O[:, k, :, g * EG:(g + 1) * EG], oh[:, k], bc(gs[:, :, g:g + 1], P, TS, EG), ALU.mult)
            after(o)
            v.tensor_tensor(Osum, O[:, 0], O[:, 1], ALU.add).then_inc(o_ready, 1)
            dve.wait_ge(rank_out, 1)
            after(v.tensor_copy(cnti, bank[3][:, TS * NE:(TS + 1) * NE]))
            after(v.tensor_single_scalar(cnti, cnti, B - 1, ALU.add))
            after(v.tensor_single_scalar(cnti, cnti, 6, ALU.logical_shift_right))
            after(v.tensor_copy(nblk, cnti))
            after(v.tensor_tensor_scan(cum, bc(ones[:, 0:1], P, NE), nblk, 0.0, ALU.mult, ALU.add))
            after(v.tensor_single_scalar(act_e, nblk, 0.0, ALU.is_gt))
            after(v.tensor_tensor_scan(ordn, bc(ones[:, 0:1], P, NE), act_e, 0.0, ALU.mult, ALU.add))
            after(v.tensor_tensor(cnt, cum, nblk, ALU.subtract))
            after(v.tensor_scalar_mul(pst, cnt, float(B)))
            after(v.tensor_tensor(prk, bank[3][:, 0:TS * NE].rearrange("p (t n) -> p t n", t=TS),
                                  bc(pst.rearrange("p (o n) -> p o n", o=1), P, TS, NE), ALU.add))
            for k in range(2):
                after(v.tensor_tensor(t32, O[:, k], prk, ALU.mult))
                after(v.tensor_reduce(slot[:, k, :], t32, axis=AX.X, op=ALU.add))
            after(v.tensor_copy(sloti, slot.rearrange("p k t -> p (k t)")))
            after(v.tensor_single_scalar(addri, sloti, 6, ALU.logical_shift_right))
            after(v.tensor_copy(colf, addri))
            after(v.tensor_single_scalar(sloti, sloti, B - 1, ALU.bitwise_and))
            after(v.tensor_copy(addr.rearrange("p k t -> p (k t)"), sloti))
            after(v.scalar_tensor_tensor(addr.rearrange("p k t -> p (k t)"), addr.rearrange("p k t -> p (k t)"), float(NB), colf, ALU.mult, ALU.add))
            v.tensor_copy(addri, addr.rearrange("p k t -> p (k t)")).then_inc(addr_ready, 1)
            after(v.tensor_scalar_add(ordn, ordn, -1.0))
            row = lambda ap: ap[0:1].rearrange("p (o n) -> p o n", o=1)
            col = lambda ap, n: ap[0:1].rearrange("p (n o) -> p n o", o=1)[:, 0:n, :]
            io = cst("iota")
            eq = big[0:1, 0:NE, :]
            after(v.tensor_tensor(eq, row(ordn).to_broadcast([1, NE, NE]), col(io, NE).to_broadcast([1, NE, NE]), ALU.is_equal))
            after(v.tensor_tensor(eq, eq, row(act_e).to_broadcast([1, NE, NE]), ALU.mult))
            after(v.tensor_tensor(bigb, eq, row(io[:, 0:NE]).to_broadcast([1, NE, NE]), ALU.mult))
            after(v.tensor_reduce(elist[0:1], bigb, axis=AX.X, op=ALU.add))
            after(v.tensor_tensor(bigb, eq, row(cnt).to_broadcast([1, NE, NE]), ALU.mult))
            after(v.tensor_reduce(clist[0:1], bigb, axis=AX.X, op=ALU.add))
            after(v.tensor_tensor(big[0:1], row(cum).to_broadcast([1, NB, NE]), col(io, NB).to_broadcast([1, NB, NE]), ALU.is_le))
            after(v.tensor_tensor(big[0:1], big[0:1], row(act_e).to_broadcast([1, NB, NE]), ALU.mult))
            after(v.tensor_reduce(jlist[0:1], big[0:1], axis=AX.X, op=ALU.add))
            v.tensor_scalar_add(tab[0:1, 0:1], ordn[0:1, NE - 1:NE], 1.0)
            v.tensor_copy(tab[0:1, 1:2], cum[0:1, NE - 1:NE])
            v.tensor_copy(tab[0:1, OFF_E:OFF_E + NE], elist[0:1])
            v.tensor_copy(tab[0:1, OFF_C:OFF_C + NE], clist[0:1])
            after(v.tensor_copy(tab[0:1, OFF_J:OFF_J + NB], jlist[0:1]))
            dve.sem_inc(table_ready, 1)
            dve.wait_ge(slots_in, 32)
            after(v.tensor_single_scalar(gidx_i, slots_i, 1, ALU.logical_shift_right))
            after(v.tensor_single_scalar(gidx_i, gidx_i, 1, ALU.logical_shift_left))
            after(v.tensor_single_scalar(gidx_i[B:P], gidx_i[B:P], 1, ALU.add))
            v.tensor_single_scalar(slots_i[B:P], slots_i[B:P], 2 * S, ALU.add).then_inc(gidx_ready, 1)

            n_blk = dve.value_load(tab[0:1, 1:2], min_val=1, max_val=NB - 1)
            halves = lambda ap: ap.rearrange("p (h k) o -> p h k o", h=2)
            sc4 = mods[:, 4 * KD:5 * KD, 0:1]
            sh3 = mods[:, 3 * KD:4 * KD, 0:1]

            def modulate(n):
                dve.wait_ge(xg_turned, n + 1)
                for b in range(2):
                    src = bank[b][:, :].rearrange("p (k h n) -> p h k n", h=2, n=B)
                    dst = xgT.rearrange("p (h k) n -> p h k n", h=2)[:, :, 4 * b:4 * b + 4, :]
                    sc = halves(sc4)[:, :, 4 * b:4 * b + 4, :].to_broadcast([P, 2, 4, B])
                    v.tensor_tensor(dst, src, sc, ALU.mult).then_inc(xg_scaled, 1)
                dve.wait_ge(xg_scaled, n * 2 + 2)
                v.tensor_tensor(xgT, xgT, bc(sh3, P, KD, B), ALU.add).then_inc(xgT_ready, 1)

            modulate(0)
            with dve.Fori(0, n_blk) as g:
                dve.wait_ge(silu_done, g + 1)
                v.tensor_tensor(actT, bank[3][:, :].rearrange("p (k h n) -> p k h n", h=2, n=B)[:, :, 1, :], sil, ALU.mult).then_inc(act_ready, 1)
                modulate(g + 1)
                dve.wait_ge(w_used[7], g + 2)
                dve.wait_ge(ye_free, g + 1)
                v.tensor_copy(ye[:, S:2 * S], bank[5][:, :]).then_inc(ye_b, 1)

            dve.wait_ge(g5_out, 1)
            for q in range(4):
                o = v.tensor_copy(g5[:, q * S:(q + 1) * S], bank[q][:, :])
            after(o)
            for t in range(TS):
                y0, y1 = Y[:, t, 0, :], Y[:, t, 1, :]
                dve.wait_ge(w0_done, t + 1)
                after(v.scalar_tensor_tensor(y0, y1, wtok[:, t, 1:2], y0, ALU.mult, ALU.add))
                after(v.tensor_tensor(y0, y0, g5, ALU.mult))
                after(v.scalar_tensor_tensor(y0, X1[:, t, :], ALPHA, y0, ALU.mult, ALU.add))
                full_stats(t, y0)
                after(norm(t, y0, y0, t + 1, fin_need, fin_rstd))
                if t == 0:
                    dve.wait_ge(lnf_in, 32)
                after(v.tensor_tensor(y0, y0, lnf_b[:, 0, :], ALU.mult))
                v.tensor_tensor(X1[:, t, :], y0, lnf_b[:, 1, :], ALU.add).then_inc(fin_ready, 1)

        @block.gpsimd
        def _(pool):
            gp = nc.gpsimd
            gp.memset(fill_i[0:B, :], EMPTY).then_inc(fill_ready, 1)
            pool.wait_ge(fill_ready, 1)
            pool.dma_start(slot_dram.rearrange("(p n) o -> p (n o)", n=NB), fill_i[0:B, :]).then_inc(fill_done, 16)
            gp.memset(glu, 0.0).then_inc(glu_zero, 1)

            def root(ap, need, n, ready):
                pool.wait_ge(need, n)
                gp.tensor_tensor(ap, ap, half[:, 0:1].to_broadcast([P, ap.shape[1]]), ALU.pow).then_inc(ready, 1)

            def mod_bias(i):
                m_i = mods[:, i * KD:(i + 1) * KD, :]
                pool.wait_ge(mod_col_ready, i + 1)
                b = par("b_mod")[:, i * KD:(i + 1) * KD].rearrange("p (k o) -> p k o", o=1).to_broadcast([P, KD, 2])
                if i in (1, 4):
                    gp.tensor_tensor(m_i, m_i, b, ALU.add).then_inc(mod_one, 1)
                    pool.wait_ge(mod_one, 1 if i == 1 else 2)
                    gp.tensor_scalar_add(m_i, m_i, 1.0).then_inc(mod_biased, 1)
                else:
                    gp.tensor_tensor(m_i, m_i, b, ALU.add).then_inc(mod_biased, 1)

            for t in range(TS + TC):
                root(rstd[:, t, :], z_rstd_need, t + 1, z_rstd_ready)
            mod_bias(0)
            mod_bias(1)
            pool.wait_ge(xt_out, 2 * KD)
            pool.wait_ge(fill_done, 16)
            pool.dma_start(dft_s.rearrange("p t r n -> p (t r n)"), dfts).then_inc(dft_in, 16)
            pool.dma_start(wf, w_fourier.rearrange("(k p) n -> p k n", p=P)).then_inc(wf_in, 16)
            pool.wait_ge(f_out, 8 + NF)
            pool.dma_start(wpw, w_pw.rearrange("(k p) n -> p k n", p=P)).then_inc(wpw_in, 16)

            def rotate(i0, dst):
                with pool.Fori(0, QK_IT) as i:
                    for u in range(2):
                        pool.wait_ge(raw_ready, i * 2 + (i0 + u + 1))
                        o = dst[:, bass.ds(i * 2 + u, 1), 0:S].rearrange("p o n -> p (o n)")
                        gp.tensor_tensor(rope_raw[:, u, :], rope_raw[:, u, :], cst("cos"), ALU.mult).then_inc(rot, 1)
                        gp.tensor_tensor(rope_swap[:, u, :], rope_swap[:, u, :], cst("sin"), ALU.mult).then_inc(rot, 1)
                        pool.wait_ge(rot, i * 4 + (2 * i0 + 2 * u + 2))
                        gp.tensor_tensor(o, rope_raw[:, u, :], rope_swap[:, u, :], ALU.add).then_inc(raw_free, 1)

            mod_bias(2)
            rotate(0, QT)
            root(crstd, cvar_done, 1, crstd_ready)
            pool.wait_ge(pw_out, NCV)
            pool.dma_start(bv_b, b_v.to_broadcast([P, HEADS * P])).then_inc(bv_in, 16)
            rotate(HEADS, KT)
            for i in range(3, 6):
                mod_bias(i)
            for h in range(HEADS):
                root(o_var, ovar_done, h + 1, orstd_ready)
            for n in range(2 * TS):
                root(rstd[:, n // 2, :], z_rstd_need, 6 + n + 1, z_rstd_ready)

            pool.wait_ge(addr_ready, 1)
            for k in range(2):
                for t in range(TS):
                    c = k * TS + t
                    pool.indirect_dma_start(slot_dram, bass.IndirectOffsetOnAxis(ap=addri[:, c:c + 1], axis=0),
                                            vali[:, c:c + 1], None).then_inc(slots_scattered, 16)
            pool.wait_ge(gidx_ready, 1)
            pool.wait_ge(rows_out, 16 * TS)
            gp.memset(xg, 0.0).then_inc(idx_ready, 1)
            gp.tensor_copy(igat, gidx_i[:, 0:1]).then_inc(idx_ready, 1)
            pool.wait_ge(idx_ready, 2)

            def gather():
                pool.indirect_dma_start(xg, None, row_dram, bass.IndirectOffsetOnAxis(ap=igat, axis=0),
                                        bounds_check=2 * S - 1, oob_is_err=False).then_inc(gathered, 16)

            gather()
            pool.sem_inc(ye_free, 1)
            n_blk = pool.value_load(tab[0:1, 1:2], min_val=1, max_val=NB - 1)
            with pool.Fori(0, n_blk) as g:
                pool.wait_ge(xg_turned, g + 1)
                pool.wait_ge(gathered, g * 16 + 16)
                gp.tensor_copy(igat, gidx_i[:, bass.ds(g + 1, 1)]).then_inc(idx_ready, 1)
                pool.wait_ge(idx_ready, g + 3)
                pool.sem_inc(pool_step, 1)
                gather()
                gp.tensor_copy(isca, slots_i[:, bass.ds(g, 1)]).then_inc(isca_ready, 1)
                pool.wait_ge(isca_ready, g + 1)
                pool.wait_ge(ye_a, g + 1)
                pool.wait_ge(ye_b, g + 1)
                pool.sem_inc(pool_step, 1)
                pool.indirect_dma_start(y_dram, bass.IndirectOffsetOnAxis(ap=isca, axis=0), ye, None,
                                        bounds_check=4 * S - 1, oob_is_err=False).then_inc(scattered, 16)
                pool.wait_ge(scattered, g * 16 + 16)
                pool.sem_inc(ye_free, 1)
            pool.wait_ge(gathered, n_blk * 16 + 16)
            pool.wait_ge(scattered, n_blk * 16)
            for t in range(TS):
                root(rstd[:, t, :], fin_need, t + 1, fin_rstd)


def kernel(**inputs):
    import numpy as np
    import concourse.bacc as bacc
    from concourse.bass_utils import run_bass_kernel_spmd

    f = {k: np.asarray(v) for k, v in inputs.items()}
    consts = np.zeros((P, N_CONST), np.float32)

    def put(name, v):
        lo, hi = CONST[name]
        consts[:, lo:hi] = v

    put("ident", np.eye(P))
    put("ones", 1.0)
    put("upper", np.triu(np.ones((P, P)), 1))
    t = np.arange(S)
    inv = (1.0 / (10000.0 ** (np.arange(16, dtype=np.float32) / np.float32(16)))).astype(np.float32)
    ang = np.concatenate([(t // 64).astype(np.float32)[:, None] * inv, (t % 64).astype(np.float32)[:, None] * inv], -1)
    cos, sin = np.cos(ang).T, np.sin(ang).T
    put("cos", np.concatenate([cos] * 4, 0))
    put("sin", np.concatenate([-sin, sin] * 2, 0))
    th = 2 * np.pi * (np.outer(np.arange(P), np.arange(P)) % P) / P
    put("dftc", np.concatenate([np.cos(th), np.sin(th)], 1) / np.sqrt(P))
    put("iota", np.arange(NB))
    put("first", np.arange(EG, 0, -1))
    put("val", 2 * (np.arange(TS)[None, None, :] * P + np.arange(P)[:, None, None]).repeat(2, 1).reshape(P, 2 * TS)
        + np.repeat(np.arange(2), TS)[None, :])
    ph = 2 * np.pi * (np.outer(t, t) % S) / S
    dfts = (np.stack([np.cos(ph), -np.sin(ph)], 1) / np.sqrt(S)).reshape(TS, P, 2, S).transpose(1, 0, 2, 3)
    dfts = np.ascontiguousarray(dfts.reshape(P, -1), dtype=np.float32)

    params = np.zeros((P, N_PARAM), np.float32)

    def lay(name, v):
        lo, hi = PARAM[name]
        params[:v.shape[0], lo:hi] = v

    cols = lambda v: v.reshape(-1, P).T
    lay("c", np.tile(np.stack([f["c"][0].reshape(KD, P).T, f["c_ctx"].reshape(KD, P).T], 2), (1, 1, CB // 2)).reshape(P, KD * CB))
    lay("b_in", cols(f["b_in"][0, :28 * P]))
    lay("b_mod", cols(f["b_mod"][0]))
    lay("conv_w", f["conv_w"][0].reshape(CW, NCV, P).transpose(2, 1, 0).reshape(P, NCV * CW))
    lay("conv_b", cols(f["conv_b"][0]))
    lay("cln_g", cols(f["conv_ln_g"][0]))
    lay("cln_b", cols(f["conv_ln_b"][0]))
    lay("subln", cols(f["subln_g"][0]))
    lay("lam", np.stack([f["lam_q1"][0], f["lam_q2"][0], f["lam_k1"][0], f["lam_k2"][0]], 1))
    lay("b_r", np.broadcast_to(np.concatenate([f["b_rg"][0], f["b_re"][0]])[None, :], (P, NG + NE)))
    tiled = lambda w: np.ascontiguousarray(w.reshape(KD, P, -1, P).transpose(2, 1, 0, 3).reshape(-1, P, KD * P))
    arrays = {
        "consts": consts, "dfts": dfts, "params": params, "x": f["x"][0], "ctx_in": f["ctx"][0],
        "w_mod": f["w_mod"][0].reshape(KD, P, 6, D).transpose(2, 0, 1, 3).reshape(N_MODT, P, D), "w_in": tiled(f["w_in"][0]), "b_v": f["b_in"][:, 28 * P:],
        "w_fourier": f["w_fourier"][0], "w_pw": f["w_pw"][0], "w_out": tiled(f["w_out"][0]),
        "ln_a": np.concatenate([f["ln_a_g"], f["ln_a_b"]], 0), "ln_f": np.concatenate([f["ln_f_g"], f["ln_f_b"]], 0),
        "w_r": np.concatenate([f["w_rg"][0], f["w_re"][0]], 1).reshape(KD, P, NG + NE).transpose(1, 0, 2).reshape(P, -1),
        "w_gate": f["w_gate"][0], "w_up": f["w_up"][0], "w_down": f["w_down"][0],
    }
    arrays = {k: np.ascontiguousarray(v) for k, v in arrays.items()}
    nc = bacc.Bacc("TRN2", target_bir_lowering=False, num_devices=1)
    args = {k: nc.dram_tensor(f"in_{k}", v.shape, mybir.dt.from_np(v.dtype), kind="ExternalInput").ap() for k, v in arrays.items()}
    res = nc.dram_tensor("out_rows", (S, D), F32, kind="ExternalOutput").ap()
    build(nc, out=res, **args)
    r = run_bass_kernel_spmd(nc, [{f"in_{k}": v for k, v in arrays.items()}], core_ids=[0])
    return r.results[0]["out_rows"].reshape(1, S, D)
```

```python
import math
from contextlib import ExitStack

import concourse.bass as bass
from concourse import mybir

F32, I32, F32R = mybir.dt.float32, mybir.dt.int32, mybir.dt.float32r
ALU = mybir.AluOpType
ACT = mybir.ActivationFunctionType
AX = mybir.AxisListType

P = 128
D = 2048
KD = D // P
S = 512
C = 256
TS, TC = S // P, C // P
NT = S + C
HEADS, DQ = 8, 64
NF, NCV = 4, 4
CW = 31
PAD = CW // 2
UW = S + 2 * PAD
N_IN = 36
N_MODT = 96
N_MOD01 = 2 * KD
NE, NG, EG = 32, 4, 8
DE = 512
KE = DE // P
B = 64
NB = 50
EPS = 1e-6
ALPHA = 2.0 ** 0.25
LAM_INIT = 0.8 - 0.6 * math.exp(0.0)
ATT_SCALE = 1.0 / math.sqrt(DQ)
EMPTY = 8192
CB = 32

CONST = {}
_at = 0
for _n, _w in (("ident", P), ("ones", P), ("upper", P), ("iota", NB), ("iota_p", 1), ("first", EG), ("val", 2 * TS),
               ("cos", S), ("sin", S), ("dftc", 2 * P)):
    CONST[_n] = (_at, _at + _w)
    _at += _w
N_CONST = _at
PARAM = {}
_at = 0
for _n, _w in (("c", KD * CB), ("conv_w", NCV * CW), ("conv_b", NCV), ("cln_g", NCV), ("cln_b", NCV),
               ("b_in", 28), ("b_mod", N_MODT), ("subln", 1), ("lam", 4), ("b_r", NG + NE)):
    PARAM[_n] = (_at, _at + _w)
    _at += _w
N_PARAM = _at


def build(nc, consts, dfts, params, x, ctx_in, w_mod, w_in, b_v, w_fourier, w_pw, w_out, ln_a, ln_f,
          w_r, w_gate, w_up, w_down, out):
    stack = ExitStack()
    with stack:
        def rounded(name, kb, *shape):
            with nc.sbuf_tensor(f"below_{name}", [P, int(kb * 256)], F32), \
                    nc.sbuf_tensor(name, [P, math.prod(shape)], F32R) as r:
                return r[:, :].rearrange("p (a b) -> p a b", b=shape[-1])

        mix_hi_r = [rounded(f"mix_high{i}", 120 + 8 * i, 4, S) for i in range(4)]
        mix_lo_r = [rounded(f"mix_low{i}", 160 + 8 * i, 4, S) for i in range(4)]
        w_hi_r = [rounded(f"w_high{i}", kb, KD, P) for i, kb in enumerate((152, 104, 112))]
        w_lo_r = [rounded(f"w_low{i}", 48 + 8 * i, KD, P) for i in range(6)]
        arena = stack.enter_context(nc.sbuf_tensor("arena", [P, 207 * 256], F32))

        def at(kb, *shape):
            lo = int(kb * 256)
            n = math.prod(shape)
            v = arena[:, lo:lo + n]
            if len(shape) == 2:
                v = v.rearrange("p (a b) -> p a b", b=shape[1])
            if len(shape) == 3:
                v = v.rearrange("p (a b c) -> p a b c", b=shape[1], c=shape[2])
            return v

        sem = lambda name: stack.enter_context(nc.semaphore(name))
        bank = [stack.enter_context(nc.psum_tensor(f"bank{i}", [P, 512], F32)) for i in range(8)]
        row_dram = nc.dram_tensor("normed_rows", (2 * S, D // 2), F32, kind="Internal").ap()
        slot_dram = nc.dram_tensor("slot_table", (B * NB, 1), I32, kind="Internal").ap()
        y_dram = nc.dram_tensor("expert_rows", (4 * S, D // 2), F32, kind="Internal").ap()

        K_ = at(193, N_CONST)
        cst = lambda n: K_[:, CONST[n][0]:CONST[n][1]]
        P_ = at(193 + N_CONST / 256, N_PARAM)
        par = lambda n: P_[:, PARAM[n][0]:PARAM[n][1]]
        base = 193 + (N_CONST + N_PARAM) / 256
        mods = at(base, N_MODT, 2)
        base += N_MODT * 2 / 256
        wr = at(base, KD, NG + NE)
        base += KD * (NG + NE) / 256
        cond = par("c").rearrange("p (k n) -> p k n", n=CB)
        stats = at(base, 6, 4, 6)
        base += 144 / 256
        mv = at(base, 6, 2)
        rstd = at(base + 12 / 256, 6, 1)
        mv2 = at(base + 51 / 256, TS, 2)
        rstd2 = at(base + 59 / 256, TS, 1)
        nmean = at(base + 63 / 256, TS, 1)
        half = at(base + 18 / 256, 8)
        qb8 = at(base + 26 / 256, 8)
        lamt = at(base + 34 / 256, 8)
        g08 = at(base + 42 / 256, 1)
        wtok = at(base + 43 / 256, TS, 2)
        assert base + 67 / 256 <= 207
        ident, ones, upper = cst("ident"), cst("ones"), cst("upper")

        fill_i = at(144, NB).bitcast(I32)
        hT = at(0, KD, NT)
        ring = at(48, 6, KD, P)
        ring_row = at(48, 6, D)
        xn = at(96, 6, D)
        uT = at(96, NF, S)
        ab = at(104, TS, NF, 2 * P)
        dft_s = at(120, TS, 2, S)
        yT = at(136, NF, S)
        wf = at(144, NF, S)
        wpw = at(104, NCV, S)
        cmean, crstd = at(96, S), at(98, TS)
        rope_raw, rope_swap = at(112, 2, S), at(116, 2, S)
        V = at(96, TS + TC, HEADS * P)
        KT = at(120, HEADS, NT)
        QT = at(144, HEADS, S)
        mixT = at(160, KD, S)
        sig = at(168, NCV, S)
        glu = at(176, NCV, UW)
        conv = at(176 + NCV * UW / 256, NCV, S)
        bv_b = at(176, HEADS * P)
        mod_row = [at(kb, S) for kb in (158, 156, 158, 102, 182, 184)]
        AT = at(0, 2, 6, S)
        E = at(24, 3, 2, NT)
        o_sq, o_var = at(42, S), at(44, TS)
        nmax, zsum, rz = at(45, 64, 1), at(45.25, 64, 1), at(45.5, 64, 1)
        zpart = at(44.25, 128, 1)
        Z = at(0, TS, D)
        lna_b = at(32, 2, D)
        zT = at(96, 2, S)
        XH = at(100, TS, D)
        h2 = at(48, 4, S)
        rt = 136
        lg = at(rt, TS, NG + NE)
        lgb = at(rt + 0.625, NG + NE)
        gl = at(rt + 1, TS, NG)
        gs = at(rt + 1.25, TS, NG)
        r1 = at(rt + 1.5, TS, 1)
        r2 = at(rt + 1.75, TS, 1)
        r3 = at(rt + 2, TS, 1)
        le = at(rt + 2.25, TS, EG)
        t8 = at(rt + 2.5, TS, EG)
        oh = at(rt + 3, 2, TS, EG)
        O = at(rt + 4, 2, TS, NE)
        Osum = at(rt + 5, TS, NE)
        nblk = at(rt + 6.25, NE)
        cum = at(rt + 6.5, NE)
        act_e = at(rt + 6.75, NE)
        ordn = at(rt + 7, NE)
        pst = at(rt + 7.25, NE)
        prk = at(rt + 7.5, TS, NE)
        t32 = at(rt + 8, TS, NE)
        slot = at(rt + 8.5, 2, TS)
        addr = at(rt + 8.75, 2, TS)
        vali = at(rt + 9, 2 * TS).bitcast(I32)
        addri = at(rt + 9.25, 2 * TS).bitcast(I32)
        sloti = at(rt + 9.5, 2 * TS).bitcast(I32)
        colf = at(rt + 9.75, 2 * TS)
        place = at(rt + 10, NE)
        tcol = at(rt + 10.25, 3)
        cnti = at(rt + 10.5, NE).bitcast(I32)
        X1 = at(160, TS, D)
        OFF_E = 2
        OFF_C = OFF_E + NE
        OFF_J = OFF_C + NE + 1
        tab = at(192, OFF_J + NB).bitcast(I32)
        slots_i = at(192.72, NB).bitcast(I32)
        igat = at(192.93, 1).bitcast(I32)
        isca = at(192.94, 1).bitcast(I32)
        gidx_i = wr.rearrange("p k n -> p (k n)")[:, 0:NB].bitcast(I32)
        H2 = D // 2
        WGU = at(0, 4, 2, 4 * DE)
        WD = at(64, KE, D)
        WD_in = at(112, KE, D)
        xg_in = at(96, H2)
        xg = at(100, H2)
        xgT = at(104, KD, B)
        gu = at(108, DE)
        sil = at(110, KE, B)
        actT = at(111, KE, B)
        g5b = at(156, H2)
        used = 193 + CONST["cos"][0] / 256
        assert N_CONST - CONST["cos"][0] + PARAM["b_mod"][1] >= 2 * H2
        ye, ye_out = at(used, H2), at(used + 4, H2)
        Y = at(0, TS, 2, D)
        lnf_b = at(112, 2, D)

        consts_in = sem("consts_in")
        params_in = sem("params_in")
        token_rows_in = [sem(f"token_rows_in{t}") for t in range(6)]
        ring_full = [sem(f"ring_full{s}") for s in range(6)]
        ring_used = [sem(f"ring_used{s}") for s in range(6)]
        mod_row_ready = sem("mod_row_ready")
        mod_turned = sem("mod_turned")
        mod_col_ready = sem("mod_col_ready")
        mod_biased = sem("mod_biased")
        tile_bank_free = sem("tile_bank_free")
        silu_ready = sem("silu_ready")
        xn_ready = sem("xn_ready")
        xt_out = sem("xt_out")
        xt_evac = sem("xt_evac")
        lat_modulated = sem("lat_modulated")
        ctx_modulated = sem("ctx_modulated")
        dft_in = sem("dft_in")
        wf_in = sem("wf_in")
        wpw_in = sem("wpw_in")
        bv_in = sem("bv_in")
        f_out = sem("f_out")
        f_evac = sem("f_evac")
        glu_zero = sem("glu_zero")
        a_ready = sem("a_ready")
        sig_ready = sem("sig_ready")
        conv_done = sem("conv_done")
        cstat_out = sem("cstat_out")
        cmean_done = sem("cmean_done")
        csq_ready = sem("csq_ready")
        cvar_done = sem("cvar_done")
        crstd_ready = sem("crstd_ready")
        cnorm_done = sem("cnorm_done")
        csilu_done = sem("csilu_done")
        pw_out = sem("pw_out")
        pw_evac = sem("pw_evac")
        raw_ready = sem("raw_ready")
        raw_free = sem("raw_free")
        dve_chain = sem("dve_chain")
        rope_raw_done = sem("rope_raw_done")
        ctx_keys_done = sem("ctx_keys_done")
        rot = sem("rot")
        mod_one = sem("mod_one")
        conv_step = sem("conv_step")
        dve_max = sem("dve_max")
        ye_free = sem("ye_free")
        pool_step = sem("pool_step")
        sp_step = sem("sp_step")
        act_step = sem("act_step")
        v_tile_out = sem("v_tile_out")
        lam_out = sem("lam_out")
        lam_exp = sem("lam_exp")
        lam_prod = sem("lam_prod")
        sc_out = sem("sc_out")
        mx_done = sem("mx_done")
        e_done = sem("e_done")
        comb_done = sem("comb_done")
        at_out = sem("at_out")
        at_evac = sem("at_evac")
        pv_out = sem("pv_out")
        o_copied = sem("o_copied")
        o_squared = sem("o_squared")
        oss_out = sem("oss_out")
        ovar_done = sem("ovar_done")
        orow_out = sem("orow_out")
        orstd_ready = sem("orstd_ready")
        att_done = sem("att_done")
        zt_ready = sem("zt_ready")
        zt_out = sem("zt_out")
        z_added = sem("z_added")
        xres_in = sem("xres_in")
        mix_hi_ready = sem("mix_hi_ready")
        mix_split = sem("mix_split")
        w_hi_ready = sem("w_hi_ready")
        w_split = sem("w_split")
        lna_in = sem("lna_in")
        z_rstd_need = sem("z_rstd_need")
        x_rstd_need = sem("x_rstd_need")
        x_stat = sem("x_stat")
        x_rstd_ready = sem("x_rstd_ready")
        shift_out = sem("shift_out")
        shift_copied = sem("shift_copied")
        wr_scaled = sem("wr_scaled")
        lgb_ready = sem("lgb_ready")
        z_rstd_ready = sem("z_rstd_ready")
        xh_ready = sem("xh_ready")
        rows_out = sem("rows_out")
        h_out = sem("h_out")
        h_evac = sem("h_evac")
        logits_out = sem("logits_out")
        gexp_need = sem("gexp_need")
        gexp_done = sem("gexp_done")
        o_ready = sem("o_ready")
        total_out = sem("total_out")
        rank_out = sem("rank_out")
        fill_ready = sem("fill_ready")
        addr_ready = sem("addr_ready")
        slots_scattered = sem("slots_scattered")
        slots_in = sem("slots_in")
        table_ready = sem("table_ready")
        tcol_ready = sem("tcol_ready")
        tcol_turned = sem("tcol_turned")
        xg_ready = sem("xg_ready")
        gidx_ready = sem("gidx_ready")
        w_full = [sem(f"w_full{c}") for c in range(8)]
        wd_moved = sem("wd_moved")
        w_used = [sem(f"w_used{c}") for c in range(8)]
        idx_ready = sem("idx_ready")
        gathered = sem("gathered")
        xg_turned = sem("xg_turned")
        xg_scaled = sem("xg_scaled")
        xgT_ready = sem("xgT_ready")
        gu_ready = sem("gu_ready")
        gu_turned = sem("gu_turned")
        silu_done = sem("silu_done")
        act_ready = sem("act_ready")
        ye_ready = sem("ye_ready")
        isca_ready = sem("isca_ready")
        scattered = sem("scattered")
        lnf_in = sem("lnf_in")
        g5_out = sem("g5_out")
        g5_ready = sem("g5_ready")
        w0_done = sem("w0_done")
        x1_scaled = sem("x1_scaled")
        res_done = sem("res_done")
        fin_need = sem("fin_need")
        fin_rstd = sem("fin_rstd")
        fin_ready = sem("fin_ready")
        out_done = sem("out_done")

        FAG_IT, QK_IT = 6, 4
        MOD_IT = FAG_IT + 2 * QK_IT
        filled = lambda s: (N_MOD01 - s + 5) // 6
        ATT_STEPS = HEADS * TS
        TURN_FROM = 14
        head_at = lambda s, lag: (s - lag) // 4 if s >= lag and (s - lag) % 4 == 3 and (s - lag) // 4 < HEADS else None

        V_SLOTS = ((0, 1, 2, 3), (4, 5, 0, 1))
        split_at = {ATT_STEPS - 4 + k: (k,) for k in range(8)}
        split_at.update({ATT_STEPS + 4: (8, 9), ATT_STEPS + 5: (10, 11), ATT_STEPS + 6: (12, 13), ATT_STEPS + 7: (14,)})
        wo_fills = [filled(s) + MOD_IT + (2, 2, 1, 1, 5, 5)[s] for s in range(6)]

        block = stack.enter_context(nc.Block())

        @block.sync
        def _(sp):
            sp.dma_start(P_, params).then_inc(params_in, 16)
            sp.dma_start(K_, consts).then_inc(consts_in, 16)
            for t in range(TS):
                sp.dma_start(xn[:, t, :], x[t * P:(t + 1) * P, :]).then_inc(token_rows_in[t], 16)
            for t in range(TC):
                sp.dma_start(xn[:, TS + t, :], ctx_in[t * P:(t + 1) * P, :]).then_inc(token_rows_in[TS + t], 16)

            for s in range(6):
                sp.sem_inc(ring_used[s], 1)
            for c in range(8):
                sp.sem_inc(w_used[c], 1)

            def load(s, src, n):
                sp.wait_ge(ring_used[s], n)
                sp.dma_start(ring[:, s, :, :], src).then_inc(ring_full[s], 16)

            for n in range(N_MOD01):
                load(n % 6, w_mod[n], n // 6 + 1)
            with sp.Fori(0, MOD_IT) as j:
                for s in range(6):
                    if s % 3 == 0:
                        src = w_in[bass.ds(j * 2 + s // 3, 1), :, :]
                    else:
                        src = w_mod[bass.ds(j * 4 + (N_MOD01 + s - 1 - s // 3), 1), :, :]
                    load(s, src.rearrange("o p n -> p (o n)"), j + (filled(s) + 1))
            for s in range(4):
                load(s, w_in[28 + s], filled(s) + MOD_IT + 1)
            for q in range(8):
                s = 4 + q % 2
                load(s, w_mod[N_MOD01 + 4 * MOD_IT + q], filled(s) + MOD_IT + q // 2 + 1)
            for n, s in enumerate(V_SLOTS[1]):
                load(s, w_in[32 + n], filled(s) + MOD_IT + (5 if s >= 4 else 2))
            sp.dma_start(wr.rearrange("p k n -> p (k n)"), w_r).then_inc(consts_in, 16)
            for m in range(6):
                load(m, w_out[m], wo_fills[m] + 1)
            sp.wait_ge(att_done, HEADS)
            sp.dma_start(Z, x.rearrange("(t p) d -> p t d", p=P)).then_inc(xres_in, 16)
            for n in range(2):
                sp.dma_start(lna_b[:, n, :], ln_a[n:n + 1, :].to_broadcast([P, D])).then_inc(lna_in, 16)
            for m in range(6, KD):
                load(m % 6, w_out[m], wo_fills[m % 6] + m // 6 + 1)
            for t in range(TS):
                sp.wait_ge(xh_ready, t + 1)
                sp.dma_start(row_dram.rearrange("(t p h) d -> t p (h d)", t=TS, h=2)[t], XH[:, t, :]).then_inc(rows_out, 16)
            sp.wait_ge(table_ready, 1)
            n_exp = sp.value_load(tab[0:1, 0:1], min_val=2, max_val=NE)

            def load_expert(j, stages):
                e = sp.value_load(tab[0:1, bass.ds(j + OFF_E, 1)], min_val=0, max_val=NE - 1)
                before = sp.value_load(tab[0:1, bass.ds(j + OFF_C, 1)], min_val=0, max_val=NB)
                for c in stages:
                    if c < 4:
                        sp.wait_ge(w_used[c], before + 1)
                    else:
                        sp.wait_ge(wd_moved, j * 4 + (c - 3))
                    sp.sem_inc(sp_step, 1)
                    if c < 4:
                        for n, w in enumerate((w_gate, w_up)):
                            src = w[bass.ds(e, 1), c * 4 * P:(c + 1) * 4 * P, :].rearrange("o (k p) n -> p (o k) n", p=P)
                            sp.dma_start(WGU[:, c, n, :].rearrange("p (k n) -> p k n", k=4), src).then_inc(w_full[c], 16)
                    else:
                        src = w_down[bass.ds(e, 1), (c - 4) * P:(c - 3) * P, :].rearrange("o p n -> p (o n)")
                        sp.dma_start(WD_in[:, c - 4, :], src).then_inc(w_full[c], 16)

            sp.sem_inc(wd_moved, KE)
            load_expert(0, range(1))
            sp.wait_ge(slots_scattered, 16 * 2 * TS)
            for h in range(2):
                sp.dma_start(slots_i[h * B:(h + 1) * B, :], slot_dram.rearrange("(p n) o -> p (n o)", n=NB)).then_inc(slots_in, 16)
            load_expert(0, range(1, 2))
            sp.wait_ge(gathered, 16)
            load_expert(0, range(2, 8))
            with sp.Fori(1, n_exp) as j:
                load_expert(j, (4, 5, 6, 7, 0, 1, 2, 3))
            sp.wait_ge(rows_out, 16 * TS)
            sp.wait_ge(wd_moved, n_exp * 4 + 4)
            for n in range(2):
                sp.dma_start(lnf_b[:, n, :], ln_f[n:n + 1, :].to_broadcast([P, D])).then_inc(lnf_in, 16)
            n_blk = sp.value_load(tab[0:1, 1:2], min_val=1, max_val=NB - 3)
            sp.wait_ge(scattered, n_blk * 16 + 16)
            yv = y_dram.rearrange("(h t p k) d -> t p h k d", h=2, p=P, k=2)
            for t in range(TS):
                for h in range(2):
                    sp.dma_start(Y[:, t, :, h * H2:(h + 1) * H2], yv[t, :, h]).then_inc(token_rows_in[t], 16)
            for t in range(TS):
                sp.wait_ge(fin_ready, t + 1)
                sp.dma_start(out[t * P:(t + 1) * P, :], X1[:, t, :]).then_inc(out_done, 16)
            sp.wait_ge(out_done, 16 * TS)

        @block.tensor
        def _(pe):
            taken = [0] * 6

            def take(s):
                taken[s] += 1
                pe.wait_ge(ring_full[s], 16 * taken[s])

            def mod_tile(s, n):
                i, k = divmod(n, KD)
                if k == 0 and i >= 2:
                    pe.wait_ge(mod_col_ready, i - 1)
                take(s)
                for q in range(4):
                    mm = nc.tensor.matmul(bank[4 + i % 2][32 * q:32 * q + 32, :], cond[:, k, :], ring_row[:, s, q * S:(q + 1) * S],
                                          start=(k == 0), stop=(k == KD - 1), tile_position=(0, 32 * q))
                mm.then_inc(ring_used[s], 1)

            def mod_turn(i):
                pe.wait_ge(mod_row_ready, i + 1)
                for q in range(4):
                    mm = nc.tensor.transpose(bank[4 + i % 2][:, q * P:(q + 1) * P], mod_row[i][:, q * P:(q + 1) * P], ident)
                mm.then_inc(mod_turned, 1)

            pe.wait_ge(consts_in, 16)
            pe.wait_ge(silu_ready, 1)
            for n in range(N_MOD01):
                mod_tile(n % 6, n)
                k = n - TURN_FROM
                if 0 <= k < KD:
                    for part, tiles in enumerate((range(TS), range(TS, TS + TC))):
                        i = 2 * k + part
                        if i >= 4:
                            pe.wait_ge(xt_evac, i - 3)
                        for col, t in enumerate(tiles):
                            if k == 0:
                                pe.wait_ge(xn_ready, t + 1)
                            mm = nc.tensor.transpose(bank[i % 4][:, col * P:(col + 1) * P], xn[:, t, k * P:(k + 1) * P], ident)
                        mm.then_inc(xt_out, 1)

            pe.wait_ge(lam_prod, 1)
            nc.tensor.matmul(bank[7][:, 0:2], ones[0:DQ, :], lamt[0:DQ, 0:2], start=True, stop=True).then_inc(lam_out, 1)

            mod_turn(0)
            mod_turn(1)
            pe.wait_ge(xt_evac, 2 * KD)

            n_in = [0]

            def in_tile(s, b, with_ctx):
                take(s)
                n_in[0] += 1
                pe.wait_ge(tile_bank_free, n_in[0])
                for k in range(KD):
                    if n_in[0] == 1:
                        pe.wait_ge(lat_modulated, k + 1)
                    mm = nc.tensor.matmul(bank[b][:, :], ring[:, s, k, :], hT[:, k, 0:S], start=(k == 0), stop=(k == KD - 1))
                    if with_ctx:
                        mm = nc.tensor.matmul(bank[2 + b][:, 0:C], ring[:, s, k, :], hT[:, k, S:NT],
                                              start=(k == 0), stop=(k == KD - 1))
                mm.then_inc(ring_used[s], 1)

            def project(j0, count, with_ctx):
                for j in range(j0, j0 + count):
                    for u in range(2):
                        in_tile(3 * u, u, with_ctx)
                        for q in range(2):
                            mod_tile(3 * u + 1 + q, N_MOD01 + 4 * j + 2 * u + q)
                    if j == FAG_IT - 1:
                        mod_turn(2)

            def spread(b, col, done):
                for t in range(TS):
                    mm = nc.tensor.matmul(bank[b][:, t * P:(t + 1) * P], col[:, t:t + 1].to_broadcast([P, P]), ident,
                                          start=True, stop=True)
                mm.then_inc(done, 1)

            project(0, FAG_IT, False)

            pe.wait_ge(f_evac, NF)
            pe.wait_ge(lam_exp, 1)
            nf = 0
            for t in range(TS):
                for h in range(2):
                    if nf >= 2:
                        pe.wait_ge(f_evac, NF + nf - 1)
                    for g in range(2):
                        mm = nc.tensor.matmul(bank[6 + nf % 2][:, g * 2 * P:(g + 1) * 2 * P],
                                              uT[:, 2 * h + g, t * P:(t + 1) * P], cst("dftc"), start=True, stop=True)
                    mm.then_inc(f_out, 1)
                    nf += 1
            pe.wait_ge(dft_in, 16)
            pe.wait_ge(f_evac, NF + nf)
            for g in range(NF):
                if g >= 2:
                    pe.wait_ge(f_evac, NF + nf - 1)
                for t in range(TS):
                    for r in range(2):
                        mm = nc.tensor.matmul(bank[6 + nf % 2][:, :], ab[:, t, g, r * P:(r + 1) * P], dft_s[:, t, r, :],
                                              start=(t == 0 and r == 0), stop=(t == TS - 1 and r == 1))
                mm.then_inc(f_out, 1)
                nf += 1
            pe.wait_ge(wf_in, 16)
            pe.wait_ge(f_evac, NF + nf)
            for m in range(NF):
                if m >= 2:
                    pe.wait_ge(f_evac, NF + nf - 1)
                for k in range(NF):
                    mm = nc.tensor.matmul(bank[6 + nf % 2][:, :], wf[:, k, m * P:(m + 1) * P], yT[:, k, :],
                                          start=(k == 0), stop=(k == NF - 1))
                mm.then_inc(f_out, 1)
                nf += 1

            project(FAG_IT, QK_IT, False)

            pe.wait_ge(conv_done, NCV)
            pe.wait_ge(f_evac, NF + nf)
            for k in range(NCV):
                mm = nc.tensor.matmul(bank[6][:, :], ones, conv[:, k, :], start=(k == 0), stop=(k == NCV - 1))
            mm.then_inc(cstat_out, 1)
            pe.wait_ge(ctx_modulated, KD)
            in_tile(0, 0, True)
            pe.wait_ge(csq_ready, NCV)
            for t in range(TS):
                for k in range(NCV):
                    mm = nc.tensor.matmul(bank[7][:, t:t + 1], sig[:, k, t * P:(t + 1) * P], ones[:, 0:1], start=(k == 0), stop=(k == NCV - 1))
            mm.then_inc(cstat_out, 1)
            in_tile(3, 1, True)
            pe.wait_ge(crstd_ready, 1)
            spread(7, crstd, cstat_out)
            pe.wait_ge(wpw_in, 16)
            pe.wait_ge(csilu_done, NCV)
            for m in range(NCV):
                if m >= 2:
                    pe.wait_ge(pw_evac, m - 1)
                for k in range(NCV):
                    mm = nc.tensor.matmul(bank[6 + m % 2][:, :], wpw[:, k, m * P:(m + 1) * P], conv[:, k, :],
                                          start=(k == 0), stop=(k == NCV - 1))
                mm.then_inc(pw_out, 1)
            mod_turn(3)

            for s, n in ((1, 0), (2, 1), (4, 2), (5, 3)):
                mod_tile(s, N_MOD01 + 4 * (FAG_IT + QK_IT) + n)
            project(FAG_IT + QK_IT + 1, QK_IT - 1, True)

            q = 0
            for g in range(2):
                for t in range(TS + TC):
                    n_in[0] += 1
                    pe.wait_ge(tile_bank_free, n_in[0])
                    pairs = ((0, 4),) if g == 0 and t > 0 else ((0, 2), (2, 2))
                    for first, count in pairs:
                        s = V_SLOTS[g][first]
                        if t == 0:
                            for i in range(count):
                                take(s + i)
                        for k in range(KD):
                            mm = nc.tensor.matmul(bank[t % 2][:, first * P:(first + count) * P].rearrange("p (s n) -> p s n", n=P),
                                                  hT[:, k, t * P:(t + 1) * P], ring[:, s:s + count, k, :], start=(k == 0), stop=(k == KD - 1))
                    mm.then_inc(v_tile_out, 1)
                    if g == 0:
                        for _ in range((2, 2, 2, 1, 1, 0)[t]):
                            mod_tile(4 + q % 2, N_MOD01 + 4 * MOD_IT + q)
                            q += 1
                    if t == 1:
                        mod_turn(4 + g)
                pe.wait_ge(v_tile_out, 6 * (g + 1))
                for s in V_SLOTS[g]:
                    pe.sem_inc(ring_used[s], 1)
            pe.wait_ge(raw_free, 2 * HEADS + 2)
            pe.wait_ge(tile_bank_free, 28 + 12 + 2)

            def out_tile(m, ks):
                s = m % 6
                if ks[0] == 0:
                    pe.wait_ge(ring_full[s], 16 * (wo_fills[s] + m // 6 + 1))
                    pe.wait_ge(w_split, m + 1)
                if m >= 2:
                    pe.wait_ge(zt_ready, m - 1)
                for k in ks:
                    if m == 0:
                        pe.wait_ge(mix_split, k + 1)
                    wh, wl = w_hi_r[m % 3][:, k, :], w_lo_r[s][:, k, :]
                    xh, xl = mix_hi_r[k // 4][:, k % 4, :], mix_lo_r[k // 4][:, k % 4, :]
                    for i, (w, x_) in enumerate(((wh, xh), (wh, xl), (wl, xh))):
                        mm = nc.tensor.matmul(bank[m % 2][:, :], w, x_, start=(k == 0 and i == 0), stop=(k == KD - 1 and i == 2))
                if ks[-1] == KD - 1:
                    mm.then_inc(ring_used[s], 1)

            early = {ATT_STEPS + 6: range(8), ATT_STEPS + 7: range(8, 12)}

            for s in range(ATT_STEPS + 10):
                if s < ATT_STEPS:
                    h, qb = divmod(s, TS)
                    for m in range(2):
                        if s >= 1:
                            pe.wait_ge(e_done, 2 * (s - 1) + m + 1)
                        rows = slice(m * DQ, (m + 1) * DQ)
                        q = QT[rows, h, qb * P:(qb + 1) * P]
                        nc.tensor.matmul(bank[2 * m][:, :], q, KT[rows, h, 0:S], start=True, stop=True)
                        nc.tensor.matmul(bank[2 * m + 1][:, 0:C], q, KT[rows, h, S:NT], start=True, stop=True)\
                            .then_inc(sc_out, 1)
                if 2 <= s < ATT_STEPS + 2:
                    u = s - 2
                    pe.wait_ge(comb_done, u + 1)
                    if u >= 1:
                        pe.wait_ge(at_evac, 2 * u)
                    for kt in range(TS + TC):
                        mm = nc.tensor.transpose(bank[4 + kt // 4][:, (kt % 4) * P:(kt % 4 + 1) * P],
                                                 E[:, u % 3, 0, kt * P:(kt + 1) * P], ident)
                        if kt in (3, 5):
                            mm.then_inc(at_out, 1)
                if 6 <= s < 6 + 4 * HEADS:
                    h, part = divmod(s - 6, 4)
                    if part == 0:
                        pe.wait_ge(at_evac, 8 * (h + 1))
                    if part == 0 and h >= 1:
                        pe.wait_ge(o_copied, h)
                    for kt in ((0, 1), (2, 3), (4,), (5,))[part]:
                        mm = nc.tensor.matmul(bank[6][:, :], V[:, kt, h * P:(h + 1) * P], AT[:, h % 2, kt, :],
                                              start=(kt == 0), stop=(kt == TS + TC - 1))
                    if part == 3:
                        mm.then_inc(pv_out, 1)
                h = head_at(s, 8)
                if h is not None:
                    pe.wait_ge(o_squared, h + 1)
                    if h >= 1:
                        pe.wait_ge(att_done, h)
                    for qb in range(TS):
                        mm = nc.tensor.matmul(bank[7][:, qb:qb + 1], o_sq[:, qb * P:(qb + 1) * P], ones[:, 0:1], start=True, stop=True)
                    mm.then_inc(oss_out, 1)
                h = head_at(s, 9)
                if h is not None:
                    pe.wait_ge(orstd_ready, h + 1)
                    spread(7, o_var, orow_out)
                if s in early:
                    out_tile(0, early[s])
            pe.wait_ge(att_done, HEADS)

            def turn(m):
                pe.wait_ge(zt_ready, m + 1)
                if m >= 2:
                    pe.wait_ge(z_added, m - 1)
                for t in range(TS):
                    mm = nc.tensor.transpose(bank[4 + m % 2][:, t * P:(t + 1) * P], zT[:, m % 2, t * P:(t + 1) * P], ident)
                mm.then_inc(zt_out, 1)

            for m in range(KD):
                out_tile(m, range(12, KD) if m == 0 else range(KD))
                if m >= 1:
                    turn(m - 1)
            turn(KD - 1)
            pe.wait_ge(consts_in, 32)
            pe.wait_ge(mod_biased, 6)
            for k in range(KD):
                mm = nc.tensor.matmul(bank[3][:, 0:NG + NE], mods[:, 3 * KD + k, 0:1].to_broadcast([P, P]), wr[:, k, :],
                                      start=(k == 0), stop=(k == KD - 1))
            mm.then_inc(shift_out, 1)
            pe.wait_ge(z_added, KD)
            for h in range(2):
                for k in range(KD // 2):
                    mm = nc.tensor.matmul(bank[4 + k // 4][h * B:(h + 1) * B, (k % 4) * P:(k % 4 + 1) * P],
                                          mods[:, 5 * KD + h * (KD // 2) + k, 0:1].to_broadcast([P, B]), ident, start=True, stop=True,
                                          tile_position=(0, h * B))
            mm.then_inc(g5_out, 1)

            def logits(n):
                t, q = divmod(n, 4)
                pe.wait_ge(h_evac, n + 1)
                for i in range(4):
                    mm = nc.tensor.matmul(bank[2][:, t * (NG + NE):(t + 1) * (NG + NE)], h2[:, n % 4, i * P:(i + 1) * P],
                                          wr[:, 4 * q + i, :], start=(q == 0 and i == 0), stop=(q == 3 and i == 3))
                return mm

            pe.wait_ge(wr_scaled, 1)
            for n in range(4 * TS):
                t, q = divmod(n, 4)
                if n >= 4:
                    pe.wait_ge(h_evac, n - 3)
                if q == 0:
                    pe.wait_ge(xh_ready, t + 1)
                for i in range(4):
                    mm = nc.tensor.transpose(bank[(0, 1, 6, 7)[n % 4]][:, i * P:(i + 1) * P], XH[:, t, (4 * q + i) * P:(4 * q + i + 1) * P], ident)
                mm.then_inc(h_out, 1)
                if n >= 2:
                    logits(n - 2)
            logits(4 * TS - 2)
            logits(4 * TS - 1).then_inc(logits_out, 1)
            pe.wait_ge(o_ready, 1)
            for t in range(TS):
                mm = nc.tensor.matmul(bank[7][:, 0:NE], ones, Osum[:, t, :], start=(t == 0), stop=(t == TS - 1))
            mm.then_inc(total_out, 1)
            pe.wait_ge(shift_copied, 1)
            for t in range(TS):
                for tt in range(t + 1):
                    mm = nc.tensor.matmul(bank[3][:, t * NE:(t + 1) * NE], upper if tt == t else ones, Osum[:, tt, :],
                                          start=(tt == 0), stop=(tt == t))
            mm.then_inc(rank_out, 1)

            pe.wait_ge(tcol_ready, 1)
            for n in range(3):
                mm = nc.tensor.matmul(bank[2][:, n * P:(n + 1) * P], tcol[:, n:n + 1].to_broadcast([P, P]), ident, start=True, stop=True)
            mm.then_inc(tcol_turned, 1)

            pe.wait_ge(table_ready, 1)
            n_blk = pe.value_load(tab[0:1, 1:2], min_val=1, max_val=NB - 3)

            def turn_rows(n, ks=range(KD // 2)):
                pe.wait_ge(xg_ready, n + 1)
                for k in ks:
                    mm = nc.tensor.transpose(bank[k // 4][:, (k % 4) * P:(k % 4 + 1) * P], xg[:, k * P:(k + 1) * P], ident)
                if KD // 2 - 1 in ks:
                    mm.then_inc(xg_turned, 1)

            turn_rows(0)
            with pe.Fori(0, n_blk) as g:
                j = pe.value_load(tab[0:1, bass.ds(g + OFF_J, 1)], min_val=0, max_val=NE - 1)
                pe.wait_ge(xgT_ready, g + 1)
                for c in range(4):
                    pe.wait_ge(w_full[c], j * 32 + 32)
                    for kk in range(4):
                        k = 4 * c + kk
                        for n in range(2):
                            mm = nc.tensor.matmul(bank[2][n * B:(n + 1) * B, :], xgT[:, k, :], WGU[:, c, n, kk * DE:(kk + 1) * DE],
                                                  start=(k == 0), stop=(k == KD - 1), tile_position=(0, n * B))
                    mm.then_inc(w_used[c], 1)
                turn_rows(g + 1, range(4))
                pe.wait_ge(gu_ready, g + 1)
                for m in range(KE):
                    mm = nc.tensor.transpose(bank[3][:, m * P:(m + 1) * P], gu[:, m * P:(m + 1) * P], ident)
                mm.then_inc(gu_turned, 1)
                turn_rows(g + 1, range(4, 8))
                pe.wait_ge(act_ready, g + 1)
                for c in range(KE):
                    pe.wait_ge(wd_moved, j * 4 + (c + 5))
                    for n in range(4):
                        h, b = n % 2, n // 2
                        mm = nc.tensor.matmul(bank[4 + b][h * B:(h + 1) * B, :], actT[:, c, :],
                                              WD[:, c, (2 * h + b) * S:(2 * h + b + 1) * S],
                                              start=(c == 0), stop=(c == KE - 1), tile_position=(0, h * B))
                    mm.then_inc(w_used[4 + c], 1)

        @block.scalar
        def _(act):
            act.sem_inc(tile_bank_free, 2)
            act.wait_ge(params_in, 16)
            nc.scalar.activation(cond, cond, ACT.Silu).then_inc(silu_ready, 1)

            ring_need = lambda s, n: act.wait_ge(ring_used[s], n + 1)

            def mod_row_out(i, s, n):
                ring_need(s, n)
                nc.scalar.copy(mod_row[i], bank[4 + i % 2][:, :]).then_inc(mod_row_ready, 1)

            def mod_cols_out(i):
                act.wait_ge(mod_turned, i + 1)
                nc.scalar.copy(mods[:, i * KD:(i + 1) * KD, :].rearrange("p (q c) l -> p c q l", c=4),
                               bank[4 + i % 2][:, :].rearrange("p (c q r) -> p c q r", c=4, q=4)[:, :, :, 0:2]).then_inc(mod_col_ready, 1)

            for k in range(KD):
                for part in range(2):
                    n = 2 * k + part
                    act.wait_ge(xt_out, n + 1)
                    w = C if part else S
                    nc.scalar.copy(hT[:, k, part * S:part * S + w], bank[n % 4][:, 0:w]).then_inc(xt_evac, 1)
            mod_row_out(0, (KD - 1) % 6, (KD - 1) // 6 + 1)
            mod_row_out(1, (N_MOD01 - 1) % 6, (N_MOD01 - 1) // 6 + 1)
            mod_cols_out(0)
            mod_cols_out(1)
            act.wait_ge(lam_out, 1)
            nc.scalar.activation(lamt[:, 2:4], bank[7][:, 0:2], ACT.Exp).then_inc(lam_exp, 1)
            act.wait_ge(mod_biased, 2)
            act.wait_ge(xt_evac, 2 * KD)
            for k in range(KD):
                nc.scalar.activation(hT[:, k, 0:S], hT[:, k, 0:S], ACT.Identity, bias=mods[:, k, 0:1], scale=mods[:, KD + k, 0:1])\
                    .then_inc(lat_modulated, 1)
            nc.scalar.mul(qb8, par("b_in")[:, 12:20], ATT_SCALE).then_inc(silu_ready, 1)
            act.wait_ge(silu_ready, 2)

            def done_tile(j, u):
                act.wait_ge(ring_used[3 * u], j + (filled(3 * u) + 2))

            b_in = par("b_in")
            for j0, kind in ((0, "f"), (2, "a"), (4, "g")):
                with act.Fori(j0, j0 + 2) as j:
                    for u in range(2):
                        done_tile(j, u)
                        bias = b_in[:, bass.ds(j * 2 + u, 1)]
                        i = (j - j0) * 2 + u
                        if kind == "f":
                            o = nc.scalar.activation(uT[:, bass.ds(i, 1), :].rearrange("p o n -> p (o n)"), bank[u][:, :], ACT.Identity, bias=bias)
                        elif kind == "a":
                            if u == 0:
                                act.wait_ge(glu_zero, 1)
                            o = nc.scalar.activation(glu[:, bass.ds(i, 1), PAD:PAD + S].rearrange("p o n -> p (o n)"), bank[u][:, :], ACT.Identity, bias=bias)
                        else:
                            o = nc.scalar.activation(sig[:, bass.ds(i, 1), :].rearrange("p o n -> p (o n)"), bank[u][:, :], ACT.Sigmoid, bias=bias)
                        o.then_inc(tile_bank_free, 1)
                act.wait_ge(tile_bank_free, 2 + 2 * (j0 + 2))
                if kind == "a":
                    mod_row_out(2, 5, filled(5) + 4)
                {"f": lambda: act.sem_inc(f_evac, NF), "a": lambda: act.sem_inc(a_ready, 1), "g": lambda: act.sem_inc(sig_ready, 1)}[kind]()

            mod_cols_out(2)
            nf = 0
            for t in range(TS):
                for h in range(2):
                    act.wait_ge(f_out, nf + 1)
                    nc.scalar.copy(ab[:, t, 2 * h:2 * h + 2, :], bank[6 + nf % 2][:, :].rearrange("p (g n) -> p g n", g=2)).then_inc(f_evac, 1)
                    nf += 1
            for g in range(NF):
                act.wait_ge(f_out, nf + 1)
                nc.scalar.copy(yT[:, g, :], bank[6 + nf % 2][:, :]).then_inc(f_evac, 1)
                nf += 1
            for m in range(NF):
                act.wait_ge(f_out, nf + 1)
                nc.scalar.copy(mixT[:, m, :], bank[6 + nf % 2][:, :]).then_inc(f_evac, 1)
                nf += 1

            def rope_source(j0, count, scale, bias_all, bias_at, ctx_too):
                with act.Fori(j0, j0 + count) as j:
                    for u in range(2):
                        done_tile(j, u)
                        i = (j - j0) * 2 + u
                        bias = bias_all[:, bass.ds(i + bias_at, 1)]
                        act.wait_ge(raw_free, j * 2 + (u + 1 - 2 * FAG_IT))
                        main = nc.scalar.activation(rope_raw[:, u, :], bank[u][:, :], ACT.Identity, bias=bias, scale=scale)
                        main.then_inc(rope_raw_done, 1)
                        if ctx_too:
                            nc.scalar.activation(KT[:, bass.ds(i, 1), S:NT].rearrange("p o n -> p (o n)"), bank[2 + u][:, 0:C],
                                                 ACT.Identity, bias=bias).then_inc(ctx_keys_done, 1)
                            act.wait_ge(ctx_keys_done, i + 1)
                        act.wait_ge(rope_raw_done, j * 2 + (u + 1 - 2 * FAG_IT))
                        act.sem_inc(tile_bank_free, 1)
                        for q in range(4):
                            o = nc.scalar.copy(rope_swap[32 * q:32 * q + 32, u, :], rope_raw[32 * (q ^ 1):32 * (q ^ 1) + 32, u, :])
                        o.then_inc(raw_ready, 1)

            act.sem_inc(raw_free, 2)
            rope_source(FAG_IT, QK_IT, ATT_SCALE, qb8, 0, False)
            mod_row_out(3, 5, filled(5) + 8)

            for k in range(NCV):
                act.wait_ge(cmean_done, k + 1)
                nc.scalar.activation(sig[:, k, :], conv[:, k, :], ACT.Square).then_inc(csq_ready, 1)
            for k in range(NCV):
                act.wait_ge(cnorm_done, k + 1)
                nc.scalar.activation(conv[:, k, :], conv[:, k, :], ACT.Silu, bias=par("cln_b")[:, k:k + 1],
                                     scale=par("cln_g")[:, k:k + 1]).then_inc(csilu_done, 1)
            for m in range(NCV):
                act.wait_ge(pw_out, m + 1)
                nc.scalar.copy(mixT[:, NCV + m, :], bank[6 + m % 2][:, :]).then_inc(pw_evac, 1)
            mod_cols_out(3)

            rope_source(FAG_IT + QK_IT, QK_IT, 1.0, b_in, 20, True)

            mod_row_out(4, 5, filled(5) + 12)
            mod_row_out(5, 5, filled(5) + MOD_IT + 4)
            mod_cols_out(4)
            mod_cols_out(5)

            def mix_high(k):
                act.wait_ge(sc_out, 48 if k < 8 else 64)
                if k >= 8:
                    act.wait_ge(att_done, k - 7)
                nc.scalar.copy(mix_hi_r[k // 4][:, k % 4, :], mixT[:, k, :]).then_inc(mix_hi_ready, 1)

            def w_high(m):
                act.wait_ge(ring_full[m % 6], 16 * (wo_fills[m % 6] + m // 6 + 1))
                if m >= 3:
                    act.wait_ge(ring_used[(m - 3) % 6], wo_fills[(m - 3) % 6] + (m - 3) // 6 + 2)
                nc.scalar.copy(w_hi_r[m % 3], ring[:, m % 6, :, :]).then_inc(w_hi_ready, 1)

            for s in range(ATT_STEPS + 10):
                if s < ATT_STEPS:
                    for m in range(2):
                        n = 2 * s + m
                        act.wait_ge(mx_done, n + 1)
                        if s >= 3:
                            act.wait_ge(at_out, 2 * (s - 2))
                        for i, (lo, w) in enumerate(((0, S), (S, C))):
                            e = nc.scalar.activation(E[:, s % 3, m, lo:lo + w], bank[2 * m + i][:, 0:w], ACT.Exp, bias=nmax[:, n, :],
                                                     accum_out=zpart[:, 2 * n + i, :])
                        e.then_inc(e_done, 1)
                if 2 <= s < ATT_STEPS + 2:
                    u = s - 2
                    h, qb = divmod(u, TS)
                    if h >= 2:
                        act.wait_ge(pv_out, h - 1)
                    act.wait_ge(at_out, 2 * u + 1)
                    nc.scalar.copy(AT[:, h % 2, 0:4, qb * P:(qb + 1) * P], bank[4][:, :].rearrange("p (k n) -> p k n", n=P)).then_inc(at_evac, 1)
                    act.wait_ge(at_out, 2 * u + 2)
                    nc.scalar.copy(AT[:, h % 2, 4:6, qb * P:(qb + 1) * P], bank[5][:, 0:C].rearrange("p (k n) -> p k n", n=P)).then_inc(at_evac, 1)
                h = head_at(s, 7)
                if h is not None:
                    act.wait_ge(o_copied, h + 1)
                    if h >= 1:
                        act.wait_ge(oss_out, h)
                    nc.scalar.activation(o_sq, mixT[:, 8 + h, :], ACT.Square).then_inc(o_squared, 1)
                for k in split_at.get(s, ()):
                    mix_high(k)
                if s == ATT_STEPS + 3:
                    w_high(0)
            mix_high(KD - 1)
            w_high(1)
            act.wait_ge(mod_biased, 3)
            for m in range(KD):
                if m + 2 < KD:
                    w_high(m + 2)
                act.wait_ge(ring_used[m % 6], wo_fills[m % 6] + m // 6 + 2)
                if m >= 2:
                    act.wait_ge(zt_out, m - 1)
                nc.scalar.activation(zT[:, m % 2, :], bank[m % 2][:, :], ACT.Copy, scale=mods[:, 2 * KD + m, 0:1]).then_inc(zt_ready, 1)
            act.wait_ge(shift_out, 1)
            nc.scalar.copy(lgb, bank[3][:, 0:NG + NE]).then_inc(shift_copied, 1)
            act.wait_ge(g5_out, 1)
            for q in range(2):
                nc.scalar.copy(g5b[:, q * S:(q + 1) * S], bank[4 + q][:, :]).then_inc(g5_ready, 1)
            for t in range(TS):
                act.wait_ge(x_rstd_ready, t + 1)
                nc.scalar.activation(XH[:, t, :], X1[:, t, :], ACT.Identity, bias=nmean[:, t, :], scale=rstd2[:, t, :]).then_inc(xh_ready, 1)
                for q in range(4):
                    n = 4 * t + q
                    act.wait_ge(h_out, n + 1)
                    nc.scalar.copy(h2[:, n % 4, :], bank[(0, 1, 6, 7)[n % 4]][:, :]).then_inc(h_evac, 1)
            for n in range(2):
                act.wait_ge(gexp_need, n + 1)
                v = (gl, le)[n]
                nc.scalar.activation(v, v, ACT.Exp).then_inc(gexp_done, 1)

            act.wait_ge(table_ready, 1)
            n_exp = act.value_load(tab[0:1, 0:1], min_val=2, max_val=NE)
            with act.Fori(0, n_exp) as j:
                before = act.value_load(tab[0:1, bass.ds(j + OFF_C, 1)], min_val=0, max_val=NB)
                end = act.value_load(tab[0:1, bass.ds(j + (OFF_C + 1), 1)], min_val=1, max_val=NB)
                for c in range(KE):
                    act.wait_ge(w_used[4 + c], before + 1)
                    act.wait_ge(w_full[4 + c], j * 16 + 16)
                    act.sem_inc(act_step, 1)
                    nc.scalar.copy(WD[:, c, :], WD_in[:, c, :]).then_inc(wd_moved, 1)
                with act.Fori(before, end) as g:
                    act.wait_ge(gu_turned, g + 1)
                    nc.scalar.activation(sil, bank[3][:, :].rearrange("p (k h n) -> p k h n", h=2, n=B)[:, :, 0, :], ACT.Silu).then_inc(silu_done, 1)
            for t in range(TS):
                nc.scalar.activation(X1[:, t, :], X1[:, t, :], ACT.Copy, scale=ALPHA).then_inc(x1_scaled, 1)
            for t in range(TS):
                act.wait_ge(token_rows_in[t], 16 + 32)
                nc.scalar.activation(Y[:, t, 0, :], Y[:, t, 0, :], ACT.Copy, scale=wtok[:, t, 0:1]).then_inc(w0_done, 1)

        @block.vector
        def _(dve):
            v = nc.vector
            n_chain = [0]

            def after(ins):
                n_chain[0] += 1
                ins.then_inc(dve_chain, 1)
                dve.wait_ge(dve_chain, n_chain[0])

            after(v.memset(half, -0.5))
            for t in range(TS + TC):
                dve.wait_ge(token_rows_in[t], 16)
                for q in range(4):
                    o = v.bn_stats(stats[:, t, q, :], xn[:, t, q * S:(q + 1) * S])
                after(o)
                after(v.bn_aggr(mv[:, t, :], stats[:, t, :, :].rearrange("p q n -> p (q n)")))
                v.tensor_scalar_add(rstd[:, t, :], mv[:, t, 1:2], EPS).then_inc(z_rstd_need, 1)
                dve.wait_ge(z_rstd_ready, t + 1)
                v.tensor_scalar(xn[:, t, :], xn[:, t, :], mv[:, t, 0:1], rstd[:, t, :], ALU.subtract, ALU.mult).then_inc(xn_ready, 1)
            dve.wait_ge(params_in, 16)
            v.tensor_tensor(lamt[0:DQ, 0:2], par("lam")[0:DQ, 0:2], par("lam")[0:DQ, 2:4], ALU.mult).then_inc(lam_prod, 1)
            v.tensor_scalar_mul(g08, par("subln"), 1.0 - LAM_INIT).then_inc(lam_prod, 1)

            dve.wait_ge(mod_biased, 2)
            dve.wait_ge(xt_evac, 2 * KD)
            for k in range(KD):
                v.tensor_scalar(hT[:, k, S:NT], hT[:, k, S:NT], mods[:, KD + k, 1:2], mods[:, k, 1:2], ALU.mult, ALU.add)\
                    .then_inc(ctx_modulated, 1)

            dve.wait_ge(a_ready, 1)
            dve.wait_ge(sig_ready, 1)
            for k in range(NCV):
                after(v.tensor_tensor(glu[:, k, PAD:PAD + S], glu[:, k, PAD:PAD + S], sig[:, k, :], ALU.mult))
            cw = par("conv_w").rearrange("p (k t) -> p k t", t=CW)
            for tap in range(CW):
                for k in range(NCV):
                    if tap == 0:
                        o = v.tensor_scalar(conv[:, k, :], glu[:, k, 0:S], cw[:, k, 0:1], par("conv_b")[:, k:k + 1], ALU.mult, ALU.add)
                    else:
                        dve.wait_ge(conv_step, (tap - 1) * NCV + k + 1)
                        o = v.scalar_tensor_tensor(conv[:, k, :], glu[:, k, tap:tap + S], cw[:, k, tap:tap + 1], conv[:, k, :],
                                                   ALU.mult, ALU.add)
                    o.then_inc(conv_done if tap == CW - 1 else conv_step, 1)
            dve.wait_ge(cstat_out, 1)
            after(v.tensor_scalar_mul(cmean, bank[6][:, :], 1.0 / (NCV * P)))
            for k in range(NCV):
                v.tensor_tensor(conv[:, k, :], conv[:, k, :], cmean, ALU.subtract).then_inc(cmean_done, 1)
            dve.wait_ge(cstat_out, 2)
            v.tensor_scalar(crstd, bank[7][:, 0:TS], 1.0 / (NCV * P), EPS, ALU.mult, ALU.add).then_inc(cvar_done, 1)
            dve.wait_ge(cstat_out, 3)
            for k in range(NCV):
                v.tensor_tensor(conv[:, k, :], conv[:, k, :], bank[7][:, :], ALU.mult).then_inc(cnorm_done, 1)

            dve.wait_ge(bv_in, 16)
            dve.wait_ge(raw_free, 2 * HEADS + 2)
            for g in range(2):
                for t in range(TS + TC):
                    dve.wait_ge(v_tile_out, 6 * g + t + 1)
                    v.tensor_tensor(V[:, t, g * S:(g + 1) * S], bank[t % 2][:, :], bv_b[:, g * S:(g + 1) * S], ALU.add)\
                        .then_inc(tile_bank_free, 1)
            dve.wait_ge(lam_exp, 1)
            after(v.tensor_tensor(lamt[:, 4:5], lamt[:, 3:4], lamt[:, 2:3], ALU.subtract))
            after(v.tensor_scalar_add(lamt[:, 5:6], lamt[:, 4:5], -LAM_INIT))

            def mix_low(k):
                dve.wait_ge(mix_hi_ready, k + 1)
                v.tensor_tensor(mix_lo_r[k // 4][:, k % 4, :], mixT[:, k, :], mix_hi_r[k // 4][:, k % 4, :].bitcast(F32), ALU.subtract).then_inc(mix_split, 1)

            def w_low(m):
                dve.wait_ge(w_hi_ready, m + 1)
                w = ring[:, m % 6, :, :]
                v.tensor_tensor(w_lo_r[m % 6], w, w_hi_r[m % 3].bitcast(F32), ALU.subtract).then_inc(w_split, 1)

            def head_copy(h):
                dve.wait_ge(pv_out, h + 1)
                v.tensor_copy(mixT[:, 8 + h, :], bank[6][:, :]).then_inc(o_copied, 1)

            for s in range(ATT_STEPS + 10):
                if s < ATT_STEPS:
                    for m in range(2):
                        n = 2 * s + m
                        dve.wait_ge(sc_out, n + 1)
                        v.reduce_max(zpart[:, 2 * n, :], bank[2 * m][:, :], axis=AX.X).then_inc(dve_max, 1)
                        v.reduce_max(zpart[:, 2 * n + 1, :], bank[2 * m + 1][:, 0:C], axis=AX.X).then_inc(dve_max, 1)
                        dve.wait_ge(dve_max, 2 * n + 2)
                        v.tensor_scalar(nmax[:, n, :], zpart[:, 2 * n, :], zpart[:, 2 * n + 1, :], -1.0, ALU.max, ALU.mult).then_inc(mx_done, 1)
                if 1 <= s <= ATT_STEPS:
                    u = s - 1
                    dve.wait_ge(e_done, 2 * u + 2)
                    after(v.tensor_tensor(zsum[:, 2 * u:2 * u + 2, :], zpart[:, 4 * u:4 * u + 4:2, :], zpart[:, 4 * u + 1:4 * u + 4:2, :], ALU.add))
                    after(v.reciprocal(rz[:, 2 * u:2 * u + 2, :], zsum[:, 2 * u:2 * u + 2, :]))
                    after(v.tensor_scalar(E[:, u % 3, 1, :], E[:, u % 3, 1, :], rz[:, 2 * u + 1, :], lamt[:, 5:6], ALU.mult, ALU.mult))
                    v.scalar_tensor_tensor(E[:, u % 3, 0, :], E[:, u % 3, 0, :], rz[:, 2 * u, :], E[:, u % 3, 1, :],
                                           ALU.mult, ALU.add).then_inc(comb_done, 1)
                h = head_at(s, 6)
                if h is not None:
                    head_copy(h)
                h = head_at(s, 8)
                if h is not None:
                    dve.wait_ge(oss_out, h + 1)
                    if h >= 1:
                        dve.wait_ge(dve_chain, n_chain[0])
                    v.tensor_scalar(o_var, bank[7][:, 0:TS], 1.0 / P, EPS, ALU.mult, ALU.add).then_inc(ovar_done, 1)
                h = head_at(s, 9)
                if h is not None:
                    dve.wait_ge(orow_out, h + 1)
                    v.scalar_tensor_tensor(mixT[:, 8 + h, :], mixT[:, 8 + h, :], g08, bank[7][:, :], ALU.mult, ALU.mult).then_inc(att_done, 1)
                for k in split_at.get(s, ()):
                    mix_low(k)
                if s == ATT_STEPS + 3:
                    w_low(0)

            mix_low(KD - 1)
            w_low(1)
            dve.wait_ge(xres_in, 16)
            for m in range(KD):
                if m + 2 < KD:
                    w_low(m + 2)
                dve.wait_ge(zt_out, m + 1)
                zz = Z[:, :, m * P:(m + 1) * P]
                v.scalar_tensor_tensor(zz, zz, ALPHA, bank[4 + m % 2][:, :].rearrange("p (t n) -> p t n", n=P), ALU.mult, ALU.add)\
                    .then_inc(z_added, 1)
                if m % 4 == 3:
                    dve.wait_ge(z_added, m + 1)
                    q = m // 4
                    for t in range(TS):
                        o = v.bn_stats(stats[:, t, q, :], Z[:, t, q * S:(q + 1) * S])
            after(o)
            dve.wait_ge(lna_in, 32)

            def norm(t, src, dst, n_root, need, ready):
                after(v.bn_aggr(mv[:, t, :], stats[:, t, :, :].rearrange("p q n -> p (q n)")))
                v.tensor_scalar_add(rstd[:, t, :], mv[:, t, 1:2], EPS).then_inc(need, 1)
                dve.wait_ge(ready, n_root)
                return v.tensor_scalar(dst, src, mv[:, t, 0:1], rstd[:, t, :], ALU.subtract, ALU.mult)

            def full_stats(t, src):
                for q in range(4):
                    o = v.bn_stats(stats[:, t, q, :], src[:, q * S:(q + 1) * S])
                after(o)

            for t in range(TS):
                after(v.bn_aggr(mv[:, t, :], stats[:, t, :, :].rearrange("p q n -> p (q n)")))
                o = v.tensor_scalar_add(rstd[:, t, :], mv[:, t, 1:2], EPS)
            o.then_inc(z_rstd_need, 1)
            for t in range(TS):
                if t == 0:
                    dve.wait_ge(z_rstd_ready, 7)
                after(v.scalar_tensor_tensor(Z[:, t, :], Z[:, t, :], mv[:, t, 0:1], lna_b[:, 0, :], ALU.subtract, ALU.mult))
                after(v.scalar_tensor_tensor(X1[:, t, :], Z[:, t, :], rstd[:, t, :], lna_b[:, 1, :], ALU.mult, ALU.add))
                full_stats(t, X1[:, t, :])
                after(v.bn_aggr(mv2[:, t, :], stats[:, t, :, :].rearrange("p q n -> p (q n)")))
                v.tensor_scalar_add(rstd2[:, t, :], mv2[:, t, 1:2], EPS).then_inc(x_rstd_need, 1)

            bc = lambda ap, *shape: ap.to_broadcast(list(shape))
            after(v.tensor_copy(vali, cst("val")))
            dve.wait_ge(logits_out, 1)
            dve.wait_ge(lgb_ready, 1)
            br = lgb.rearrange("p (o n) -> p o n", o=1)
            after(v.tensor_tensor(lg, bank[2][:, 0:TS * (NG + NE)].rearrange("p (t n) -> p t n", t=TS), bc(br, P, TS, NG + NE), ALU.add))
            after(v.tensor_reduce(r1, lg[:, :, 0:NG], axis=AX.X, op=ALU.max))
            v.tensor_tensor(gl, lg[:, :, 0:NG], bc(r1, P, TS, NG), ALU.subtract).then_inc(gexp_need, 1)
            dve.wait_ge(gexp_done, 1)
            after(v.tensor_reduce(r2, gl, axis=AX.X, op=ALU.add))
            after(v.reciprocal(r3, r2))

            def first_max(dst, src, mx, n, tmp):
                first = cst("first")[:, EG - n:EG].rearrange("p (o n) -> p o n", o=1)
                after(v.tensor_tensor(tmp, src, bc(mx, P, TS, n), ALU.is_equal))
                after(v.tensor_tensor(tmp, tmp, bc(first, P, TS, n), ALU.mult))
                after(v.tensor_reduce(r2, tmp, axis=AX.X, op=ALU.max))
                after(v.tensor_tensor(dst, tmp, bc(r2, P, TS, n), ALU.is_equal))

            after(v.tensor_reduce(r1, gl, axis=AX.X, op=ALU.max))
            first_max(gs, gl, r1, NG, t8[:, :, 0:NG])
            after(v.tensor_tensor(le, lg[:, :, NG:NG + EG], bc(gs[:, :, 0:1], P, TS, EG), ALU.mult))
            for g in range(1, NG):
                after(v.tensor_tensor(t8, lg[:, :, NG + g * EG:NG + (g + 1) * EG], bc(gs[:, :, g:g + 1], P, TS, EG), ALU.mult))
                after(v.tensor_tensor(le, le, t8, ALU.add))
            after(v.tensor_reduce(r1, le, axis=AX.X, op=ALU.max))
            v.tensor_tensor(le, le, bc(r1, P, TS, EG), ALU.subtract).then_inc(gexp_need, 1)
            dve.wait_ge(gexp_done, 2)
            after(v.tensor_reduce(r1, le, axis=AX.X, op=ALU.max))
            first_max(oh[:, 0], le, r1, EG, t8)
            after(v.scalar_tensor_tensor(le, oh[:, 0], -2.0, le, ALU.mult, ALU.add))
            after(v.tensor_reduce(r1, le, axis=AX.X, op=ALU.max))
            first_max(oh[:, 1], le, r1, EG, t8)
            for k in range(2):
                for g in range(NG):
                    o = v.tensor_tensor(O[:, k, :, g * EG:(g + 1) * EG], oh[:, k], bc(gs[:, :, g:g + 1], P, TS, EG), ALU.mult)
            after(o)
            v.tensor_tensor(Osum, O[:, 0], O[:, 1], ALU.add).then_inc(o_ready, 1)
            after(v.tensor_scalar_add(r2, r1, 1.0))
            after(v.reciprocal(r2, r2))
            after(v.tensor_tensor(wtok[:, :, 0:1], r2, r3, ALU.mult))
            after(v.tensor_tensor(wtok[:, :, 1:2], wtok[:, :, 0:1], r1, ALU.mult))
            dve.wait_ge(total_out, 1)
            after(v.tensor_copy(cnti, bank[7][:, 0:NE]))
            after(v.tensor_single_scalar(cnti, cnti, B - 1, ALU.add))
            after(v.tensor_single_scalar(cnti, cnti, 6, ALU.logical_shift_right))
            after(v.tensor_copy(nblk, cnti))
            after(v.tensor_tensor_scan(cum, bc(ones[:, 0:1], P, NE), nblk, 0.0, ALU.mult, ALU.add))
            after(v.tensor_single_scalar(act_e, nblk, 0.0, ALU.is_gt))
            after(v.tensor_tensor_scan(ordn, bc(ones[:, 0:1], P, NE), act_e, 0.0, ALU.mult, ALU.add))
            after(v.tensor_scalar_add(ordn, ordn, -1.0))
            after(v.tensor_scalar(place, ordn, cst("iota_p"), None, ALU.is_equal))
            after(v.tensor_tensor(place, place, act_e, ALU.mult))
            v.tensor_tensor(t32[:, 0, :], place, cst("iota")[:, 0:NE], ALU.mult)
            after(v.tensor_scalar(t32[:, 1, :], ordn, cst("iota_p"), None, ALU.is_lt))
            after(v.tensor_tensor(t32[:, 1, :], t32[:, 1, :], nblk, ALU.mult))
            after(v.tensor_reduce(tcol[:, 0:2], t32[:, 0:2, :], axis=AX.X, op=ALU.add))
            after(v.tensor_scalar(place, cum, cst("iota_p"), None, ALU.is_le))
            after(v.tensor_tensor(place, place, act_e, ALU.mult))
            v.tensor_reduce(tcol[:, 2:3], place, axis=AX.X, op=ALU.add).then_inc(tcol_ready, 1)
            v.tensor_scalar_add(tab[0:1, 0:1], ordn[0:1, NE - 1:NE], 1.0)
            v.tensor_copy(tab[0:1, 1:2], cum[0:1, NE - 1:NE])
            after(v.tensor_tensor(pst, cum, nblk, ALU.subtract))
            after(v.tensor_scalar_mul(pst, pst, float(B)))
            dve.wait_ge(rank_out, 1)
            after(v.tensor_tensor(prk, bank[3][:, 0:TS * NE].rearrange("p (t n) -> p t n", t=TS),
                                  bc(pst.rearrange("p (o n) -> p o n", o=1), P, TS, NE), ALU.add))
            for k in range(2):
                after(v.tensor_tensor(t32, O[:, k], prk, ALU.mult))
                after(v.tensor_reduce(slot[:, k, :], t32, axis=AX.X, op=ALU.add))
            dve.wait_ge(tcol_turned, 1)
            v.tensor_copy(tab[0:1, OFF_E:OFF_E + NE], bank[2][0:1, 0:NE])
            v.tensor_copy(tab[0:1, OFF_C:OFF_C + NE + 1], bank[2][0:1, P:P + NE + 1])
            after(v.tensor_copy(tab[0:1, OFF_J:OFF_J + NB], bank[2][0:1, 2 * P:2 * P + NB]))
            dve.sem_inc(table_ready, 1)
            after(v.tensor_copy(sloti, slot.rearrange("p k t -> p (k t)")))
            after(v.tensor_single_scalar(addri, sloti, 6, ALU.logical_shift_right))
            after(v.tensor_copy(colf, addri))
            after(v.tensor_single_scalar(sloti, sloti, B - 1, ALU.bitwise_and))
            after(v.tensor_copy(addr.rearrange("p k t -> p (k t)"), sloti))
            after(v.scalar_tensor_tensor(addr.rearrange("p k t -> p (k t)"), addr.rearrange("p k t -> p (k t)"), float(NB), colf, ALU.mult, ALU.add))
            v.tensor_copy(addri, addr.rearrange("p k t -> p (k t)")).then_inc(addr_ready, 1)
            dve.wait_ge(slots_in, 32)
            after(v.tensor_single_scalar(gidx_i, slots_i, 1, ALU.logical_shift_right))
            after(v.tensor_single_scalar(gidx_i, gidx_i, 1, ALU.logical_shift_left))
            after(v.tensor_single_scalar(gidx_i[B:P], gidx_i[B:P], 1, ALU.add))
            v.tensor_single_scalar(slots_i[B:P], slots_i[B:P], 2 * S, ALU.add).then_inc(gidx_ready, 1)

            n_blk = dve.value_load(tab[0:1, 1:2], min_val=1, max_val=NB - 3)
            halves = lambda ap: ap.rearrange("p (h k) o -> p h k o", h=2)
            sc4 = mods[:, 4 * KD:5 * KD, 0:1]
            sh3 = mods[:, 3 * KD:4 * KD, 0:1]

            def modulate(n):
                dve.wait_ge(xg_turned, n + 1)
                for b in range(2):
                    src = bank[b][:, :].rearrange("p (k h n) -> p h k n", h=2, n=B)
                    dst = xgT.rearrange("p (h k) n -> p h k n", h=2)[:, :, 4 * b:4 * b + 4, :]
                    sc = halves(sc4)[:, :, 4 * b:4 * b + 4, :].to_broadcast([P, 2, 4, B])
                    v.tensor_tensor(dst, src, sc, ALU.mult).then_inc(xg_scaled, 1)
                dve.wait_ge(xg_scaled, n * 2 + 2)
                v.tensor_tensor(xgT, xgT, bc(sh3, P, KD, B), ALU.add).then_inc(xgT_ready, 1)

            dve.wait_ge(g5_ready, 2)
            modulate(0)
            with dve.Fori(0, n_blk) as g:
                dve.wait_ge(w_used[3], g + 2)
                v.tensor_copy(gu, bank[2][:, :]).then_inc(gu_ready, 1)
                dve.wait_ge(silu_done, g + 1)
                v.tensor_tensor(actT, bank[3][:, :].rearrange("p (k h n) -> p k h n", h=2, n=B)[:, :, 1, :], sil, ALU.mult).then_inc(act_ready, 1)
                modulate(g + 1)
                dve.wait_ge(w_used[7], g + 2)
                dve.wait_ge(ye_free, g + 1)
                for q in range(2):
                    v.tensor_tensor(ye[:, q * S:(q + 1) * S], bank[4 + q][:, :], g5b[:, q * S:(q + 1) * S], ALU.mult).then_inc(ye_ready, 1)

            for t in range(TS + 1):
                if t < TS:
                    y0, y1 = Y[:, t, 0, :], Y[:, t, 1, :]
                    dve.wait_ge(res_done, t + 1)
                    after(v.scalar_tensor_tensor(y0, y1, wtok[:, t, 1:2], y0, ALU.mult, ALU.add))
                    full_stats(t, y0)
                    after(v.bn_aggr(mv[:, t, :], stats[:, t, :, :].rearrange("p q n -> p (q n)")))
                    v.tensor_scalar_add(rstd[:, t, :], mv[:, t, 1:2], EPS).then_inc(fin_need, 1)
                if t >= 1:
                    y0 = Y[:, t - 1, 0, :]
                    if t == 1:
                        dve.wait_ge(lnf_in, 32)
                    after(v.scalar_tensor_tensor(y0, y0, mv[:, t - 1, 0:1], lnf_b[:, 0, :], ALU.subtract, ALU.mult))
                    dve.wait_ge(fin_rstd, t)
                    v.scalar_tensor_tensor(X1[:, t - 1, :], y0, rstd[:, t - 1, :], lnf_b[:, 1, :], ALU.mult, ALU.add).then_inc(fin_ready, 1)

        @block.gpsimd
        def _(pool):
            gp = nc.gpsimd
            gp.memset(fill_i[0:B, :], EMPTY).then_inc(fill_ready, 1)
            pool.wait_ge(fill_ready, 1)
            pool.dma_start(slot_dram.rearrange("(p n) o -> p (n o)", n=NB), fill_i[0:B, :]).then_inc(scattered, 16)
            gp.memset(glu, 0.0).then_inc(glu_zero, 1)

            def root(ap, need, n, ready):
                pool.wait_ge(need, n)
                gp.tensor_tensor(ap, ap, half[:, 0:1].to_broadcast([P, ap.shape[1]]), ALU.pow).then_inc(ready, 1)

            def mod_bias(i):
                m_i = mods[:, i * KD:(i + 1) * KD, :]
                pool.wait_ge(mod_col_ready, i + 1)
                b = par("b_mod")[:, i * KD:(i + 1) * KD].rearrange("p (k o) -> p k o", o=1).to_broadcast([P, KD, 2])
                if i in (1, 4):
                    gp.tensor_tensor(m_i, m_i, b, ALU.add).then_inc(mod_one, 1)
                    pool.wait_ge(mod_one, 1 if i == 1 else 2)
                    gp.tensor_scalar_add(m_i, m_i, 1.0).then_inc(mod_biased, 1)
                else:
                    gp.tensor_tensor(m_i, m_i, b, ALU.add).then_inc(mod_biased, 1)

            for t in range(TS + TC):
                root(rstd[:, t, :], z_rstd_need, t + 1, z_rstd_ready)
            mod_bias(0)
            mod_bias(1)
            pool.wait_ge(xt_out, 2 * KD)
            pool.wait_ge(scattered, 16)
            pool.dma_start(dft_s.rearrange("p t r n -> p (t r n)"), dfts).then_inc(dft_in, 16)
            pool.dma_start(wf, w_fourier.rearrange("(k p) n -> p k n", p=P)).then_inc(wf_in, 16)
            pool.wait_ge(f_out, 8 + NF)
            pool.dma_start(wpw, w_pw.rearrange("(k p) n -> p k n", p=P)).then_inc(wpw_in, 16)

            def rotate(i0, dst):
                with pool.Fori(0, QK_IT) as i:
                    for u in range(2):
                        pool.wait_ge(raw_ready, i * 2 + (i0 + u + 1))
                        o = dst[:, bass.ds(i * 2 + u, 1), 0:S].rearrange("p o n -> p (o n)")
                        gp.tensor_tensor(rope_raw[:, u, :], rope_raw[:, u, :], cst("cos"), ALU.mult).then_inc(rot, 1)
                        gp.tensor_tensor(rope_swap[:, u, :], rope_swap[:, u, :], cst("sin"), ALU.mult).then_inc(rot, 1)
                        pool.wait_ge(rot, i * 4 + (2 * i0 + 2 * u + 2))
                        gp.tensor_tensor(o, rope_raw[:, u, :], rope_swap[:, u, :], ALU.add).then_inc(raw_free, 1)

            mod_bias(2)
            rotate(0, QT)
            root(crstd, cvar_done, 1, crstd_ready)
            pool.wait_ge(pw_out, NCV)
            pool.dma_start(bv_b, b_v.to_broadcast([P, HEADS * P])).then_inc(bv_in, 16)
            rotate(HEADS, KT)
            for i in range(3, 6):
                mod_bias(i)
            for h in range(HEADS):
                root(o_var, ovar_done, h + 1, orstd_ready)
            pool.wait_ge(shift_out, 1)
            w4 = mods[:, 4 * KD:5 * KD, 0:1].to_broadcast([P, KD, NG + NE])
            gp.tensor_tensor(wr, wr, w4, ALU.mult).then_inc(wr_scaled, 1)
            pool.wait_ge(shift_copied, 1)
            gp.tensor_tensor(lgb, lgb, par("b_r"), ALU.add).then_inc(lgb_ready, 1)
            root(rstd[:, 0:TS, :].rearrange("p t o -> p (t o)"), z_rstd_need, 7, z_rstd_ready)
            for t in range(TS):
                root(rstd2[:, t, :], x_rstd_need, t + 1, x_stat)
                pool.wait_ge(x_stat, 2 * t + 1)
                gp.tensor_tensor(nmean[:, t, :], mv2[:, t, 0:1], rstd2[:, t, :], ALU.mult).then_inc(x_stat, 1)
                pool.wait_ge(x_stat, 2 * t + 2)
                gp.tensor_scalar_mul(nmean[:, t, :], nmean[:, t, :], -1.0).then_inc(x_rstd_ready, 1)

            pool.wait_ge(addr_ready, 1)
            for k in range(2):
                for t in range(TS):
                    c = k * TS + t
                    pool.indirect_dma_start(slot_dram, bass.IndirectOffsetOnAxis(ap=addri[:, c:c + 1], axis=0),
                                            vali[:, c:c + 1], None).then_inc(slots_scattered, 16)
            pool.wait_ge(rows_out, 16 * TS)
            gp.memset(xg_in, 0.0).then_inc(idx_ready, 1)
            pool.wait_ge(gidx_ready, 1)

            def gather(n):
                gp.tensor_copy(igat, gidx_i[:, bass.ds(n, 1)]).then_inc(idx_ready, 1)
                pool.wait_ge(idx_ready, n + 2)
                pool.sem_inc(pool_step, 1)
                pool.indirect_dma_start(xg_in, None, row_dram, bass.IndirectOffsetOnAxis(ap=igat, axis=0),
                                        bounds_check=2 * S - 1, oob_is_err=False).then_inc(gathered, 16)

            def move_on(n):
                pool.wait_ge(gathered, n * 16 + 16)
                pool.sem_inc(pool_step, 1)
                gp.tensor_copy(xg, xg_in).then_inc(xg_ready, 1)
                pool.wait_ge(xg_ready, n + 1)

            gather(0)
            move_on(0)
            gather(1)
            pool.sem_inc(ye_free, 1)
            pool.wait_ge(xg_turned, 1)
            move_on(1)
            gather(2)
            n_blk = pool.value_load(tab[0:1, 1:2], min_val=1, max_val=NB - 3)
            with pool.Fori(0, n_blk) as g:
                pool.wait_ge(xg_turned, g + 2)
                move_on(g + 2)
                gather(g + 3)
                pool.wait_ge(ye_ready, g * 2 + 2)
                pool.wait_ge(scattered, g * 16 + 16)
                pool.sem_inc(pool_step, 1)
                gp.tensor_copy(isca, slots_i[:, bass.ds(g, 1)]).then_inc(isca_ready, 1)
                gp.tensor_copy(ye_out, ye).then_inc(ye_free, 1)
                pool.wait_ge(isca_ready, g + 1)
                pool.wait_ge(ye_free, g + 2)
                pool.sem_inc(pool_step, 1)
                pool.indirect_dma_start(y_dram, bass.IndirectOffsetOnAxis(ap=isca, axis=0), ye_out, None,
                                        bounds_check=4 * S - 1, oob_is_err=False).then_inc(scattered, 16)
            pool.wait_ge(gathered, n_blk * 16 + 48)
            pool.wait_ge(scattered, n_blk * 16 + 16)
            for t in range(TS + 1):
                if t < TS:
                    pool.wait_ge(x1_scaled, t + 1)
                    pool.wait_ge(w0_done, t + 1)
                    gp.tensor_tensor(Y[:, t, 0, :], Y[:, t, 0, :], X1[:, t, :], ALU.add).then_inc(res_done, 1)
                if t >= 1:
                    root(rstd[:, t - 1, :], fin_need, t, fin_rstd)


def kernel(**inputs):
    import numpy as np
    import concourse.bacc as bacc
    from concourse.bass_utils import run_bass_kernel_spmd

    f = {k: np.asarray(v) for k, v in inputs.items()}
    consts = np.zeros((P, N_CONST), np.float32)

    def put(name, v):
        lo, hi = CONST[name]
        consts[:, lo:hi] = v

    put("ident", np.eye(P))
    put("ones", 1.0)
    put("upper", np.triu(np.ones((P, P)), 1))
    t = np.arange(S)
    inv = (1.0 / (10000.0 ** (np.arange(16, dtype=np.float32) / np.float32(16)))).astype(np.float32)
    ang = np.concatenate([(t // 64).astype(np.float32)[:, None] * inv, (t % 64).astype(np.float32)[:, None] * inv], -1)
    cos, sin = np.cos(ang).T, np.sin(ang).T
    put("cos", np.concatenate([cos] * 4, 0))
    put("sin", np.concatenate([-sin, sin] * 2, 0))
    th = 2 * np.pi * (np.outer(np.arange(P), np.arange(P)) % P) / P
    put("dftc", np.concatenate([np.cos(th), np.sin(th)], 1) / np.sqrt(P))
    put("iota", np.arange(NB))
    put("iota_p", np.arange(P)[:, None])
    put("first", np.arange(EG, 0, -1))
    put("val", 2 * (np.arange(TS)[None, None, :] * P + np.arange(P)[:, None, None]).repeat(2, 1).reshape(P, 2 * TS)
        + np.repeat(np.arange(2), TS)[None, :])
    ph = 2 * np.pi * (np.outer(t, t) % S) / S
    dfts = (np.stack([np.cos(ph), -np.sin(ph)], 1) / np.sqrt(S)).reshape(TS, P, 2, S).transpose(1, 0, 2, 3)
    dfts = np.ascontiguousarray(dfts.reshape(P, -1), dtype=np.float32)

    params = np.zeros((P, N_PARAM), np.float32)

    def lay(name, v):
        lo, hi = PARAM[name]
        params[:v.shape[0], lo:hi] = v

    cols = lambda v: v.reshape(-1, P).T
    lay("c", np.tile(np.stack([f["c"][0].reshape(KD, P).T, f["c_ctx"].reshape(KD, P).T], 2), (1, 1, CB // 2)).reshape(P, KD * CB))
    lay("b_in", cols(f["b_in"][0, :28 * P]))
    lay("b_mod", cols(f["b_mod"][0]))
    lay("conv_w", f["conv_w"][0].reshape(CW, NCV, P).transpose(2, 1, 0).reshape(P, NCV * CW))
    lay("conv_b", cols(f["conv_b"][0]))
    lay("cln_g", cols(f["conv_ln_g"][0]))
    lay("cln_b", cols(f["conv_ln_b"][0]))
    lay("subln", cols(f["subln_g"][0]))
    lay("lam", np.stack([f["lam_q1"][0], f["lam_q2"][0], f["lam_k1"][0], f["lam_k2"][0]], 1))
    lay("b_r", np.broadcast_to(np.concatenate([f["b_rg"][0], f["b_re"][0]])[None, :], (P, NG + NE)))
    tiled = lambda w: np.ascontiguousarray(w.reshape(KD, P, -1, P).transpose(2, 1, 0, 3).reshape(-1, P, KD * P))
    arrays = {
        "consts": consts, "dfts": dfts, "params": params, "x": f["x"][0], "ctx_in": f["ctx"][0],
        "w_mod": f["w_mod"][0].reshape(KD, P, 6, D).transpose(2, 0, 1, 3).reshape(N_MODT, P, D), "w_in": tiled(f["w_in"][0]), "b_v": f["b_in"][:, 28 * P:],
        "w_fourier": f["w_fourier"][0], "w_pw": f["w_pw"][0], "w_out": tiled(f["w_out"][0]),
        "ln_a": np.concatenate([f["ln_a_g"], f["ln_a_b"]], 0), "ln_f": np.concatenate([f["ln_f_g"], f["ln_f_b"]], 0),
        "w_r": np.concatenate([f["w_rg"][0], f["w_re"][0]], 1).reshape(KD, P, NG + NE).transpose(1, 0, 2).reshape(P, -1),
        "w_gate": f["w_gate"][0], "w_up": f["w_up"][0], "w_down": f["w_down"][0],
    }
    arrays = {k: np.ascontiguousarray(v) for k, v in arrays.items()}
    nc = bacc.Bacc("TRN2", target_bir_lowering=False, num_devices=1)
    args = {k: nc.dram_tensor(f"in_{k}", v.shape, mybir.dt.from_np(v.dtype), kind="ExternalInput").ap() for k, v in arrays.items()}
    res = nc.dram_tensor("out_rows", (S, D), F32, kind="ExternalOutput").ap()
    build(nc, out=res, **args)
    r = run_bass_kernel_spmd(nc, [{f"in_{k}": v for k, v in arrays.items()}], core_ids=[0])
    return r.results[0]["out_rows"].reshape(1, S, D)
```
